# Optimizing a Trainium2 kernel written in Bass

```python
import math
import jax, jax.numpy as jnp
from jax import lax
import numpy as np

D_MODEL = 1024
BATCH = 1
SEQ = 512
DEPTH = 2

EXPAND = 2
D_INNER = EXPAND * D_MODEL
N_MEM = 256
EPS = 1e-6
NEG = -1e30
BIG = 1e30

POOL_WINDOWS = (2, 4, 8, 16)
POOL_WIDTH = 3 * D_INNER // 8
POOL_GROUP = POOL_WIDTH // len(POOL_WINDOWS)

RET_HEADS = 4
RET_DK = 128
RET_DV = 192
RET_CHUNK = 128
ROPE_BASE = 10000.0

MEM_HEADS = 4
MEM_DH = 128
MEM_WIDTH = MEM_HEADS * MEM_DH

NSA_HEADS = 12
NSA_KV = 2
NSA_HPG = NSA_HEADS // NSA_KV
NSA_DH = 128
CMP_BLOCK = 32
CMP_STRIDE = 16
CMP_HIDDEN = 256
SLC_BLOCK = 64
SLC_TOPK = 8
WINDOW = 512
NSA_QBLOCK = 32

REL_BUCKETS = 32
REL_MAX_DIST = 128

EVEN_SPLITS = (POOL_WIDTH, RET_HEADS * RET_DK, RET_HEADS * RET_DK, RET_HEADS * RET_DV, MEM_WIDTH, D_INNER)
ODD_SPLITS = (NSA_HEADS * NSA_DH,) + (NSA_KV * NSA_DH,) * 6 + (3 * NSA_HEADS, MEM_WIDTH, D_INNER)
EVEN_COLS = sum(EVEN_SPLITS)
ODD_COLS = sum(ODD_SPLITS)


def rmsnorm(x, g):
    xf = x.astype(jnp.float32)
    y = xf * lax.rsqrt(jnp.mean(xf * xf, axis=-1, keepdims=True) + EPS)
    return (y * g.astype(jnp.float32)).astype(x.dtype)

def split_cols(z, sizes):
    return jnp.split(z, np.cumsum(sizes)[:-1].tolist(), axis=-1)

def t5_bucket(rel):
    n = jnp.maximum(rel, 0)
    max_exact = REL_BUCKETS // 2
    nf = jnp.maximum(n, 1).astype(jnp.float32)
    large = max_exact + (jnp.log(nf / max_exact) / math.log(REL_MAX_DIST / max_exact)
                         * (REL_BUCKETS - max_exact)).astype(jnp.int32)
    large = jnp.minimum(large, REL_BUCKETS - 1)
    return jnp.where(n < max_exact, n, large)

def pool_mixer(u, w_grp, scale):
    B_, S, W = u.shape
    uf = u.astype(jnp.float32)
    cs = jnp.concatenate([jnp.zeros((B_, 1, W), jnp.float32), jnp.cumsum(uf, axis=1)], axis=1)
    t = jnp.arange(S)
    outs = []
    for gi, w in enumerate(POOL_WINDOWS):
        sl = slice(gi * POOL_GROUP, (gi + 1) * POOL_GROUP)
        lo = jnp.maximum(t + 1 - w, 0)
        cnt = (t + 1 - lo).astype(jnp.float32)[None, :, None]
        outs.append((cs[:, 1:, sl] - cs[:, lo, sl]) / cnt - uf[..., sl])
    pooled = jnp.stack(outs, axis=2)
    y = jnp.einsum('bsgc,gcd->bsgd', pooled, w_grp.astype(jnp.float32)).reshape(B_, S, W)
    return y * scale.astype(jnp.float32)

def rotary(x):
    S, Dh = x.shape[-2], x.shape[-1]
    half = Dh // 2
    inv = ROPE_BASE ** (-jnp.arange(half, dtype=jnp.float32) / half)
    ang = jnp.arange(S, dtype=jnp.float32)[:, None] * inv[None, :]
    cos, sin = jnp.cos(ang), jnp.sin(ang)
    x1 = x[..., :half].astype(jnp.float32)
    x2 = x[..., half:].astype(jnp.float32)
    return jnp.concatenate([x1 * cos - x2 * sin, x1 * sin + x2 * cos], axis=-1)

def retention(q, k, v):
    B_, S, _ = q.shape
    H, C = RET_HEADS, RET_CHUNK
    N = S // C
    qh = rotary(q.reshape(B_, S, H, RET_DK).transpose(0, 2, 1, 3)) * (RET_DK ** -0.5)
    kh = rotary(k.reshape(B_, S, H, RET_DK).transpose(0, 2, 1, 3))
    vh = v.reshape(B_, S, H, RET_DV).transpose(0, 2, 1, 3).astype(jnp.float32)
    log_g = jnp.log(1.0 - jnp.exp2(-5.0 - jnp.arange(H, dtype=jnp.float32)))
    n = jnp.arange(C, dtype=jnp.float32)
    diff = n[:, None] - n[None, :]
    decay_in = jnp.where(diff >= 0, jnp.exp(log_g[:, None, None] * jnp.maximum(diff, 0.0)), 0.0)
    xi = jnp.exp(log_g[:, None] * (n + 1.0))
    zeta = jnp.exp(log_g[:, None] * (C - 1.0 - n))
    g_chunk = jnp.exp(log_g * C)
    qc = qh.reshape(B_, H, N, C, RET_DK)
    kc = kh.reshape(B_, H, N, C, RET_DK)
    vc = vh.reshape(B_, H, N, C, RET_DV)
    att = jnp.einsum('bhncd,bhnmd->bhncm', qc, kc) * decay_in[None, :, None]
    o_inner = jnp.einsum('bhncm,bhnmv->bhncv', att, vc)
    kv = jnp.einsum('bhnmd,bhnmv->bhndv', kc * zeta[None, :, None, :, None], vc)

    def step(R, kv_n):
        return R * g_chunk[None, :, None, None] + kv_n, R

    _, R_prev = lax.scan(step, jnp.zeros((B_, H, RET_DK, RET_DV), jnp.float32), kv.transpose(2, 0, 1, 3, 4))
    R_prev = R_prev.transpose(1, 2, 0, 3, 4)
    o_cross = jnp.einsum('bhncd,bhndv->bhncv', qc * xi[None, :, None, :, None], R_prev)
    o = (o_inner + o_cross).reshape(B_, H, S, RET_DV)
    mu = jnp.mean(o, axis=-1, keepdims=True)
    var = jnp.mean((o - mu) ** 2, axis=-1, keepdims=True)
    o = (o - mu) * lax.rsqrt(var + EPS)
    return o.transpose(0, 2, 1, 3).reshape(B_, S, H * RET_DV)

def mem_attention(xq, mem_n, w_mem_kv):
    B_, S, _ = xq.shape
    M = mem_n.shape[1]
    mk, mv = jnp.split(mem_n @ w_mem_kv, 2, axis=-1)
    mk = mk.reshape(B_, M, MEM_HEADS, MEM_DH)
    mv = mv.reshape(B_, M, MEM_HEADS, MEM_DH)
    qh = xq.reshape(B_, S, MEM_HEADS, MEM_DH).astype(jnp.float32) * (MEM_DH ** -0.5)
    p = jax.nn.softmax(jnp.einsum('bshd,bmhd->bhsm', qh, mk), axis=-1)
    o = jnp.einsum('bhsm,bmhd->bshd', p, mv)
    return o.reshape(B_, S, MEM_WIDTH)

def compress(k, pe, w1, b1, w2):
    B_, S = k.shape[:2]
    n_cmp = (S - CMP_BLOCK) // CMP_STRIDE + 1
    idx = jnp.arange(n_cmp)[:, None] * CMP_STRIDE + jnp.arange(CMP_BLOCK)[None, :]
    blocks = k[:, idx] + pe[:, None, :]
    flat = blocks.transpose(0, 1, 3, 2, 4).reshape(B_, n_cmp, NSA_KV, CMP_BLOCK * NSA_DH)
    return jax.nn.silu(flat @ w1 + b1) @ w2

def cmp_to_slc_matrix(n_cmp, n_slc):
    cst = np.arange(n_cmp)[:, None] * CMP_STRIDE
    sst = np.arange(n_slc)[None, :] * SLC_BLOCK
    ov = np.clip(np.minimum(cst + CMP_BLOCK, sst + SLC_BLOCK) - np.maximum(cst, sst), 0, None)
    return jnp.asarray(ov / CMP_STRIDE, dtype=jnp.float32)

def nsa_attention(q, kc, vc, ks, vs, kw, vw, gate_logits, cmp_pe, cmp_w1, cmp_b1, cmp_w2, rel_bias):
    B_, S = q.shape[:2]
    QB = NSA_QBLOCK
    qh = q.reshape(B_, S, NSA_KV, NSA_HPG, NSA_DH).transpose(0, 2, 3, 1, 4).astype(jnp.float32) * (NSA_DH ** -0.5)

    def kv_heads(t):
        return t.reshape(B_, S, NSA_KV, NSA_DH)

    kcmp = compress(kv_heads(kc), cmp_pe[0], cmp_w1[0], cmp_b1[0], cmp_w2[0]).transpose(0, 2, 1, 3)
    vcmp = compress(kv_heads(vc), cmp_pe[1], cmp_w1[1], cmp_b1[1], cmp_w2[1]).transpose(0, 2, 1, 3)
    n_cmp = kcmp.shape[2]
    n_slc = S // SLC_BLOCK
    kslc = kv_heads(ks).reshape(B_, n_slc, SLC_BLOCK, NSA_KV, NSA_DH).transpose(0, 3, 1, 2, 4)
    vslc = kv_heads(vs).reshape(B_, n_slc, SLC_BLOCK, NSA_KV, NSA_DH).transpose(0, 3, 1, 2, 4)
    pad = ((0, 0), (0, 0), (WINDOW, 0), (0, 0))
    kwin = jnp.pad(kv_heads(kw).transpose(0, 2, 1, 3), pad)
    vwin = jnp.pad(kv_heads(vw).transpose(0, 2, 1, 3), pad)
    gates = jax.nn.sigmoid(gate_logits.astype(jnp.float32)).reshape(B_, S, 3, NSA_KV, NSA_HPG).transpose(0, 2, 3, 4, 1)
    overlap = cmp_to_slc_matrix(n_cmp, n_slc)
    cend = jnp.arange(n_cmp) * CMP_STRIDE + CMP_BLOCK - 1
    table = rel_bias.astype(jnp.float32)
    table_g = table.reshape(REL_BUCKETS, NSA_KV, NSA_HPG)
    k_sel = min(SLC_TOPK, n_slc)
    b_idx = jnp.arange(B_)[:, None, None, None]
    g_idx = jnp.arange(NSA_KV)[None, :, None, None]

    def head_bias(rel):
        return table[t5_bucket(rel)].transpose(2, 0, 1).reshape(NSA_KV, NSA_HPG, rel.shape[0], rel.shape[1])

    def masked_softmax(s, mask):
        return jax.nn.softmax(jnp.where(mask, s, NEG), axis=-1)

    def block(s0):
        tpos = s0 + jnp.arange(QB)
        qb = lax.dynamic_slice_in_dim(qh, s0, QB, axis=3)
        gb = lax.dynamic_slice_in_dim(gates, s0, QB, axis=4)
        rel_c = tpos[:, None] - cend[None, :]
        sc = jnp.einsum('bghqd,bgjd->bghqj', qb, kcmp) + head_bias(rel_c)
        pc = masked_softmax(sc, rel_c >= 0) * (tpos >= CMP_BLOCK - 1).astype(jnp.float32)[:, None]
        oc = jnp.einsum('bghqj,bgjd->bghqd', pc, vcmp)
        imp = jnp.einsum('bghqj,js->bgqs', pc, overlap)
        sblk = jnp.arange(n_slc)[None, :]
        cur = (tpos // SLC_BLOCK)[:, None]
        forced = (sblk == 0) | (sblk == cur) | (sblk == cur - 1)
        future = sblk * SLC_BLOCK > tpos[:, None]
        imp = jnp.where(forced, BIG, jnp.where(future, -BIG, imp))
        _, sel = lax.top_k(imp, k_sel)
        kg = kslc[b_idx, g_idx, sel].reshape(B_, NSA_KV, QB, k_sel * SLC_BLOCK, NSA_DH)
        vg = vslc[b_idx, g_idx, sel].reshape(B_, NSA_KV, QB, k_sel * SLC_BLOCK, NSA_DH)
        kpos_s = (sel[..., None] * SLC_BLOCK + jnp.arange(SLC_BLOCK)).reshape(B_, NSA_KV, QB, k_sel * SLC_BLOCK)
        rel_s = tpos[None, None, :, None] - kpos_s
        bias_s = table_g[t5_bucket(rel_s), g_idx].transpose(0, 1, 4, 2, 3)
        ss = jnp.einsum('bghqd,bgqkd->bghqk', qb, kg) + bias_s
        ps = masked_softmax(ss, (rel_s >= 0)[:, :, None])
        osel = jnp.einsum('bghqk,bgqkd->bghqd', ps, vg)
        kwb = lax.dynamic_slice_in_dim(kwin, s0, WINDOW + QB, axis=2)
        vwb = lax.dynamic_slice_in_dim(vwin, s0, WINDOW + QB, axis=2)
        kpos_w = s0 - WINDOW + jnp.arange(WINDOW + QB)
        rel_w = tpos[:, None] - kpos_w[None, :]
        mask_w = (rel_w >= 0) & (rel_w < WINDOW) & (kpos_w >= 0)[None, :]
        sw = jnp.einsum('bghqd,bgkd->bghqk', qb, kwb) + head_bias(rel_w)
        pw = masked_softmax(sw, mask_w)
        ow = jnp.einsum('bghqk,bgkd->bghqd', pw, vwb)
        return gb[:, 0, ..., None] * oc + gb[:, 1, ..., None] * osel + gb[:, 2, ..., None] * ow

    outs = lax.map(block, jnp.arange(S // QB) * QB)
    return outs.transpose(1, 0, 4, 2, 3, 5).reshape(B_, S, NSA_HEADS * NSA_DH)

def even_layer(h, mem_n, g, w_in, pool_w, pool_scale, w_mem_kv, w_out):
    u = rmsnorm(h, g)
    za, rq, rk, rv, xq, gate = split_cols(u @ w_in, EVEN_SPLITS)
    a = pool_mixer(za, pool_w, pool_scale)
    r = retention(rq, rk, rv)
    m = mem_attention(xq, mem_n, w_mem_kv)
    y = jnp.concatenate([a, r, m], axis=-1) * jax.nn.silu(gate.astype(jnp.float32))
    return h + (y @ w_out).astype(h.dtype)

def odd_layer(h, mem_n, g, w_in, cmp_pe, cmp_w1, cmp_b1, cmp_w2, w_mem_kv, w_out, rel_bias):
    u = rmsnorm(h, g)
    q, kc, vc, ks, vs, kw, vw, gl, xq, gate = split_cols(u @ w_in, ODD_SPLITS)
    c = nsa_attention(q, kc, vc, ks, vs, kw, vw, gl, cmp_pe, cmp_w1, cmp_b1, cmp_w2, rel_bias)
    m = mem_attention(xq, mem_n, w_mem_kv)
    y = jnp.concatenate([c, m], axis=-1) * jax.nn.silu(gate.astype(jnp.float32))
    return h + (y @ w_out).astype(h.dtype)

def first_inputs(seed: int = 0) -> dict:
    key = jax.random.key(seed)
    ks = jax.random.split(key, 20)
    n_even = (DEPTH + 1) // 2
    n_odd = DEPTH // 2

    def nrm(k, shape, scale):
        return scale * jax.random.normal(k, shape, jnp.float32)

    return {
        'x': nrm(ks[0], (BATCH, SEQ, D_MODEL), 1.0),
        'mem': nrm(ks[1], (BATCH, N_MEM, D_MODEL), 1.0),
        'norm_g': 1.0 + nrm(ks[2], (DEPTH, D_MODEL), 0.05),
        'final_g': 1.0 + nrm(ks[3], (D_MODEL,), 0.05),
        'mem_norm_g': 1.0 + nrm(ks[4], (D_MODEL,), 0.05),
        'rel_bias': nrm(ks[5], (REL_BUCKETS, NSA_HEADS), 0.5),
        'ev_w_in': nrm(ks[6], (n_even, D_MODEL, EVEN_COLS), D_MODEL ** -0.5),
        'ev_pool_w': nrm(ks[7], (n_even, len(POOL_WINDOWS), POOL_GROUP, POOL_GROUP), POOL_GROUP ** -0.5),
        'ev_pool_scale': 1.0 + nrm(ks[8], (n_even, POOL_WIDTH), 0.1),
        'ev_w_mem_kv': nrm(ks[9], (n_even, D_MODEL, 2 * MEM_WIDTH), D_MODEL ** -0.5),
        'ev_w_out': nrm(ks[10], (n_even, D_INNER, D_MODEL), D_INNER ** -0.5),
        'od_w_in': nrm(ks[11], (n_odd, D_MODEL, ODD_COLS), D_MODEL ** -0.5),
        'od_cmp_pe': nrm(ks[12], (n_odd, 2, CMP_BLOCK, NSA_DH), 0.1),
        'od_cmp_w1': nrm(ks[13], (n_odd, 2, CMP_BLOCK * NSA_DH, CMP_HIDDEN), (CMP_BLOCK * NSA_DH) ** -0.5),
        'od_cmp_b1': nrm(ks[14], (n_odd, 2, CMP_HIDDEN), 0.01),
        'od_cmp_w2': nrm(ks[15], (n_odd, 2, CMP_HIDDEN, NSA_DH), CMP_HIDDEN ** -0.5),
        'od_w_mem_kv': nrm(ks[16], (n_odd, D_MODEL, 2 * MEM_WIDTH), D_MODEL ** -0.5),
        'od_w_out': nrm(ks[17], (n_odd, D_INNER, D_MODEL), D_INNER ** -0.5),
    }

def first_block(x, mem, norm_g, final_g, mem_norm_g, rel_bias, ev_w_in, ev_pool_w, ev_pool_scale, ev_w_mem_kv, ev_w_out,
              od_w_in, od_cmp_pe, od_cmp_w1, od_cmp_b1, od_cmp_w2, od_w_mem_kv, od_w_out):
    mem_n = rmsnorm(mem, mem_norm_g)
    h = x
    for i in range(DEPTH):
        j = i // 2
        if i % 2 == 0:
            h = even_layer(h, mem_n, norm_g[i], ev_w_in[j], ev_pool_w[j], ev_pool_scale[j], ev_w_mem_kv[j], ev_w_out[j])
        else:
            h = odd_layer(h, mem_n, norm_g[i], od_w_in[j], od_cmp_pe[j], od_cmp_w1[j], od_cmp_b1[j], od_cmp_w2[j],
                          od_w_mem_kv[j], od_w_out[j], rel_bias)
    return rmsnorm(h, final_g)


DEPTH_2 = 1

FOURIER_WIDTH = D_MODEL // 2
FOURIER_GROUPS = 4
FOURIER_GROUP_CH = FOURIER_WIDTH // FOURIER_GROUPS
SSM_WIDTH = D_MODEL // 2
SSM_GROUP_CH = 16
SSM_GROUPS = SSM_WIDTH // SSM_GROUP_CH
SSM_STATE = 64
DT_MIN = 1e-3
DT_MAX = 1e-1
N_BRANCHES = 2
IN_WIDTH = FOURIER_WIDTH + SSM_WIDTH + N_BRANCHES * D_MODEL
MOE_GROUPS = 8
EXPERTS_PER_GROUP = 8
N_EXPERTS = MOE_GROUPS * EXPERTS_PER_GROUP
MOE_TOP_K = 2
D_EXPERT = D_MODEL // 2
MOE_BLOCK = 128
RMS_EPS = 1e-6


def _rmsnorm(x, g):
    xf = x.astype(jnp.float32)
    inv = lax.rsqrt(jnp.mean(xf * xf, axis=-1, keepdims=True) + RMS_EPS)
    return (xf * inv * g.astype(jnp.float32)).astype(x.dtype)

def _fourier_mix(u):
    b, l, _ = u.shape
    ug = u.astype(jnp.float32).reshape(b, l, FOURIER_GROUPS, FOURIER_GROUP_CH)
    f = jnp.fft.fft2(ug, axes=(1, 3), norm='ortho').real
    return f.reshape(b, l, FOURIER_WIDTH).astype(u.dtype)

def _scan_combine(e1, e2):
    a1, b1 = e1
    a2, b2 = e2
    return a1 * a2, a2 * b1 + b2

def _ssm_direction(ug, a_re, a_im, log_dt, b_re, b_im, c_re, c_im, reverse):
    lam = lax.complex(a_re.astype(jnp.float32), a_im.astype(jnp.float32))
    dt = jnp.exp(log_dt.astype(jnp.float32))[:, None]
    a_bar = jnp.exp(lam * dt)
    b_mat = lax.complex(b_re.astype(jnp.float32), b_im.astype(jnp.float32))
    b_bar = ((a_bar - 1.0) / lam)[..., None] * b_mat
    bu = jnp.einsum('blgc,gnc->blgn', ug.astype(jnp.complex64), b_bar)
    a = jnp.broadcast_to(a_bar, bu.shape)
    _, h = lax.associative_scan(_scan_combine, (a, bu), axis=1, reverse=reverse)
    c_mat = lax.complex(c_re.astype(jnp.float32), c_im.astype(jnp.float32))
    return jnp.einsum('blgn,gcn->blgc', h, c_mat).real

def _ssm_mix(u, a_re, a_im, log_dt, b_re, b_im, c_re, c_im, d_skip, w_glu):
    b, l, _ = u.shape
    uf = u.astype(jnp.float32)
    ug = uf.reshape(b, l, SSM_GROUPS, SSM_GROUP_CH)
    y = (_ssm_direction(ug, a_re[0], a_im[0], log_dt[0], b_re[0], b_im[0], c_re[0], c_im[0], False)
         + _ssm_direction(ug, a_re[1], a_im[1], log_dt[1], b_re[1], b_im[1], c_re[1], c_im[1], True))
    y = y.reshape(b, l, SSM_WIDTH) + d_skip.astype(jnp.float32) * uf
    y = jax.nn.gelu(y)
    y = y * jax.nn.sigmoid(y @ w_glu.astype(jnp.float32))
    return y.astype(u.dtype)

def _hier_moe(h, wg, bg, we, be, w_gate, w_up, w_down):
    bsz, l, d = h.shape
    t = bsz * l
    ht = h.reshape(t, d)
    g_prob = jax.nn.softmax((ht @ wg).astype(jnp.float32) + bg.astype(jnp.float32), axis=-1)
    p_g, g_idx = lax.top_k(g_prob, 1)
    e_logits = ((ht @ we).astype(jnp.float32) + be.astype(jnp.float32)).reshape(t, MOE_GROUPS, EXPERTS_PER_GROUP)
    e_sel = jnp.take_along_axis(e_logits, g_idx[:, :, None], axis=1)[:, 0]
    top_l, top_i = lax.top_k(e_sel, MOE_TOP_K)
    gate_w = p_g * jax.nn.softmax(top_l, axis=-1)
    expert = g_idx * EXPERTS_PER_GROUP + top_i

    n_assign = t * MOE_TOP_K
    e_flat = expert.reshape(n_assign)
    w_flat = gate_w.reshape(n_assign)
    tok_flat = jnp.repeat(jnp.arange(t, dtype=jnp.int32), MOE_TOP_K)
    order = jnp.argsort(e_flat)
    e_s = e_flat[order]
    tok_s = tok_flat[order]
    w_s = w_flat[order]
    counts = jnp.bincount(e_flat, length=N_EXPERTS)
    starts = jnp.cumsum(counts) - counts
    padded = ((counts + MOE_BLOCK - 1) // MOE_BLOCK) * MOE_BLOCK
    pstarts = jnp.cumsum(padded) - padded
    pends = pstarts + padded
    dest = pstarts[e_s] + jnp.arange(n_assign, dtype=jnp.int32) - starts[e_s]
    n_blocks = -(-n_assign // MOE_BLOCK) + N_EXPERTS
    rows = n_blocks * MOE_BLOCK
    x_pad = jnp.zeros((rows, d), h.dtype).at[dest].set(ht[tok_s])
    block_start = jnp.arange(n_blocks, dtype=jnp.int32) * MOE_BLOCK
    block_e = jnp.minimum(jnp.searchsorted(pends, block_start, side='right'), N_EXPERTS - 1)

    def expert_block(args):
        xb, e = args
        a = jax.nn.silu(xb @ w_gate[e]) * (xb @ w_up[e])
        return a @ w_down[e]

    y_pad = lax.map(expert_block, (x_pad.reshape(n_blocks, MOE_BLOCK, d), block_e)).reshape(rows, d)
    y = y_pad[dest] * w_s[:, None].astype(h.dtype)
    out = jax.ops.segment_sum(y, tok_s, num_segments=t)
    return out.reshape(bsz, l, d)

def second_inputs(seed: int = 0) -> dict:
    key = jax.random.key(seed)
    ks = jax.random.split(key, 24)
    f32 = jnp.float32

    def nrm(k, shape, scale):
        return jax.random.normal(k, shape, f32) * scale

    S, F, D = SSM_WIDTH, FOURIER_WIDTH, D_MODEL
    G, N, C = SSM_GROUPS, SSM_STATE, SSM_GROUP_CH
    n_idx = jnp.arange(N, dtype=f32)
    return {
        'x': nrm(ks[0], (BATCH, SEQ, D), 1.0),
        'mix_norm_g': 1.0 + nrm(ks[1], (DEPTH_2, D), 0.02),
        'w_in': nrm(ks[2], (DEPTH_2, D, IN_WIDTH), D ** -0.5),
        'w_fourier_out': nrm(ks[3], (DEPTH_2, F, D), F ** -0.5),
        'ssm_A_re': -0.5 + nrm(ks[4], (DEPTH_2, 2, G, N), 0.01),
        'ssm_A_im': math.pi * n_idx + nrm(ks[5], (DEPTH_2, 2, G, N), 0.01),
        'ssm_log_dt': jax.random.uniform(ks[6], (DEPTH_2, 2, G), f32, math.log(DT_MIN), math.log(DT_MAX)),
        'ssm_B_re': nrm(ks[7], (DEPTH_2, 2, G, N, C), (2 * C) ** -0.5),
        'ssm_B_im': nrm(ks[8], (DEPTH_2, 2, G, N, C), (2 * C) ** -0.5),
        'ssm_C_re': nrm(ks[9], (DEPTH_2, 2, G, C, N), N ** -0.5),
        'ssm_C_im': nrm(ks[10], (DEPTH_2, 2, G, C, N), N ** -0.5),
        'ssm_D': nrm(ks[11], (DEPTH_2, S), 1.0),
        'ssm_w_glu': nrm(ks[12], (DEPTH_2, S, S), S ** -0.5),
        'w_ssm_out': nrm(ks[13], (DEPTH_2, S, D), S ** -0.5),
        'w_out': nrm(ks[14], (DEPTH_2, D, D), D ** -0.5),
        'ffn_norm_g': 1.0 + nrm(ks[15], (DEPTH_2, D), 0.02),
        'router_group_w': nrm(ks[16], (DEPTH_2, D, MOE_GROUPS), D ** -0.5),
        'router_group_b': nrm(ks[17], (DEPTH_2, MOE_GROUPS), 0.01),
        'router_expert_w': nrm(ks[18], (DEPTH_2, D, N_EXPERTS), D ** -0.5),
        'router_expert_b': nrm(ks[19], (DEPTH_2, N_EXPERTS), 0.01),
        'expert_w_gate': nrm(ks[20], (DEPTH_2, N_EXPERTS, D, D_EXPERT), D ** -0.5),
        'expert_w_up': nrm(ks[21], (DEPTH_2, N_EXPERTS, D, D_EXPERT), D ** -0.5),
        'expert_w_down': nrm(ks[22], (DEPTH_2, N_EXPERTS, D_EXPERT, D), D_EXPERT ** -0.5),
        'final_norm_g': 1.0 + nrm(ks[23], (D,), 0.02),
    }

def second_block(x, mix_norm_g, w_in, w_fourier_out, ssm_A_re, ssm_A_im, ssm_log_dt,
              ssm_B_re, ssm_B_im, ssm_C_re, ssm_C_im, ssm_D, ssm_w_glu, w_ssm_out,
              w_out, ffn_norm_g, router_group_w, router_group_b, router_expert_w,
              router_expert_b, expert_w_gate, expert_w_up, expert_w_down, final_norm_g):
    for i in range(DEPTH_2):
        h = _rmsnorm(x, mix_norm_g[i])
        z = h @ w_in[i]
        u_f = z[..., :FOURIER_WIDTH]
        u_s = z[..., FOURIER_WIDTH:FOURIER_WIDTH + SSM_WIDTH]
        gates = jax.nn.sigmoid(z[..., FOURIER_WIDTH + SSM_WIDTH:].astype(jnp.float32)).astype(x.dtype)
        y_f = _fourier_mix(u_f) @ w_fourier_out[i]
        y_s = _ssm_mix(u_s, ssm_A_re[i], ssm_A_im[i], ssm_log_dt[i], ssm_B_re[i], ssm_B_im[i],
                       ssm_C_re[i], ssm_C_im[i], ssm_D[i], ssm_w_glu[i]) @ w_ssm_out[i]
        merged = gates[..., :D_MODEL] * y_f + gates[..., D_MODEL:] * y_s
        x = x + merged @ w_out[i]
        hn = _rmsnorm(x, ffn_norm_g[i])
        x = x + _hier_moe(hn, router_group_w[i], router_group_b[i], router_expert_w[i],
                          router_expert_b[i], expert_w_gate[i], expert_w_up[i], expert_w_down[i])
    return _rmsnorm(x, final_norm_g)


def setup_inputs(seed=0):
    out = dict(first_inputs(seed))
    for name, value in second_inputs(seed + 1).items():
        if name != "x":
            out[name + "_2"] = value
    return out


def reference(
    x, mem, norm_g, final_g, mem_norm_g, rel_bias, ev_w_in, ev_pool_w, ev_pool_scale,
    ev_w_mem_kv, ev_w_out, od_w_in, od_cmp_pe, od_cmp_w1, od_cmp_b1, od_cmp_w2, od_w_mem_kv,
    od_w_out, mix_norm_g_2, w_in_2, w_fourier_out_2, ssm_A_re_2, ssm_A_im_2, ssm_log_dt_2,
    ssm_B_re_2, ssm_B_im_2, ssm_C_re_2, ssm_C_im_2, ssm_D_2, ssm_w_glu_2, w_ssm_out_2, w_out_2,
    ffn_norm_g_2, router_group_w_2, router_group_b_2, router_expert_w_2, router_expert_b_2,
    expert_w_gate_2, expert_w_up_2, expert_w_down_2, final_norm_g_2,
):
    x = first_block(
        x, mem, norm_g, final_g, mem_norm_g, rel_bias, ev_w_in, ev_pool_w, ev_pool_scale,
        ev_w_mem_kv, ev_w_out, od_w_in, od_cmp_pe, od_cmp_w1, od_cmp_b1, od_cmp_w2, od_w_mem_kv,
        od_w_out,
    )
    return second_block(
        x, mix_norm_g_2, w_in_2, w_fourier_out_2, ssm_A_re_2, ssm_A_im_2, ssm_log_dt_2,
        ssm_B_re_2, ssm_B_im_2, ssm_C_re_2, ssm_C_im_2, ssm_D_2, ssm_w_glu_2, w_ssm_out_2,
        w_out_2, ffn_norm_g_2, router_group_w_2, router_group_b_2, router_expert_w_2,
        router_expert_b_2, expert_w_gate_2, expert_w_up_2, expert_w_down_2, final_norm_g_2,
    )


_drawn_inputs = setup_inputs


def setup_inputs(seed=0):
    import zlib

    import numpy as np

    out = dict(_drawn_inputs(seed))
    spreads = {}
    factors = {'mem_norm_g': 5.456,
     'od_cmp_pe': 2.803,
     'od_cmp_b1': 46.024,
     'mix_norm_g_2': 2.912,
     'ssm_A_re_2': 64.0,
     'router_group_b_2': 15.666,
     'router_expert_b_2': 20.141,
     'final_norm_g_2': 8.107,
     'ssm_B_re_2': 2.764,
     'ssm_B_im_2': 2.688,
     'ssm_C_re_2': 2.878,
     'ssm_C_im_2': 2.97,
     'ffn_norm_g_2': 4.013}
    for name, (base, spread) in spreads.items():
        noise = np.random.default_rng([zlib.crc32(name.encode()), seed]).standard_normal(out[name].shape)
        drawn = base * np.exp(spread * noise) if base else spread * noise
        out[name] = __import__('jax').numpy.asarray(drawn.astype(out[name].dtype))
    for name, factor in factors.items():
        out[name] = (out[name] * factor).astype(out[name].dtype)
    return out
```

```python
from contextlib import ExitStack

import numpy as np

import concourse.bass as bass
from concourse import mybir

ALU = mybir.AluOpType
ACT = mybir.ActivationFunctionType
AX_X = mybir.AxisListType.X
F32 = mybir.dt.float32
I32 = mybir.dt.int32
U32 = mybir.dt.uint32

P = 128
S = 512
NT = S // P
D = 1024
KD = D // P
EPS = 1e-6
BIG = 1e30

POOL_W, N_WIN = 768, 4
WINDOWS = (2, 4, 8, 16)
PG = POOL_W // N_WIN
PH = PG // 2
RH, RDK, RDV = 4, 128, 192
MH, MDH, N_MEM = 4, 128, 256
MT = N_MEM // P
D_IN = 2048
KI = D_IN // P
NH, NKV, DH = 12, 2, 128
HPG = NH // NKV
NCMP = 31
CMP_HID = 256
NBUCKET = 32
FW, FG = 512, 4
SG, SC, SN = 32, 16, 64
GP = SG // 2
L = 8
NCH = S // L
EG, EPG, NE = 8, 8, 64
DE = 512
KE = DE // P
SLOTS = 64
XB = 15
N_ROWS = (NE + XB) * SLOTS

SLOT = 4096
RING, NRING = 0, 3
H0 = RING + NRING * SLOT
Y0 = H0 + 4096
U0 = Y0 + 8192
Z0 = U0 + 8192
C0 = Z0 + 17408
TOTAL = C0 + 3000


def shape_constants():
    c = {}
    c["ident"] = np.eye(P, dtype=np.float32)
    half = RDK // 2
    inv = np.float32(10000.0) ** (-np.arange(half, dtype=np.float32) / half)
    ang = (np.arange(S, dtype=np.float32)[:, None] * inv[None, :].astype(np.float32)).astype(np.float32)
    cos, sin = np.cos(ang.astype(np.float64)), np.sin(ang.astype(np.float64))
    sc = RDK ** -0.5
    rot = np.stack([cos * sc, sin * sc, cos, sin])
    c["rot"] = rot.reshape(4, NT, P, half).transpose(2, 0, 1, 3).reshape(P, -1).astype(np.float32)
    lg = np.log(1.0 - np.exp2(-5.0 - np.arange(RH)))
    diff = np.arange(S)[None, :] - np.arange(P)[:, None]
    dec = np.where(diff >= 0, np.exp(lg[:, None, None] * np.maximum(diff, 0)), 0.0)
    c["decay"] = dec.transpose(1, 0, 2).reshape(P, -1).astype(np.float32)
    s, t = np.arange(P)[:, None], np.arange(P)[None, :]
    band = []
    for w in WINDOWS:
        cur = ((t >= s) & (t - s < w)).astype(np.float64)
        first = cur / np.minimum(t + 1, w) - (s == t)
        prev = ((t + P - s) < w).astype(np.float64) / w
        band += [first, cur / w - (s == t), prev]
    c["band"] = np.stack(band).transpose(1, 0, 2).reshape(P, -1).astype(np.float32)

    def bucket(rel):
        n = np.maximum(rel, 0)
        nf = np.maximum(n, 1).astype(np.float32)
        large = 16 + (np.log(nf / np.float32(16)) / np.float32(np.log(8.0)) * np.float32(16)).astype(np.int32)
        return np.where(n < 16, n, np.minimum(large, 31))

    rel_n = np.arange(1024) - 512
    b, m = np.arange(16)[:, None], np.arange(64)[None, :]
    rel_c = (497 + b - 16 * m).reshape(-1)
    rel = np.concatenate([rel_n, rel_c])
    hot = np.zeros((NBUCKET + 1, 2048), np.float32)
    ok = rel >= 0
    hot[bucket(rel)[ok], np.nonzero(ok)[0]] = 1
    hot[NBUCKET, ~ok] = 1
    c["hot"] = hot
    c["from31"] = (np.arange(P) >= 31).astype(np.float32)[:, None]
    a = 2 * np.pi * np.outer(np.arange(S), np.arange(S)) / S
    c["cosS"] = (np.cos(a) / 256).reshape(NT, P, S).transpose(1, 0, 2).reshape(P, -1).astype(np.float32)
    c["sinS"] = (-np.sin(a) / 256).reshape(NT, P, S).transpose(1, 0, 2).reshape(P, -1).astype(np.float32)
    a = 2 * np.pi * np.outer(np.arange(P), np.arange(P)) / P
    c["dft"] = np.concatenate([np.cos(a), np.sin(a)], 1).astype(np.float32)
    c["before"] = (s < t).astype(np.float32)
    c["iota"] = np.tile(np.arange(64, dtype=np.float32), (P, 1))
    return c


def view(k, off, *shape):
    n = int(np.prod(shape))
    ap = k.mem[:, off:off + n]
    if len(shape) == 2:
        return ap.rearrange("p (a b) -> p a b", a=shape[0])
    if len(shape) == 3:
        return ap.rearrange("p (a b c) -> p a b c", a=shape[0], b=shape[1])
    if len(shape) == 4:
        return ap.rearrange("p (a b c d) -> p a b c d", a=shape[0], b=shape[1], c=shape[2])
    return ap


def spread(ap, dim, n):
    dims = [list(x) for x in ap.ap]
    dims.insert(dim, [0, n])
    return bass.AP(ap.tensor, ap.offset, dims)


def backwards(ap):
    dims = [list(x) for x in ap.ap]
    step, n = dims[-1]
    dims[-1] = [-step, n]
    return bass.AP(ap.tensor, ap.offset + step * (n - 1), dims)


class Counter:

    def __init__(self, sem):
        self.sem, self.n = sem, 0

    def inc(self, ins, by=1):
        ins.then_inc(self.sem, by)
        self.n += by
        return self.n


class Kernel:
    def __init__(self, nc, ctx, dram, out):
        self.nc, self.ctx, self.d, self.out = nc, ctx, dram, out
        self.mem = ctx.enter_context(nc.sbuf_tensor("mem", [P, TOTAL], F32))
        self.ps = ctx.enter_context(nc.psum_tensor("ps", [P, 8, 512], F32))
        self.phase_sems = []
        self.w_loaded = [self.lasting_sem(f"w_loaded{i}") for i in range(NRING)]
        self.chunk_used = self.lasting_sem("chunk_used")
        self.dve_step = Counter(self.lasting_sem("dve_step"))
        self.act_step = Counter(self.lasting_sem("act_step"))
        self.ident = view(self, C0, P)
        self.g_even = view(self, C0 + 128, KD)
        self.g_odd = view(self, C0 + 136, KD)
        self.g_mem = view(self, C0 + 144, KD)
        self.g_mix = view(self, C0 + 152, KD)
        self.stat = view(self, C0 + 160, 64)
        self.misc = C0 + 256

    def lasting_sem(self, name):
        return self.ctx.enter_context(self.nc.semaphore(name))

    def sem(self, name):
        s = self.nc.alloc_semaphore(name)
        self.phase_sems.append(s)
        return s

    def end_phase(self):
        self.nc.all_engine_barrier()
        self.nc.clear_and_free_semaphores(self.phase_sems)
        self.nc.all_engine_barrier()
        self.phase_sems = []

    def link(self, eng, ins, which=None):
        c = which or self.dve_step
        c.inc(ins)
        eng.wait_ge(c.sem, c.n)

    def slot(self, n):
        return RING + (n % NRING) * SLOT



def weight_chunks(k):
    d = k.d
    w = []

    def cols(phase, src, lo, n):
        w.append((phase, src.rearrange("(k p) n -> p k n", p=P)[:, :, lo:lo + n]))

    for layer in (d["ev_w_mem_kv"][0], d["od_w_mem_kv"][0]):
        for c in range(2):
            cols("even_in", layer, 512 * c, 512)
    for _, lo, n, _ in EVEN_IN:
        cols("even_in", d["ev_w_in"][0], lo, n)

    def out_proj(phase, src):
        for n in range(2):
            for half in range(2):
                w.append((phase, src[half * D:(half + 1) * D].rearrange("(k p) n -> p k n", p=P)
                          [:, :, 512 * n:512 * n + 512]))

    out_proj("even_out", d["ev_w_out"][0])
    for _, lo, n, _ in ODD_IN:
        cols("odd_in", d["od_w_in"][0], lo, n)
    for kv in range(2):
        for half in range(2):
            w.append(("compress", d["od_cmp_w1"][0, kv].rearrange("(l d) n -> d l n", d=DH)
                      [:, 16 * half:16 * half + 16, :]))
    out_proj("odd_out", d["od_w_out"][0])
    for _, lo, n, _ in MIX_IN:
        cols("mix_in", d["w_in_2"][0], lo, n)
    w.append(("mix_mid", d["ssm_w_glu_2"][0].rearrange("(k p) n -> p k n", p=P)))
    w.append(("mix_mid", d["w_ssm_out_2"][0].rearrange("(k p) n -> p k n", p=P)))
    w.append(("mix_mid", d["w_fourier_out_2"][0].rearrange("(k p) n -> p k n", p=P)))
    for c in range(2):
        cols("mix_out", d["w_out_2"][0], 512 * c, 512)
    return w


PHASES = ["even_in", "even_mix", "even_out", "odd_in", "compress", "nsa", "odd_out", "mix_in", "ssm", "mix_mid",
          "mix_out"]

EVEN_IN = ([("za", 0, 384, False), ("za", 384, 384, False), ("rq", 768, 512, False), ("rk", 1280, 512, False),
            ("rv", 1792, 384, False), ("rv", 2176, 384, False), ("xq", 2560, 512, True)]
           + [("gate", 3072 + 512 * i, 512, False) for i in range(4)])
ODD_IN = ([("q", 512 * i, 512, True) for i in range(3)]
          + [("kcvc", 1536, 512, True), ("ks", 2048, 256, True), ("vs", 2304, 256, False), ("kw", 2560, 256, True),
             ("vw", 2816, 256, False), ("gl", 3072, 36, False), ("xq", 3108, 512, True)]
          + [("gate", 3620 + 512 * i, 512, False) for i in range(4)])
MIX_IN = ([("us", 512, 512, False), ("uf", 0, 512, True)] + [("gate", 1024 + 512 * i, 512, False) for i in range(4)])


def load_weights(k, eng, phase):
    at = PHASES.index(phase)
    while k.next_chunk < len(k.chunks):
        n = k.next_chunk
        if n >= NRING and PHASES.index(k.chunks[n - NRING][0]) > at:
            return
        src = k.chunks[n][1]
        if n >= NRING:
            eng.wait_ge(k.chunk_used, n - NRING + 1)
        a, b = src.shape[1], src.shape[2]
        eng.dma_start(view(k, k.slot(n), a, b), src).then_inc(k.w_loaded[n % NRING], 16)
        k.next_chunk += 1


def first_chunk(k, phase):
    return [i for i, c in enumerate(k.chunks) if c[0] == phase][0]


def wait_chunk(k, eng, n):
    eng.wait_ge(k.w_loaded[n % NRING], 16 * (n // NRING + 1))


class Group:

    def __init__(self, i, n, what, col, width, turned, t, last, done, evac, place):
        self.i, self.n, self.what, self.col, self.width, self.turned, self.t = i, n, what, col, width, turned, t
        self.last, self.done, self.evac, self.place = last, done, evac, place
        self.bank = i % 8


def plan(table, first, row_tiles, on_act):
    groups, done, place = [], 0, {"act": 0, "dve": 0}
    base_col = {}
    for c, (what, lo, n, turned) in enumerate(table):
        base_col.setdefault(what, lo)
        tiles = n // P if turned else row_tiles
        for t in range(tiles):
            last = t == tiles - 1
            done += 0 if last else 1
            eng = "act" if what in on_act else "dve"
            place[eng] += 1
            groups.append(Group(len(groups), first + c, what, lo - base_col[what], n, turned, t, last, done, eng,
                                place[eng]))
    return groups


class Projection:

    def __init__(self, k, name, table, first, row_tiles, on_act, uT, n_tok):
        self.k, self.uT, self.n_tok = k, uT, n_tok
        self.groups = plan(table, first, row_tiles, on_act)
        self.group_done = k.sem(name + "_group_done")
        self.emptied = {"act": k.sem(name + "_emptied_by_act"), "dve": k.sem(name + "_emptied_by_dve")}

    def tensor(self, pe):
        k = self.k
        for g in self.groups:
            if g.t == 0:
                wait_chunk(k, pe, g.n)
            if g.i >= 8:
                old = self.groups[g.i - 8]
                pe.wait_ge(self.emptied[old.evac], old.place)
            w = view(k, k.slot(g.n), KD, g.width)
            for kk in range(KD):
                if g.turned:
                    mm = pe.matmul(k.ps[:, g.bank, 0:self.n_tok], w[:, kk, g.t * P:(g.t + 1) * P],
                                   self.uT[:, kk, :], start=kk == 0, stop=kk == KD - 1)
                else:
                    mm = pe.matmul(k.ps[:, g.bank, 0:g.width], self.uT[:, kk, g.t * P:(g.t + 1) * P],
                                   w[:, kk, :], start=kk == 0, stop=kk == KD - 1)
            mm.then_inc(k.chunk_used if g.last else self.group_done, 1)

    def wait_group(self, eng, g):
        if g.last:
            eng.wait_ge(self.k.chunk_used, g.n + 1)
        else:
            eng.wait_ge(self.group_done, g.done)



class Norm:

    def __init__(self, k, name, src, T, uT=None, gT=None, scratch=None, stat=0, prior=None, dst=None):
        self.k, self.src, self.T, self.uT, self.gT, self.scratch = k, src, T, uT, gT, scratch
        self.dst = src if dst is None else dst
        self.ss = k.stat[:, stat:stat + T]
        self.ms = k.stat[:, stat + T:stat + 2 * T]
        self.sd = k.stat[:, stat + 2 * T:stat + 3 * T]
        self.rs = k.stat[:, stat + 3 * T:stat + 4 * T]
        self.squared, self.mean, self.root = k.sem(name + "_squared"), k.sem(name + "_mean"), k.sem(name + "_root")
        self.normed, self.turned, self.ready = k.sem(name + "_normed"), k.sem(name + "_turned"), k.sem(name + "_uT")
        self.prior = prior

    def scalar_sums(self, act, loaded=None):
        for m in range(self.T):
            if loaded is not None:
                act.wait_ge(loaded[m], 16)
            if m:
                act.wait_ge(self.squared, m)
            ins = act.activation(self.scratch, self.src[:, m, :], ACT.Square, accum_out=self.ss[:, m:m + 1])
            ins.then_inc(self.squared, 1)

    def vector_mean(self, dve):
        dve.wait_ge(self.squared, self.T)
        dve.tensor_scalar(self.ms, self.ss, 1.0 / D, EPS, ALU.mult, ALU.add).then_inc(self.mean, 1)

    def scalar_root(self, act):
        act.wait_ge(self.mean, 1)
        act.activation(self.sd, self.ms, ACT.Sqrt).then_inc(self.root, 1)

    def vector_scale(self, dve):
        dve.wait_ge(self.root, 1)
        self.k.link(dve, dve.reciprocal(self.rs, self.sd))
        for m in range(self.T):
            dve.tensor_scalar(self.dst[:, m, :], self.src[:, m, :], self.rs[:, m:m + 1], None,
                              ALU.mult).then_inc(self.normed, 1)

    def tensor_turn(self, pe):
        pe.wait_ge(self.normed, self.T)
        for kk in range(KD):
            if self.prior:
                pe.wait_ge(self.prior, kk + 1)
            for m in range(self.T):
                t = pe.transpose(self.k.ps[:, kk, m * P:(m + 1) * P], self.dst[:, m, kk * P:(kk + 1) * P],
                                 self.k.ident)
            t.then_inc(self.turned, 1)

    def scalar_out(self, act):
        for kk in range(KD):
            act.wait_ge(self.turned, kk + 1)
            act.activation(self.uT[:, kk, :], self.k.ps[:, kk, 0:self.T * P], ACT.Copy,
                           scale=self.gT[:, kk:kk + 1]).then_inc(self.ready, 1)



MEM_KV_E = [("mk_e", 0, 512, True), ("mv_e", 512, 512, False)]
MEM_KV_O = [("mk_o", 0, 512, True), ("mv_o", 512, 512, False)]


def even_in(k):
    nc, d = k.nc, k.d
    mem_nat = view(k, Y0, MT, D)
    memT = view(k, U0 + 6144, KD, N_MEM)
    x_nat = view(k, H0, NT, D)
    uT = view(k, U0, KD, S)
    rot = view(k, U0 + 4096, 4, NT, 64)
    tmp = view(k, U0 + 5120, 4, 64)
    squares = view(k, Z0, D)
    za = view(k, H0, NT, POOL_W)
    rq, rk = view(k, Z0, NT, 512), view(k, Z0 + 2048, NT, 512)
    rv = view(k, Z0 + 4096, NT, RH * RDV)
    k.xqT = view(k, Z0 + 7168, MH, S)
    k.mk = [view(k, Z0 + 9216, MH, N_MEM), view(k, Z0 + 11264, MH, N_MEM)]
    k.mv = [view(k, Z0 + 10240, MT, 512), view(k, Z0 + 12288, MT, 512)]
    y = view(k, Y0, NT, D_IN)

    zeros = view(k, Z0 + 14336, D)
    const_loaded, rot_loaded = k.sem("const_loaded"), k.sem("rot_loaded")
    zeroed, ypad_zeroed = k.sem("zeroed"), k.sem("ypad_zeroed")
    mem_loaded = [k.sem(f"mem_loaded{m}") for m in range(MT)]
    x_loaded = [k.sem(f"x_loaded{m}") for m in range(NT)]
    norm_m = Norm(k, "norm_mem", mem_nat, MT, memT, k.g_mem, squares, 0)
    norm_x = Norm(k, "norm_even", x_nat, NT, uT, k.g_even, squares, 8, prior=norm_m.ready)
    kv = Projection(k, "mem_kv", MEM_KV_E + MEM_KV_O, 0, MT, ("mv_e", "mv_o"), memT, N_MEM)
    pr = Projection(k, "even", EVEN_IN, 4, NT, ("gate",), uT, S)
    n_kv = len(kv.groups)
    kv_last = {e: sum(g.evac == e for g in kv.groups) for e in ("act", "dve")}

    with nc.Block() as block:
        @block.sync
        def _(sp):
            mem_r = d["mem"][0].rearrange("(m p) n -> p m n", p=P)
            x_r = d["x"][0].rearrange("(m p) n -> p m n", p=P)
            for m in range(MT):
                sp.dma_start(mem_nat[:, m, :], mem_r[:, m, :]).then_inc(mem_loaded[m], 16)
            sp.dma_start(k.ident, d["ident"]).then_inc(const_loaded, 16)
            with nc.allow_non_contiguous_dma(reason="a norm's gains, one per partition"):
                sp.dma_start(k.g_mem, d["mem_norm_g"].rearrange("(k p) -> p k", p=P)).then_inc(const_loaded, 16)
                for m in range(NT):
                    sp.dma_start(x_nat[:, m, :], x_r[:, m, :]).then_inc(x_loaded[m], 16)
                sp.dma_start(k.g_even, d["norm_g"][0].rearrange("(k p) -> p k", p=P)).then_inc(const_loaded, 16)
                sp.dma_start(k.g_odd, d["norm_g"][1].rearrange("(k p) -> p k", p=P)).then_inc(const_loaded, 16)
                sp.dma_start(k.g_mix, d["mix_norm_g_2"][0].rearrange("(k p) -> p k", p=P)).then_inc(const_loaded, 16)
            sp.dma_start(view(k, U0 + 4096, 1024), d["rot"]).then_inc(rot_loaded, 16)
            load_weights(k, sp, "even_in")
            sp.wait_ge(zeroed, 1)
            sp.dma_start(k.ypad[NE * SLOTS:].rearrange("(p r) n -> p r n", r=8),
                         spread(zeros[0:XB * SLOTS // 8, :], 1, 8)).then_inc(ypad_zeroed, 16)
            sp.wait_ge(ypad_zeroed, 16)

        @block.gpsimd
        def _(pool):
            pool.memset(zeros, 0.0).then_inc(zeroed, 1)

        @block.tensor
        def _(pe):
            pe.wait_ge(const_loaded, 16 * 5)
            norm_m.tensor_turn(pe)
            norm_x.tensor_turn(pe)
            pe.wait_ge(norm_x.ready, KD)
            kv.tensor(pe)
            for e, s in kv.emptied.items():
                pe.wait_ge(s, kv_last[e])
            pr.tensor(pe)

        @block.scalar
        def _(act):
            norm_m.scalar_sums(act, mem_loaded)
            norm_m.scalar_root(act)
            act.wait_ge(norm_m.squared, MT)
            norm_x.scalar_sums(act, x_loaded)
            norm_x.scalar_root(act)
            act.wait_ge(const_loaded, 16 * 5)
            norm_m.scalar_out(act)
            norm_x.scalar_out(act)
            for g in kv.groups:
                if g.evac == "act":
                    kv.wait_group(act, g)
                    dst = k.mv[g.what == "mv_o"]
                    act.activation(dst[:, g.t, :], k.ps[:, g.bank, :], ACT.Copy).then_inc(kv.emptied["act"], 1)
            for g in pr.groups:
                if g.evac == "act":
                    pr.wait_group(act, g)
                    act.activation(y[:, g.t, g.col:g.col + g.width], k.ps[:, g.bank, :],
                                   ACT.Silu).then_inc(pr.emptied["act"], 1)

        @block.vector
        def _(dve):
            norm_m.vector_mean(dve)
            norm_m.vector_scale(dve)
            norm_x.vector_mean(dve)
            norm_x.vector_scale(dve)
            for g in kv.groups:
                if g.evac == "dve":
                    kv.wait_group(dve, g)
                    dst = k.mk[g.what == "mk_o"]
                    dve.tensor_copy(dst[:, g.t, :], k.ps[:, g.bank, 0:N_MEM]).then_inc(kv.emptied["dve"], 1)
            dve.wait_ge(rot_loaded, 16)
            for g in pr.groups:
                if g.evac != "dve":
                    continue
                pr.wait_group(dve, g)
                bank = k.ps[:, g.bank, 0:g.width]
                if g.what in ("rq", "rk"):
                    dve.wait_ge(pr.emptied["dve"], g.place - 1)
                    tab = 0 if g.what == "rq" else 2
                    cos, sin = (spread(rot[:, tab + i, g.t, :], 1, RH) for i in range(2))
                    x = bank.rearrange("p (h c) -> p h c", h=RH)
                    o = (rq if g.what == "rq" else rk)[:, g.t, :].rearrange("p (h c) -> p h c", h=RH)
                    dve.tensor_tensor(o[:, :, 0:64], x[:, :, 0:64], cos, ALU.mult)
                    k.link(dve, dve.tensor_tensor(tmp, x[:, :, 64:128], sin, ALU.mult))
                    k.link(dve, dve.tensor_tensor(o[:, :, 0:64], o[:, :, 0:64], tmp, ALU.subtract))
                    dve.tensor_tensor(o[:, :, 64:128], x[:, :, 0:64], sin, ALU.mult)
                    k.link(dve, dve.tensor_tensor(tmp, x[:, :, 64:128], cos, ALU.mult))
                    ins = dve.tensor_tensor(o[:, :, 64:128], o[:, :, 64:128], tmp, ALU.add)
                elif g.what == "xq":
                    ins = dve.tensor_scalar(k.xqT[:, g.t, :], bank, -(MDH ** -0.5), None, ALU.mult)
                else:
                    dst = za if g.what == "za" else rv
                    ins = dve.tensor_copy(dst[:, g.t, g.col:g.col + g.width], bank)
                ins.then_inc(pr.emptied["dve"], 1)



class MemAttention:

    def __init__(self, k, name, layer, xqT, scratch, stat):
        self.k, self.mk, self.mv, self.xqT = k, k.mk[layer], k.mv[layer], xqT
        self.p = view(k, scratch, 2, N_MEM)
        self.pT = view(k, scratch + 2 * N_MEM, 2, MT, P)
        self.st = view(k, stat, 2, 4)
        self.y = view(k, Y0, NT, D_IN)
        self.scored, self.low, self.exped, self.turned, self.copied, self.mixed, self.stored = (
            k.sem(f"{name}_{n}") for n in ("scored", "low", "exped", "turned", "copied", "mixed", "stored"))
        self.steps = [(h, t) for h in range(MH) for t in range(NT)]

    def tensor(self, pe):
        k, n = self.k, len(self.steps)
        for u in range(n + 2):
            if u < n:
                h, t = self.steps[u]
                if u >= 2:
                    pe.wait_ge(self.exped, u - 1)
                pe.matmul(k.ps[:, u % 2, 0:N_MEM], self.xqT[:, h, t * P:(t + 1) * P], self.mk[:, h, :],
                          start=True, stop=True).then_inc(self.scored, 1)
            if 1 <= u <= n:
                v = u - 1
                pe.wait_ge(self.exped, v + 1)
                if v >= 2:
                    pe.wait_ge(self.copied, v - 1)
                for m in range(MT):
                    tr = pe.transpose(k.ps[:, 2 + v % 2, m * P:(m + 1) * P], self.p[:, v % 2, m * P:(m + 1) * P],
                                      k.ident)
                tr.then_inc(self.turned, 1)
            if u >= 2:
                v = u - 2
                h = self.steps[v][0]
                pe.wait_ge(self.copied, v + 1)
                if v >= 2:
                    pe.wait_ge(self.stored, v - 1)
                for m in range(MT):
                    mm = pe.matmul(k.ps[:, 4 + v % 2, 0:MDH], self.pT[:, v % 2, m, :],
                                   self.mv[:, m, h * MDH:(h + 1) * MDH], start=m == 0, stop=m == MT - 1)
                mm.then_inc(self.mixed, 1)

    def scalar(self, act):
        for u in range(len(self.steps)):
            act.wait_ge(self.low, u + 1)
            if u >= 2:
                act.wait_ge(self.turned, u - 1)
                act.wait_ge(self.stored, u - 1)
            act.activation(self.p[:, u % 2, :], self.k.ps[:, u % 2, 0:N_MEM], ACT.Exp, scale=-1.0,
                           bias=self.st[:, u % 2, 0:1], accum_out=self.st[:, u % 2, 1:2]).then_inc(self.exped, 1)

    def vector(self, dve):
        k, n = self.k, len(self.steps)
        for u in range(n + 2):
            if u < n:
                dve.wait_ge(self.scored, u + 1)
                if u >= 2:
                    dve.wait_ge(self.exped, u - 1)
                dve.tensor_reduce(self.st[:, u % 2, 0:1], k.ps[:, u % 2, 0:N_MEM], AX_X, ALU.min).then_inc(self.low, 1)
            if 1 <= u <= n:
                v = u - 1
                dve.wait_ge(self.turned, v + 1)
                if v >= 2:
                    dve.wait_ge(self.mixed, v - 1)
                dve.tensor_copy(self.pT[:, v % 2, :, :], k.ps[:, 2 + v % 2, 0:N_MEM]
                                .rearrange("p (m q) -> p m q", m=MT)).then_inc(self.copied, 1)
            if u >= 2:
                v = u - 2
                h, t = self.steps[v]
                dve.wait_ge(self.mixed, v + 1)
                k.link(dve, dve.reciprocal(self.st[:, v % 2, 2:3], self.st[:, v % 2, 1:2]))
                ys = self.y[:, t, 1536 + h * MDH:1536 + (h + 1) * MDH]
                dve.scalar_tensor_tensor(out=ys, in0=k.ps[:, 4 + v % 2, 0:MDH], scalar=self.st[:, v % 2, 2:3],
                                         in1=ys, op0=ALU.mult, op1=ALU.mult).then_inc(self.stored, 1)



def even_mix(k):
    nc, d = k.nc, k.d
    za = view(k, H0, NT, POOL_W)
    rq, rk = view(k, Z0, NT, 512), view(k, Z0 + 2048, NT, 512)
    rv = view(k, Z0 + 4096, NT, RH * RDV)
    rqT, rkT = view(k, U0, RH, S), view(k, U0 + 2048, RH, S)
    decay = view(k, U0 + 4096, RH, S)
    att = view(k, Z0, 2, NT, S)
    pooled = [view(k, U0 + 7168, 2, S), view(k, H0 + 3072, 2, S)]
    band = view(k, Z0 + 13312, N_WIN * 3, P)
    pool_w = view(k, Z0 + 14848, N_WIN, 2, PG)
    pscale = view(k, Z0 + 16384, POOL_W)
    ln = view(k, k.misc + 1024, 2, RDV)
    bn = view(k, k.misc + 1408, 2, NT, 6)
    mv = view(k, k.misc + 1456, 2, NT, 2)
    sd = view(k, k.misc + 1472, 2, NT, 3)
    ptmp = view(k, U0 + 6144, 2, PG)
    y = view(k, Y0, NT, D_IN)
    ma = MemAttention(k, "mem_e", 0, k.xqT, k.misc, k.misc + 1536)
    tab, turned, copied_a, copied_v, scored, decayed, mixed, ln_in, ln_root, ln_out = (
        k.sem("ret_" + n) for n in ("tables", "turned", "copied_act", "copied_dve", "scored", "decayed", "mixed",
                                    "moments", "root", "normed"))
    pool_in, pooled_by, pool_mm, pool_out = (k.sem("pool_" + n) for n in ("banded", "copied", "mixed", "stored"))

    with nc.Block() as block:
        @block.sync
        def _(sp):
            sp.dma_start(view(k, U0 + 4096, 2048), d["decay"]).then_inc(tab, 16)
            sp.dma_start(view(k, Z0 + 13312, 1536), d["band"]).then_inc(tab, 16)
            sp.dma_start(pool_w[0:PH], d["ev_pool_w"][0].rearrange("g (h c) n -> c g h n", h=2)).then_inc(tab, 16)
            sp.dma_start(pscale, d["ev_pool_scale"].to_broadcast([P, POOL_W])).then_inc(tab, 16)
            load_weights(k, sp, "even_mix")

        @block.tensor
        def _(pe):
            for i in range(2 * RH):
                src = rq if i % 2 == 0 else rk
                for m in range(NT):
                    t = pe.transpose(k.ps[:, i, m * P:(m + 1) * P], src[:, m, (i // 2) * P:(i // 2 + 1) * P], k.ident)
                t.then_inc(turned, 1)
            pe.wait_ge(copied_a, RH)
            pe.wait_ge(copied_v, RH)
            for h in range(RH + 1):
                if h < RH:
                    for kt in range(NT):
                        if h:
                            pe.wait_ge(decayed, NT * (h - 1) + kt + 1)
                        pe.matmul(k.ps[:, kt, kt * P:S], rkT[:, h, kt * P:(kt + 1) * P], rqT[:, h, kt * P:S],
                                  start=True, stop=True).then_inc(scored, 1)
                if h:
                    g = h - 1
                    pe.wait_ge(decayed, NT * (g + 1))
                    if g >= 2:
                        pe.wait_ge(ln_out, g - 1)
                    for t in range(NT):
                        bank = 4 + 2 * (g % 2) + t // 2
                        o = (t % 2) * RDV
                        for kt in range(t + 1):
                            mm = pe.matmul(k.ps[:, bank, o:o + RDV], att[:, g % 2, kt, t * P:(t + 1) * P],
                                           rv[:, kt, g * RDV:(g + 1) * RDV], start=kt == 0, stop=kt == t)
                    mm.then_inc(mixed, 1)
            pe.wait_ge(ln_out, RH)
            pe.wait_ge(tab, 16 * 4)
            for g in range(N_WIN):
                for c in range(2):
                    i = 2 * g + c
                    if i >= 2:
                        pe.wait_ge(pooled_by, i - 1)
                    for t in range(NT):
                        o = k.ps[0:PH, i % 2, t * P:(t + 1) * P]
                        ch = slice(i * PH, (i + 1) * PH)
                        if t:
                            pe.matmul(o, za[:, t - 1, ch], band[:, 3 * g + 2, :], start=True, stop=False)
                        mm = pe.matmul(o, za[:, t, ch], band[:, 3 * g + (t > 0), :], start=t == 0, stop=True)
                    mm.then_inc(pool_in, 1)
                for t in range(NT):
                    u = NT * g + t
                    pe.wait_ge(pooled_by, 2 * g + 2)
                    if u >= 4:
                        pe.wait_ge(pool_out, u - 3)
                    for c in range(2):
                        mm = pe.matmul(k.ps[:, 2 + u % 4, 0:PG], pooled[g % 2][0:PH, c, t * P:(t + 1) * P],
                                       pool_w[0:PH, g, c, :], start=c == 0, stop=c == 1)
                    mm.then_inc(pool_mm, 1)
            pe.wait_ge(pool_out, N_WIN * NT)
            ma.tensor(pe)

        @block.scalar
        def _(act):
            for h in range(RH):
                act.wait_ge(turned, 2 * h + 1)
                act.copy(rqT[:, h, :], k.ps[:, 2 * h, :]).then_inc(copied_a, 1)
            for h in range(RH):
                act.wait_ge(ln_in, h + 1)
                act.activation(sd[:, h % 2, :, 1], sd[:, h % 2, :, 0], ACT.Sqrt).then_inc(ln_root, 1)
            for i in range(2 * N_WIN):
                act.wait_ge(pool_in, i + 1)
                if i >= 4:
                    act.wait_ge(pool_mm, NT * (i // 2 - 1))
                act.copy(pooled[(i // 2) % 2][0:PH, i % 2, :], k.ps[0:PH, i % 2, :]).then_inc(pooled_by, 1)
            ma.scalar(act)

        @block.vector
        def _(dve):
            for h in range(RH):
                dve.wait_ge(turned, 2 * h + 2)
                dve.tensor_copy(rkT[:, h, :], k.ps[:, 2 * h + 1, :]).then_inc(copied_v, 1)
            dve.wait_ge(tab, 16 * 4)
            dve.wait_ge(turned, 2 * RH)
            for h in range(RH + 1):
                if h < RH:
                    for kt in range(NT):
                        dve.wait_ge(scored, NT * h + kt + 1)
                        if h >= 2 and kt == 0:
                            dve.wait_ge(mixed, h - 1)
                        dve.tensor_tensor(att[:, h % 2, kt, kt * P:S], k.ps[:, kt, kt * P:S],
                                          decay[:, h, 0:S - kt * P], ALU.mult).then_inc(decayed, 1)
                if h:
                    g = h - 1
                    dve.wait_ge(mixed, h)
                    o = [k.ps[:, 4 + 2 * (g % 2) + t // 2, (t % 2) * RDV:(t % 2 + 1) * RDV] for t in range(NT)]
                    for t in range(NT):
                        ins = dve.bn_stats(bn[:, g % 2, t, :], o[t])
                    k.link(dve, ins)
                    for t in range(NT):
                        ins = dve.bn_aggr(mv[:, g % 2, t, :], bn[:, g % 2, t, :])
                    k.link(dve, ins)
                    dve.tensor_scalar(sd[:, g % 2, :, 0], mv[:, g % 2, :, 1], EPS, None, ALU.add).then_inc(ln_in, 1)
                    dve.wait_ge(ln_root, g + 1)
                    k.link(dve, dve.reciprocal(sd[:, g % 2, :, 2], sd[:, g % 2, :, 1]))
                    for t in range(NT):
                        ys = y[:, t, POOL_W + g * RDV:POOL_W + (g + 1) * RDV]
                        k.link(dve, dve.tensor_scalar(ln[:, t % 2, :], o[t], mv[:, g % 2, t, 0:1],
                                                      sd[:, g % 2, t, 2:3], ALU.subtract, ALU.mult))
                        ins = dve.tensor_tensor(ys, ys, ln[:, t % 2, :], ALU.mult)
                        if t < NT - 1:
                            k.link(dve, ins)
                    ins.then_inc(ln_out, 1)
                    dve.wait_ge(ln_out, g + 1)
            for g in range(N_WIN):
                for t in range(NT):
                    u = NT * g + t
                    dve.wait_ge(pool_mm, u + 1)
                    if u >= 2:
                        dve.wait_ge(pool_out, u - 1)
                    ys = y[:, t, g * PG:(g + 1) * PG]
                    k.link(dve, dve.tensor_tensor(ptmp[:, u % 2, :], k.ps[:, 2 + u % 4, 0:PG],
                                                  pscale[:, g * PG:(g + 1) * PG], ALU.mult))
                    dve.tensor_tensor(ys, ys, ptmp[:, u % 2, :], ALU.mult).then_inc(pool_out, 1)
            ma.vector(dve)



def out_projection(k, name, phase, h_dram, spill):
    nc = k.nc
    y, yT = view(k, Y0, NT, D_IN), view(k, U0, KI, S)
    h = view(k, H0, NT, D)
    first = first_chunk(k, phase)
    turned, out_a, out_v, loaded, bank_done, added, spilled = (
        k.sem(f"{name}_{n}") for n in ("turned", "yT_act", "yT_dve", "h_loaded", "bank_done", "added", "spilled"))

    with nc.Block() as block:
        @block.sync
        def _(sp):
            sp.dma_start(h, h_dram.rearrange("(m p) n -> p m n", p=P)).then_inc(loaded, 16)
            load_weights(k, sp, phase)
            if spill is not None:
                sp.wait_ge(added, 2 * NT)
                sp.dma_start(spill.rearrange("(m p) n -> p m n", p=P), h).then_inc(spilled, 16)
                sp.wait_ge(spilled, 16)

        @block.tensor
        def _(pe):
            for kk in range(KI):
                if kk >= 8:
                    pe.wait_ge(out_v if kk % 2 else out_a, (kk - 8) // 2 + 1)
                for m in range(NT):
                    t = pe.transpose(k.ps[:, kk % 8, m * P:(m + 1) * P], y[:, m, kk * P:(kk + 1) * P], k.ident)
                t.then_inc(turned, 1)
            pe.wait_ge(out_a, KI // 2)
            pe.wait_ge(out_v, KI // 2)
            for n in range(2):
                for half in range(2):
                    c = first + 2 * n + half
                    wait_chunk(k, pe, c)
                    w = view(k, k.slot(c), KD, 512)
                    for m in range(NT):
                        for kk in range(KD):
                            mm = pe.matmul(k.ps[:, 4 * n + m, :], yT[:, half * KD + kk, m * P:(m + 1) * P],
                                           w[:, kk, :], start=half == 0 and kk == 0,
                                           stop=half == 1 and kk == KD - 1)
                        if m < NT - 1 and half == 1:
                            mm.then_inc(bank_done, 1)
                    mm.then_inc(k.chunk_used, 1)

        @block.scalar
        def _(act):
            for kk in range(0, KI, 2):
                act.wait_ge(turned, kk + 1)
                act.copy(yT[:, kk, :], k.ps[:, kk % 8, :]).then_inc(out_a, 1)

        @block.vector
        def _(dve):
            for kk in range(1, KI, 2):
                dve.wait_ge(turned, kk + 1)
                dve.tensor_copy(yT[:, kk, :], k.ps[:, kk % 8, :]).then_inc(out_v, 1)
            dve.wait_ge(loaded, 16)
            for n in range(2):
                for m in range(NT):
                    if m < NT - 1:
                        dve.wait_ge(bank_done, (NT - 1) * n + m + 1)
                    else:
                        dve.wait_ge(k.chunk_used, first + 2 * n + 2)
                    hs = h[:, m, n * 512:(n + 1) * 512]
                    dve.tensor_tensor(hs, hs, k.ps[:, 4 * n + m, :], ALU.add).then_inc(added, 1)



def odd_in(k):
    nc, d = k.nc, k.d
    h = view(k, H0, NT, D)
    uT = view(k, U0, KD, S)
    squares = view(k, U0 + 4096, D)
    y = view(k, Y0, NT, D_IN)
    k.kc2 = view(k, H0, 2, 2, NKV, S)
    k.qT = view(k, Z0, NH, S)
    k.ksT, k.kwT = view(k, Z0 + 6144, NKV, S), view(k, Z0 + 7168, NKV, S)
    k.xqT = view(k, Z0 + 8192, MH, S)
    k.vs, k.vw = view(k, Z0 + 13312, NT, 256), view(k, Z0 + 14336, NT, 256)
    k.gsig = view(k, Z0 + 15360, NT, 36)
    pe_nat = view(k, Z0 + 15504, DH)
    k.posT = view(k, Z0 + 15632, 2, 2, 16)
    from31 = view(k, Z0 + 15696, 1)
    norm = Norm(k, "norm_odd", h, NT, uT, k.g_odd, squares, 0)
    first = first_chunk(k, "odd_in")
    pr = Projection(k, "odd", ODD_IN, first, NT, ("gate", "gl"), uT, S)
    small, posed, posed_out = k.sem("odd_small"), k.sem("odd_positions"), k.sem("odd_positions_copied")

    with nc.Block() as block:
        @block.sync
        def _(sp):
            sp.dma_start(pe_nat[0:64, :], d["od_cmp_pe"][0].rearrange("a l d -> (a l) d")).then_inc(small, 16)
            sp.dma_start(from31, d["from31"]).then_inc(small, 16)
            load_weights(k, sp, "odd_in")

        @block.tensor
        def _(pe):
            norm.tensor_turn(pe)
            pe.wait_ge(norm.ready, KD)
            pe.wait_ge(small, 32)
            pe.transpose(k.ps[:, 7, 0:64], pe_nat[0:64, :], k.ident[0:64, 0:64]).then_inc(posed, 1)
            pe.wait_ge(posed_out, 1)
            pr.tensor(pe)

        @block.scalar
        def _(act):
            norm.scalar_sums(act)
            norm.scalar_root(act)
            norm.scalar_out(act)
            for g in pr.groups:
                if g.evac != "act":
                    continue
                pr.wait_group(act, g)
                bank = k.ps[:, g.bank, 0:g.width]
                if g.what == "gl":
                    ins = act.activation(k.gsig[:, g.t, :], bank, ACT.Sigmoid)
                else:
                    ins = act.activation(y[:, g.t, g.col:g.col + g.width], bank, ACT.Silu)
                ins.then_inc(pr.emptied["act"], 1)

        @block.vector
        def _(dve):
            norm.vector_mean(dve)
            norm.vector_scale(dve)
            dve.wait_ge(posed, 1)
            dve.tensor_copy(k.posT, k.ps[:, 7, 0:64].rearrange("p (a b c) -> p a b c", a=2, b=2)).then_inc(posed_out, 1)
            dve.wait_ge(posed_out, 1)
            for g in pr.groups:
                if g.evac != "dve":
                    continue
                pr.wait_group(dve, g)
                bank = k.ps[:, g.bank, 0:S if g.turned else g.width]
                if g.what == "q":
                    ins = dve.tensor_scalar(k.qT[:, g.col // P + g.t, :], bank, -(DH ** -0.5), None, ALU.mult)
                elif g.what == "xq":
                    ins = dve.tensor_scalar(k.xqT[:, g.t, :], bank, -(MDH ** -0.5), None, ALU.mult)
                elif g.what == "kcvc":
                    for half in range(2):
                        dst = k.kc2[:, g.t // 2, half, g.t % 2, :].rearrange("p (j l) -> p j l", l=16)
                        ins = dve.tensor_tensor(dst, bank.rearrange("p (j l) -> p j l", l=16),
                                                spread(k.posT[:, g.t // 2, half, :], 1, S // 16), ALU.add)
                elif g.turned:
                    ins = dve.tensor_copy({"ks": k.ksT, "kw": k.kwT}[g.what][:, g.t, :], bank)
                else:
                    ins = dve.tensor_copy({"vs": k.vs, "vw": k.vw}[g.what][:, g.t, :], bank)
                ins.then_inc(pr.emptied["dve"], 1)



def compress(k):
    nc, d = k.nc, k.d
    w2 = view(k, U0, 2, 2, DH)
    b1 = view(k, U0 + 512, 2, 2)
    hid = view(k, U0 + 516, 2, 2, NKV * NCMP)
    k.kcmpT = view(k, Z0 + 10240, NKV, NCMP)
    k.vcmp = view(k, Z0 + 10302, NKV, DH)
    table = view(k, U0 + 1024, NH)
    hot = view(k, U0 + 1040, 2048)
    tab = view(k, U0 + 3088, 2048)
    first = first_chunk(k, "compress")
    small, masked, hid_done, hid_out, k_done, k_out, t_done, t_out = (
        k.sem("cmp_" + n) for n in ("small", "mask_row", "hidden", "silu", "second", "copied", "biased", "negated"))
    k.bias_stored = k.lasting_sem("bias_stored")

    with nc.Block() as block:
        @block.sync
        def _(sp):
            for kv in range(2):
                sp.dma_start(w2[:, kv, :, :], d["od_cmp_w2"][0, kv].rearrange("(h p) n -> p h n", p=P)).then_inc(small, 16)
                with nc.allow_non_contiguous_dma(reason="512 biases, one per partition"):
                    for ht in range(2):
                        sp.dma_start(b1[:, kv, ht:ht + 1], d["od_cmp_b1"][0, kv, ht * P:(ht + 1) * P]
                                     .rearrange("(p a) -> p a", a=1)).then_inc(small, 16)
            sp.dma_start(table[0:NBUCKET, :], d["rel_bias"]).then_inc(small, 16)
            sp.dma_start(hot[0:NBUCKET + 1, :], d["hot"]).then_inc(small, 16)
            load_weights(k, sp, "compress")
            sp.wait_ge(t_out, 4)
            sp.dma_start(k.bias_dram, tab[0:NH, :]).then_inc(k.bias_stored, 16)
            sp.wait_ge(k.bias_stored, 16)

        @block.tensor
        def _(pe):
            pe.wait_ge(small, 16 * 8)
            pe.wait_ge(masked, 1)
            for c in range(4):
                pe.matmul(k.ps[0:NH, 4 + c, :], table[0:NBUCKET + 1, :], hot[0:NBUCKET + 1, 512 * c:512 * c + 512],
                          start=True, stop=True).then_inc(t_done, 1)
            for kv in range(2):
                for half in range(2):
                    c = first + 2 * kv + half
                    wait_chunk(k, pe, c)
                    w = view(k, k.slot(c), 16, CMP_HID)
                    for ht in range(2):
                        for l in range(16):
                            src = k.kc2[:, kv, half, :, 16 * half + l:16 * half + l + 16 * (NCMP - 1) + 1:16]
                            mm = pe.matmul(k.ps[:, 2 * kv + ht, 0:NKV * NCMP], w[:, l, ht * P:(ht + 1) * P], src,
                                           start=half == 0 and l == 0, stop=half == 1 and l == 15)
                        if half == 1 and ht == 0:
                            mm.then_inc(hid_done, 1)
                    mm.then_inc(k.chunk_used, 1)
            pe.wait_ge(t_out, 4)
            pe.wait_ge(hid_out, 4)
            for ht in range(2):
                mm = pe.matmul(k.ps[:, 4, 0:NKV * NCMP], w2[:, 0, ht, :], hid[:, 0, ht, :], start=ht == 0, stop=ht == 1)
            mm.then_inc(k_done, 1)
            for g in range(NKV):
                for ht in range(2):
                    mm = pe.matmul(k.ps[0:NCMP, 5 + g, 0:DH], hid[:, 1, ht, g * NCMP:(g + 1) * NCMP], w2[:, 1, ht, :],
                                   start=ht == 0, stop=ht == 1)
                mm.then_inc(k_done, 1)

        @block.scalar
        def _(act):
            act.wait_ge(small, 16 * 8)
            for kv in range(2):
                for ht in range(2):
                    if ht == 0:
                        act.wait_ge(hid_done, kv + 1)
                    else:
                        act.wait_ge(k.chunk_used, first + 2 * kv + 2)
                    act.activation(hid[:, kv, ht, :], k.ps[:, 2 * kv + ht, 0:NKV * NCMP], ACT.Silu,
                                   bias=b1[:, kv, ht:ht + 1]).then_inc(hid_out, 1)

        @block.vector
        def _(dve):
            dve.memset(table[NBUCKET:NBUCKET + 1, :], -BIG).then_inc(masked, 1)
            for c in range(4):
                dve.wait_ge(t_done, c + 1)
                dve.tensor_scalar(tab[0:NH, 512 * c:512 * c + 512], k.ps[0:NH, 4 + c, :], -1.0, None,
                                  ALU.mult).then_inc(t_out, 1)
            k.link(dve, dve.tensor_scalar(k.gsig[:, 0, 0:NH], k.gsig[:, 0, 0:NH], view(k, Z0 + 15696, 1)[:, 0:1], None,
                                          ALU.mult))
            dve.wait_ge(k_done, 1)
            dve.tensor_copy(k.kcmpT, k.ps[:, 4, 0:NKV * NCMP].rearrange("p (g j) -> p g j", g=NKV)).then_inc(k_out, 1)
            for g in range(NKV):
                dve.wait_ge(k_done, g + 2)
                dve.tensor_copy(k.vcmp[0:NCMP, g, :], k.ps[0:NCMP, 5 + g, 0:DH]).then_inc(k_out, 1)



def nsa(k):
    nc = k.nc
    bias_n = view(k, U0, 2, 512)
    pc = view(k, U0 + 1024, NH, NT, NCMP)
    sc = [view(k, U0 + 2512 + 1024 * i, 2, 512) for i in range(2)]
    pT = [view(k, U0 + 4560 + 1152 * i, 1152) for i in range(2)]
    acc = view(k, U0 + 6864, 2, P)
    st = view(k, U0 + 7120, 2, 4, 2)
    c_low, c_sum, c_inv = (view(k, U0 + 7136 + 48 * i, NH, NT) for i in range(3))
    y = view(k, Y0, NT, D_IN)
    ma = MemAttention(k, "mem_o", 1, k.xqT, k.misc, k.misc + 1536)
    steps = [(h, t) for h in range(NH) for t in range(NT)]
    n = len(steps)
    bc, c_scored, c_biased, c_shifted, c_exped, c_ready = (
        k.sem("cmp_att_" + x) for x in ("bias_loaded", "scored", "biased", "shifted", "exped", "ready"))
    scored, low, exped, turned, cop_a, cop_v, mixed, stored = (
        k.sem("nsa_" + x) for x in ("scored", "low", "exped", "turned", "copied_act", "copied_dve", "mixed", "stored"))
    bias_loaded = [k.sem(f"nsa_bias{i}") for i in range(2)]

    with nc.Block() as block:
        @block.sync
        def _(sp):
            b = k.bias_dram
            for a in range(8):
                for t in range(NT):
                    src = bass.AP(b.tensor, 1024 + 33 - 8 * t - a, [[64, 16], [2048, NH], [1, NCMP]])
                    sp.dma_start(pc[16 * a:16 * a + 16, :, t, :], src).then_inc(bc, 16)
            for h in range(NH):
                if h >= 2:
                    sp.wait_ge(low, 2 * NT * (h - 1))
                src = bass.AP(b.tensor, 2048 * h + 512 - (P - 1), [[1, P], [1, 512]])
                sp.dma_start(bias_n[:, h % 2, :], src).then_inc(bias_loaded[h % 2], 16)
            load_weights(k, sp, "nsa")

        @block.tensor
        def _(pe):
            for h in range(NH):
                if h >= 8:
                    pe.wait_ge(c_biased, h - 7)
                for t in range(NT):
                    mm = pe.matmul(k.ps[:, h % 8, NCMP * t:NCMP * t + NCMP], k.qT[:, h, t * P:(t + 1) * P],
                                   k.kcmpT[:, h // HPG, :], start=True, stop=True)
                mm.then_inc(c_scored, 1)
            pe.wait_ge(c_biased, NH)
            for u in range(n + 2):
                if u < n:
                    h, t = steps[u]
                    g, m = h // HPG, (t + 1) * P
                    if u >= 2:
                        pe.wait_ge(low, 2 * (u - 1))
                    for i, kT in enumerate((k.ksT, k.kwT)):
                        pe.matmul(k.ps[:, 2 * (u % 2) + i, 0:m], k.qT[:, h, t * P:(t + 1) * P], kT[:, g, 0:m],
                                  start=True, stop=True).then_inc(scored, 1)
                if u >= 2:
                    v = u - 2
                    h, t = steps[v]
                    g = h // HPG
                    pe.wait_ge(cop_a, v + 1)
                    pe.wait_ge(cop_v, 2 * (v + 1))
                    o = k.ps[:, 6 + v % 2, :]
                    for i, vv in enumerate((k.vs, k.vw)):
                        for kt in range(t + 1):
                            pe.matmul(o[:, 128 * i:128 * i + 128], pT[v % 2][:, 512 * i + kt * P:512 * i + kt * P + P],
                                      vv[:, kt, g * DH:(g + 1) * DH], start=kt == 0, stop=kt == t)
                    pe.matmul(o[:, 256:384], pT[v % 2][0:NCMP, 1024:1152], k.vcmp[0:NCMP, g, :], start=True,
                              stop=True).then_inc(mixed, 1)
                if 1 <= u <= n:
                    v = u - 1
                    h, t = steps[v]
                    if v == 0:
                        pe.wait_ge(c_ready, 1)
                    if v >= 2:
                        pe.wait_ge(stored, v - 1)
                    pe.transpose(k.ps[0:NCMP, 6 + v % 2, 384:512], pc[:, h, t, :], k.ident).then_inc(turned, 1)
                    for i in range(2):
                        pe.wait_ge(exped, 2 * v + 1 + i)
                        if v:
                            pe.wait_ge(cop_v if i else cop_a, 2 * v if i else v)
                        for kt in range(t + 1):
                            tr = pe.transpose(k.ps[:, 4 + i, kt * P:(kt + 1) * P],
                                              sc[v % 2][:, i, kt * P:(kt + 1) * P], k.ident)
                        tr.then_inc(turned, 1)
            pe.wait_ge(stored, n)
            ma.tensor(pe)

        @block.scalar
        def _(act):
            act.wait_ge(c_shifted, 1)
            act.activation(pc, pc, ACT.Exp, scale=-1.0).then_inc(c_exped, 1)
            for u in range(n + 1):
                if u < n:
                    w = (steps[u][1] + 1) * P
                    for b in range(2):
                        act.wait_ge(low, 2 * u + b + 1)
                        if u >= 2 and b == 0:
                            act.wait_ge(stored, u - 1)
                        x = sc[u % 2][:, b, 0:w]
                        act.activation(x, x, ACT.Exp, scale=-1.0, bias=st[:, u % 2, 0, b:b + 1],
                                       accum_out=st[:, u % 2, 1, b:b + 1]).then_inc(exped, 1)
                if u:
                    v = u - 1
                    w = (steps[v][1] + 1) * P
                    act.wait_ge(turned, 3 * v + 2)
                    if v >= 2:
                        act.wait_ge(mixed, v - 1)
                    act.copy(pT[v % 2][:, 0:w], k.ps[:, 4, 0:w]).then_inc(cop_a, 1)
            ma.scalar(act)

        @block.vector
        def _(dve):
            dve.wait_ge(bc, 16 * 32)
            for h in range(NH):
                dve.wait_ge(c_scored, h + 1)
                dve.tensor_tensor(pc[:, h, :, :], pc[:, h, :, :],
                                  k.ps[:, h % 8, 0:NT * NCMP].rearrange("p (t j) -> p t j", t=NT),
                                  ALU.add).then_inc(c_biased, 1)
            dve.wait_ge(c_biased, NH)
            k.link(dve, dve.tensor_reduce(c_low, pc, AX_X, ALU.min))
            rows = pc.rearrange("p h t j -> p (h t) j")

            def by_row(x):
                return spread(x.rearrange("p h t -> p (h t)"), 2, NCMP)

            dve.tensor_tensor(rows, rows, by_row(c_low), ALU.subtract).then_inc(c_shifted, 1)
            dve.wait_ge(c_exped, 1)
            k.link(dve, dve.tensor_reduce(c_sum, pc, AX_X, ALU.add))
            k.link(dve, dve.reciprocal(c_inv, c_sum))
            k.link(dve, dve.tensor_tensor(c_low, c_inv, k.gsig[:, :, 0:NH].rearrange("p t h -> p h t"), ALU.mult))
            dve.tensor_tensor(rows, rows, by_row(c_low), ALU.mult).then_inc(c_ready, 1)
            for u in range(n + 2):
                if u < n:
                    h, t = steps[u]
                    if t == 0:
                        dve.wait_ge(bias_loaded[h % 2], 16 * (h // 2 + 1))
                    w = (t + 1) * P
                    for b in range(2):
                        dve.wait_ge(scored, 2 * u + b + 1)
                        if u >= 2:
                            dve.wait_ge(turned, 3 * (u - 2) + b + 2)
                        dve.tensor_tensor_reduce(sc[u % 2][:, b, 0:w], k.ps[:, 2 * (u % 2) + b, 0:w],
                                                 backwards(bias_n[:, h % 2, 0:w]), 1.0, 3e38, ALU.add, ALU.min,
                                                 st[:, u % 2, 0, b:b + 1]).then_inc(low, 1)
                if 1 <= u <= n:
                    v = u - 1
                    w = (steps[v][1] + 1) * P
                    if v >= 2:
                        dve.wait_ge(mixed, v - 1)
                    dve.wait_ge(turned, 3 * v + 1)
                    dve.tensor_copy(pT[v % 2][0:NCMP, 1024:1152], k.ps[0:NCMP, 6 + v % 2, 384:512]).then_inc(cop_v, 1)
                    dve.wait_ge(turned, 3 * v + 3)
                    dve.tensor_copy(pT[v % 2][:, 512:512 + w], k.ps[:, 5, 0:w]).then_inc(cop_v, 1)
                if u >= 2:
                    v = u - 2
                    h, t = steps[v]
                    s = st[:, v % 2, :, :]
                    k.link(dve, dve.reciprocal(s[:, 2, :], s[:, 1, :]))
                    k.link(dve, dve.tensor_tensor(s[:, 3, :], s[:, 2, :], k.gsig[:, t, NH + h:2 * NH + h + 1:NH],
                                                  ALU.mult))
                    dve.wait_ge(mixed, v + 1)
                    o = k.ps[:, 6 + v % 2, :]
                    ys = y[:, t, h * DH:(h + 1) * DH]
                    a = acc[:, v % 2, :]
                    k.link(dve, dve.tensor_scalar(a, o[:, 0:128], s[:, 3, 0:1], None, ALU.mult))
                    k.link(dve, dve.scalar_tensor_tensor(out=a, in0=o[:, 128:256], scalar=s[:, 3, 1:2], in1=a,
                                                         op0=ALU.mult, op1=ALU.add))
                    k.link(dve, dve.tensor_tensor(a, a, o[:, 256:384], ALU.add))
                    dve.tensor_tensor(ys, ys, a, ALU.mult).then_inc(stored, 1)
            ma.vector(dve)



def mix_in(k):
    nc, d = k.nc, k.d
    h = view(k, H0, NT, D)
    normed = view(k, Y0, NT, D)
    uT = view(k, U0, KD, S)
    squares = view(k, U0 + 4096, D)
    us = view(k, Z0, NT, 512)
    final_g = view(k, Z0 + 2048, D)
    k.ufT = view(k, Z0 + 15360, FG, S)
    y = view(k, Y0, NT, 2 * D)
    n1 = Norm(k, "norm_first_final", h, NT, scratch=squares, stat=0)
    n2 = Norm(k, "norm_mix", h, NT, uT, k.g_mix, squares, 16, dst=normed)
    first = first_chunk(k, "mix_in")
    pr = Projection(k, "mix", MIX_IN, first, NT, ("gate",), uT, S)
    g_loaded, scaled, x_stored, us_out, us_stored = (
        k.sem("mix_" + n) for n in ("gain_loaded", "x_ready", "x_stored", "us_ready", "us_stored"))

    with nc.Block() as block:
        @block.sync
        def _(sp):
            sp.dma_start(final_g, d["final_g"].rearrange("(a n) -> a n", a=1).to_broadcast([P, D])).then_inc(g_loaded, 16)
            load_weights(k, sp, "mix_in")
            sp.wait_ge(scaled, NT)
            sp.dma_start(k.h_dram[1].rearrange("(m p) n -> p m n", p=P), h).then_inc(x_stored, 16)
            sp.wait_ge(pr.emptied["dve"], NT)
            sp.dma_start(k.us_dram.rearrange("(m p) n -> p m n", p=P), us).then_inc(us_stored, 16)
            sp.wait_ge(x_stored, 16)
            sp.wait_ge(us_stored, 16)

        @block.tensor
        def _(pe):
            n2.tensor_turn(pe)
            pe.wait_ge(n2.ready, KD)
            pr.tensor(pe)

        @block.scalar
        def _(act):
            n1.scalar_sums(act)
            n1.scalar_root(act)
            act.wait_ge(scaled, NT)
            n2.scalar_sums(act)
            n2.scalar_root(act)
            n2.scalar_out(act)
            for g in pr.groups:
                if g.evac == "act":
                    pr.wait_group(act, g)
                    act.activation(y[:, g.t, g.col:g.col + g.width], k.ps[:, g.bank, :],
                                   ACT.Sigmoid).then_inc(pr.emptied["act"], 1)

        @block.vector
        def _(dve):
            n1.vector_mean(dve)
            n1.vector_scale(dve)
            dve.wait_ge(n1.normed, NT)
            dve.wait_ge(g_loaded, 16)
            for m in range(NT):
                dve.tensor_tensor(h[:, m, :], h[:, m, :], final_g, ALU.mult).then_inc(scaled, 1)
            dve.wait_ge(scaled, NT)
            n2.vector_mean(dve)
            n2.vector_scale(dve)
            for g in pr.groups:
                if g.evac == "dve":
                    pr.wait_group(dve, g)
                    dst = k.ufT if g.what == "uf" else us
                    dve.tensor_copy(dst[:, g.t, :], k.ps[:, g.bank, :]).then_inc(pr.emptied["dve"], 1)



TWO_PI_HI = 6.28125
TWO_PI_LO = 0.0019353071795864769
ROUND = 12582912.0


def ssm(k):
    nc, d = k.nc, k.d
    A = U0 + 11264
    V = view(k, U0, 2 * 2, GP, (L + 1) * SC)
    Bb = view(k, U0 + 9216, 2, 2 * GP, SC)
    u2 = view(k, H0, L, SG, SC)
    u2g = view(k, U0, SG, L, SC)
    tmpV = view(k, A, GP, L + 1, SC)
    CT = view(k, A + 2304, 2, 2 * GP, SC)
    Br = view(k, A + 3328, 2, 2 * GP, SC)
    Cn = view(k, A + 4352, 4, 4, 2, SN)
    X = view(k, A, 2, GP, P)
    tmpX = view(k, A + 4096, GP, L, SC)
    W1 = view(k, A + 4096, GP, 2, P)
    E = view(k, A, 2, GP, NCH)
    SH = view(k, A + 2048, 2, GP, NCH)
    tmpS = view(k, A + 4096, GP, NCH)
    R = view(k, A + 5120, GP, NCH)
    T = view(k, A, SG, P)
    KK = [view(k, A + 4096 + 1920 * i, 8, 15, SC) for i in range(2)]
    ysb = view(k, A + 4096, L, 512)
    Uc = view(k, U0 + 19456, SG, NCH)
    Hs = view(k, H0, 2 * 2, GP, NCH)
    PA = view(k, U0 + 21504, 2, 2 * GP, L + 1)
    PD = view(k, U0 + 22080, 2, 2 * GP, L + 1)
    pt = view(k, U0 + 22656, 7, 2 * GP)
    zz = view(k, U0 + 22880, 4, 2 * GP)
    tmp32 = view(k, U0 + 23008, 2 * GP)
    tmp128 = view(k, U0 + 23040, 2 * GP * 4)
    dT = view(k, U0 + 23168, SG)
    eye = view(k, C0, P)
    par = view(k, k.misc, 16, P)
    ldt = view(k, k.misc + 2048, 2)
    dD = view(k, k.misc + 2056, SG, SC)
    (raw, c_raw, u_raw, dt_ok, ang_ok, trig_ok, par_ok, par_T, cT, cT_out, u_T, u_out, x_ok, x_T, w_out, s_ok, h_ok,
     k_mm, kk_ok, t_ok, y_mm, y_a, y_v, y_st, u_by_g) = (
        k.sem("ssm_" + n) for n in
        ("params_loaded", "c_loaded", "u_loaded", "dt", "angles", "trig", "params", "params_turned", "c_turned",
         "c_copied", "u_turned", "u_copied", "x_ready", "x_turned", "w_copied", "s_done", "states", "k_done",
         "k_copied", "t_loaded", "y_done", "y_copied_act", "y_copied_dve", "y_stored", "u_by_group"))

    def y_bank(b):
        v = ysb[0:NCH].rearrange("p i (q a c) -> p i q a c", a=2, c=SC)
        return v[:, :, 4 * (b % 4):4 * (b % 4) + 4, b // 4, :]

    def cmul(dve, o_re, o_im, a_re, a_im, b_re, b_im, tmp, neg_im=False):
        dve.tensor_tensor(o_re, a_re, b_re, ALU.mult)
        k.link(dve, dve.tensor_tensor(tmp, a_im, b_im, ALU.mult))
        k.link(dve, dve.tensor_tensor(o_re, o_re, tmp, ALU.subtract))
        dve.tensor_tensor(o_im, a_re, b_im, ALU.mult)
        k.link(dve, dve.tensor_tensor(tmp, a_im, b_re, ALU.mult))
        if neg_im:
            k.link(dve, dve.scalar_tensor_tensor(out=o_im, in0=o_im, scalar=-1.0, in1=tmp, op0=ALU.mult,
                                                 op1=ALU.subtract))
        else:
            k.link(dve, dve.tensor_tensor(o_im, o_im, tmp, ALU.add))

    with nc.Block() as block:
        @block.gpsimd
        def _(pool):
            pool.wait_ge(u_raw, 16)
            for b in range(4):
                pool.tensor_copy(u2g[0:NCH, 8 * b:8 * b + 8, :, :],
                                 u2[0:NCH, :, 8 * b:8 * b + 8, :].rearrange("p j g c -> p g j c")).then_inc(u_by_g, 1)

        @block.sync
        def _(sp):
            q = 2 * GP
            sp.dma_start(par[0:q, 0, :], d["ssm_A_re_2"][0].rearrange("d (q a) n -> (d q) (a n)", a=2)).then_inc(raw, 16)
            sp.dma_start(par[0:q, 1, :], d["ssm_A_im_2"][0].rearrange("d (q a) n -> (d q) (a n)", a=2)).then_inc(raw, 16)
            sp.dma_start(ldt[0:q, :], d["ssm_log_dt_2"][0].rearrange("d (q a) -> (d q) a", a=2)).then_inc(raw, 16)
            sp.dma_start(view(k, H0, S * L)[0:NCH], k.us_dram.rearrange("(c j) n -> c (j n)", j=L)).then_inc(u_raw, 16)
            with nc.allow_non_contiguous_dma(reason="512 skips, channel by group"):
                sp.dma_start(dT[0:SC, :], d["ssm_D_2"][0].rearrange("(g c) -> c g", c=SC)).then_inc(c_raw, 16)
            for i, n in enumerate(("ssm_C_re_2", "ssm_C_im_2")):
                for dr in range(2):
                    for twice in range(2):
                        sp.dma_start(Cn[:, 2 * i + dr, :, twice, :],
                                     d[n][0, dr].rearrange("(t g) c n -> (g c) t n", t=4)).then_inc(c_raw, 16)
            for i, n in enumerate(("ssm_B_re_2", "ssm_B_im_2")):
                sp.dma_start(Br[:, i, :, :], d[n][0].rearrange("d (q a) n c -> (a n) (d q) c", a=2)).then_inc(c_raw, 16)
            load_weights(k, sp, "ssm")
            for b in range(4):
                sp.wait_ge(kk_ok, b + 1)
                for j in range(L):
                    sp.dma_start(T[SC * j:SC * (j + 1), 8 * b:8 * b + 8, :],
                                 KK[b % 2][0:SC, :, L - 1 - j:2 * L - 1 - j, :]
                                 .rearrange("p g s c -> p g (s c)")).then_inc(t_ok, 16)
            sp.wait_ge(y_a, 4)
            sp.wait_ge(y_v, 4)
            sp.dma_start(k.ys_dram.rearrange("(c j) n -> c j n", j=L), ysb[0:NCH]).then_inc(y_st, 16)
            sp.wait_ge(y_st, 16)

        @block.tensor
        def _(pe):
            for g in range(SG):
                if g % 8 == 0:
                    pe.wait_ge(u_by_g, g // 8 + 1)
                t = pe.transpose(k.ps[:, g // 8, NCH * (g % 8):NCH * (g % 8 + 1)],
                                 u2g[0:NCH, g, :, :].rearrange("p j c -> p (j c)"), k.ident[0:NCH, 0:NCH])
                if g % 8 == 7:
                    t.then_inc(u_T, 1)
            pe.wait_ge(c_raw, 16 * 11)
            for i in range(4):
                for t4 in range(4):
                    t = pe.transpose(k.ps[:, 4 + i, P * t4:P * (t4 + 1)],
                                     Cn[:, i, t4, :, :].rearrange("p a n -> p (a n)"), k.ident)
                t.then_inc(cT, 1)
            pe.wait_ge(par_ok, 1)
            pe.wait_ge(u_out, 4)
            for i in range(7):
                t = pe.transpose(k.ps[:, 0, 32 * i:32 * (i + 1)], par[0:2 * GP, i + 2, :], k.ident[0:32, 0:32])
            t.then_inc(par_T, 1)
            for dr in range(2):
                pe.wait_ge(x_ok, dr + 1)
                if dr == 0:
                    pe.wait_ge(cT_out, 4)
                for i in range(8):
                    if i >= 4 or dr:
                        pe.wait_ge(w_out, 8 * dr + i - 3)
                    for a in range(2):
                        for ri in range(2):
                            t = pe.transpose(k.ps[:, 4 + i % 4, P * (2 * a + ri):P * (2 * a + ri + 1)],
                                             X[:, ri, 2 * i + a, :], k.ident)
                    t.then_inc(x_T, 1)
                pe.wait_ge(w_out, 8 * (dr + 1))
                if dr:
                    pe.wait_ge(h_ok, 1)
                for ri in range(2):
                    for q in range(GP):
                        for a in range(2):
                            mm = pe.matmul(k.ps[SN * a:SN * (a + 1), 2 * ri + q // 8, NCH * (q % 8):NCH * (q % 8 + 1)],
                                           W1[:, q, ri, SN * a:SN * (a + 1)], Uc[:, 2 * q + a, :], start=True, stop=True)
                mm.then_inc(s_ok, 1)
            pe.wait_ge(h_ok, 2)
            for b in range(4):
                if b >= 2:
                    pe.wait_ge(kk_ok, b - 1)
                for dr in range(2):
                    for g8 in range(8):
                        g = 8 * b + g8
                        q, a = g // 2, g % 2
                        half = slice(SN * a, SN * (a + 1))
                        for ri in range(2):
                            mm = pe.matmul(k.ps[0:SC, 4 * (b % 2) + 2 * dr + a, P * (g8 // 2):P * (g8 // 2 + 1)],
                                           Bb[half, ri, GP * dr + q, :],
                                           V[half, 2 * dr + ri, q, SC * dr:SC * dr + P], start=ri == 0, stop=ri == 1)
                mm.then_inc(k_mm, 1)
            pe.wait_ge(t_ok, 16 * L * 4)
            pe.wait_ge(kk_ok, 4)
            for i in range(SG):
                a, q = i // GP, i % GP
                g = 2 * q + a
                half = slice(SN * a, SN * (a + 1))
                o = k.ps[0:NCH, i // 4, P * (i % 4):P * (i % 4 + 1)]
                pe.matmul(o, Uc[:, g, :], T[:, g, :], start=True, stop=False)
                for dr in range(2):
                    v0 = SC * (1 - dr)
                    for ri in range(2):
                        mm = pe.matmul(o, Hs[half, 2 * dr + ri, q, :], V[half, 2 * dr + ri, q, v0:v0 + P], start=False,
                                       stop=dr == 1 and ri == 1)
                if i % 4 == 3:
                    mm.then_inc(y_mm, 1)

        @block.scalar
        def _(act):
            act.wait_ge(raw, 48)
            act.activation(ldt[0:32, :], ldt[0:32, :], ACT.Exp).then_inc(dt_ok, 1)
            act.wait_ge(ang_ok, 1)
            act.activation(par[0:32, 8, :], par[0:32, 9, :], ACT.Exp).then_inc(trig_ok, 1)
            act.activation(par[0:32, 7, :], par[0:32, 10, :], ACT.Sin).then_inc(trig_ok, 1)
            act.activation(par[0:32, 12, :], par[0:32, 11, :], ACT.Sin).then_inc(trig_ok, 1)
            for b in range(4):
                act.wait_ge(u_T, b + 1)
                act.copy(Uc[:, 8 * b:8 * b + 8, :], k.ps[:, b, :].rearrange("p (g c) -> p g c", g=8)).then_inc(u_out, 1)
            for dr in range(2):
                for i in range(8):
                    act.wait_ge(x_T, 8 * dr + i + 1)
                    act.copy(W1[:, 2 * i:2 * i + 2, :, :], k.ps[:, 4 + i % 4, :]
                             .rearrange("p (a r n) -> p a r n", a=2, r=2)).then_inc(w_out, 1)
            for b in range(0, 8, 2):
                act.wait_ge(y_mm, b + 1)
                act.copy(y_bank(b),
                         k.ps[0:NCH, b, :].rearrange("p (g i c) -> p i g c", g=4, i=L)).then_inc(y_a, 1)

        @block.vector
        def _(dve):
            def ts(o, i, s1, s2, op0, op1=None):
                k.link(dve, dve.tensor_scalar(o, i, s1, s2, op0, op1) if op1 else dve.tensor_scalar(o, i, s1, None, op0))

            def tt(o, a, b, op):
                k.link(dve, dve.tensor_tensor(o, a, b, op))

            r = {n: par[0:32, i, :] for i, n in enumerate(
                ("A_re", "A_im", "a_re", "a_im", "c_re", "c_im", "cos", "sin", "mod", "x", "th", "half", "s2", "n",
                 "t", "inv"))}
            dve.wait_ge(raw, 48)
            dve.wait_ge(dt_ok, 1)
            dt = spread(ldt[0:32, :], 2, SN)
            for o, i in (("x", "A_re"), ("th", "A_im")):
                tt(r[o].rearrange("p (a n) -> p a n", a=2), r[i].rearrange("p (a n) -> p a n", a=2), dt, ALU.mult)
            ts(r["n"], r["th"], 1.0 / (TWO_PI_HI + TWO_PI_LO), ROUND, ALU.mult, ALU.add)
            ts(r["n"], r["n"], ROUND, None, ALU.subtract)
            for c in (TWO_PI_HI, TWO_PI_LO):
                k.link(dve, dve.scalar_tensor_tensor(out=r["th"], in0=r["n"], scalar=-c, in1=r["th"], op0=ALU.mult,
                                                     op1=ALU.add))
            ts(r["th"], r["th"], 3.1415925, -3.1415925, ALU.min, ALU.max)
            dve.tensor_scalar(r["half"], r["th"], 0.5, None, ALU.mult).then_inc(ang_ok, 1)
            dve.wait_ge(trig_ok, 3)
            tt(r["t"], r["s2"], r["s2"], ALU.mult)
            ts(r["cos"], r["t"], -2.0, 1.0, ALU.mult, ALU.add)
            tt(r["a_re"], r["mod"], r["cos"], ALU.mult)
            tt(r["a_im"], r["mod"], r["sin"], ALU.mult)
            tt(r["t"], r["A_re"], r["A_re"], ALU.mult)
            tt(r["inv"], r["A_im"], r["A_im"], ALU.mult)
            tt(r["inv"], r["inv"], r["t"], ALU.add)
            k.link(dve, dve.reciprocal(r["inv"], r["inv"]))
            ts(r["n"], r["a_re"], -1.0, None, ALU.add)
            tt(r["c_re"], r["n"], r["A_re"], ALU.mult)
            tt(r["t"], r["a_im"], r["A_im"], ALU.mult)
            tt(r["c_re"], r["c_re"], r["t"], ALU.add)
            tt(r["c_re"], r["c_re"], r["inv"], ALU.mult)
            tt(r["c_im"], r["a_im"], r["A_re"], ALU.mult)
            tt(r["t"], r["n"], r["A_im"], ALU.mult)
            tt(r["c_im"], r["c_im"], r["t"], ALU.subtract)
            dve.tensor_tensor(r["c_im"], r["c_im"], r["inv"], ALU.mult).then_inc(par_ok, 1)
            for i in range(4):
                dve.wait_ge(cT, i + 1)
                src = k.ps[:, 4 + i, :].rearrange("p (q a c) -> p q a c", a=2, c=SC)
                for a in range(2):
                    half = slice(SN * a, SN * (a + 1))
                    ins = dve.tensor_copy(CT[half, i // 2, GP * (i % 2):GP * (i % 2 + 1), :], src[half, :, a, :])
                ins.then_inc(cT_out, 1)
            dve.wait_ge(par_T, 1)
            k.link(dve, dve.tensor_copy(pt, k.ps[:, 0, 0:224].rearrange("p (i q) -> p i q", i=7)))
            dve.memset(PA[:, 0, :, 0:1], 1.0)
            dve.memset(PA[:, 1, :, 0:1], 0.0)
            k.link(dve, dve.tensor_copy(PA[:, :, :, 1], pt[:, 0:2, :]))
            for lo, n in ((1, 1), (2, 2), (4, 4)):
                def by(ri):
                    return spread(PA[:, ri, :, lo], 2, n)
                cmul(dve, PA[:, 0, :, lo + 1:lo + 1 + n], PA[:, 1, :, lo + 1:lo + 1 + n], PA[:, 0, :, 1:1 + n],
                     PA[:, 1, :, 1:1 + n], by(0), by(1), tmp128.rearrange("p (q n) -> p q n", n=4)[:, :, 0:n])
            for ri in range(2):
                ins = dve.tensor_copy(PD[:, ri, :, :], backwards(PA[:, ri, :, :]))
            k.link(dve, ins)
            src = (pt[:, 4, :], pt[:, 5, :])
            for i in range(3):
                dst = (zz[:, 2 * (i % 2), :], zz[:, 2 * (i % 2) + 1, :])
                cmul(dve, *dst, *src, *src, tmp32)
                src = dst
            z_re, z_im = src
            for i in range(3):
                tt(pt[:, 6, :], pt[:, 6, :], pt[:, 6, :], ALU.mult)
            dve.wait_ge(c_raw, 16 * 11)
            dve.wait_ge(cT_out, 4)
            cmul(dve, Bb[:, 0, :, :], Bb[:, 1, :, :], Br[:, 0, :, :], Br[:, 1, :, :], spread(pt[:, 2, :], 2, SC),
                 spread(pt[:, 3, :], 2, SC), tmpV.rearrange("p q s c -> p (q s c)")[:, 0:512]
                 .rearrange("p (q c) -> p q c", c=SC))
            for dr in range(2):
                pw, q = (PA, PD)[dr], slice(GP * dr, GP * (dr + 1))
                cmul(dve, *(V[:, 2 * dr + ri, :, :].rearrange("p q (s c) -> p q s c", c=SC) for ri in range(2)),
                     *(spread(pw[:, ri, q, :], 3, SC) for ri in range(2)),
                     *(spread(CT[:, ri, q, :], 2, L + 1) for ri in range(2)), tmpV, neg_im=True)
            for dr in range(2):
                q = slice(GP * dr, GP * (dr + 1))
                pw = PA[:, :, q, 0:L] if dr else PD[:, :, q, 1:L + 1]
                cmul(dve, *(X[:, ri, :, :].rearrange("p q (s c) -> p q s c", c=SC) for ri in range(2)),
                     *(spread(pw[:, ri, :, :], 3, SC) for ri in range(2)),
                     *(spread(Bb[:, ri, q, :], 2, L) for ri in range(2)), tmpX)
                dve.sem_inc(x_ok, 1)
                dve.wait_ge(x_T, 8 * (dr + 1))
                k.link(dve, dve.tensor_copy(E[:, 0, :, 0], z_re[:, q]))
                k.link(dve, dve.tensor_copy(E[:, 1, :, 0], z_im[:, q]))
                dve.wait_ge(s_ok, dr + 1)
                n = 1
                while n < NCH:
                    cmul(dve, E[:, 0, :, n:2 * n], E[:, 1, :, n:2 * n], E[:, 0, :, 0:n], E[:, 1, :, 0:n],
                         spread(E[:, 0, :, n - 1], 2, n), spread(E[:, 1, :, n - 1], 2, n), tmpS[:, :, 0:n])
                    n *= 2
                k.link(dve, dve.tensor_copy(R, spread(pt[:, 6, q], 2, NCH)))
                k.link(dve, dve.memset(R[:, :, 0:1], 0.0))
                s_re, s_im = (k.ps[:, 2 * ri:2 * ri + 2, :].rearrange("p b (q c) -> p (b q) c", c=NCH) for ri in range(2))
                if dr:
                    s_re, s_im = backwards(s_re), backwards(s_im)
                tt(SH[:, 0, :, :], s_re, E[:, 0, :, :], ALU.mult)
                tt(tmpS, s_im, E[:, 1, :, :], ALU.mult)
                tt(SH[:, 0, :, :], SH[:, 0, :, :], tmpS, ALU.add)
                tt(SH[:, 1, :, :], s_im, E[:, 0, :, :], ALU.mult)
                tt(tmpS, s_re, E[:, 1, :, :], ALU.mult)
                tt(SH[:, 1, :, :], SH[:, 1, :, :], tmpS, ALU.subtract)
                for ri in range(2):
                    flat = SH[:, ri, :, :].rearrange("p q c -> p (q c)")
                    k.link(dve, dve.tensor_tensor_scan(flat, R.rearrange("p q c -> p (q c)"), flat, 0.0, ALU.mult,
                                                       ALU.add))
                hs = [Hs[:, 2 * dr + ri, :, :] for ri in range(2)]
                m = NCH - 1
                dst = [backwards(x[:, :, 0:m]) if dr else x[:, :, 1:NCH] for x in hs]
                cmul(dve, *dst, SH[:, 0, :, 0:m], SH[:, 1, :, 0:m], E[:, 0, :, 0:m], E[:, 1, :, 0:m], tmpS[:, :, 0:m])
                z = slice(NCH - 1, NCH) if dr else slice(0, 1)
                dve.memset(hs[0][:, :, z], 0.0)
                dve.memset(hs[1][:, :, z], 0.0).then_inc(h_ok, 1)
            tt(dD[0:SC], spread(dT[0:SC, :], 2, SC), spread(eye[0:SC, 0:SC], 1, SG), ALU.mult)
            for b in range(4):
                dve.wait_ge(k_mm, b + 1)
                if b >= 2:
                    dve.wait_ge(t_ok, 16 * L * b)
                f, g = (k.ps[0:SC, 4 * (b % 2) + 2 * dr:4 * (b % 2) + 2 * dr + 2, :]
                        .rearrange("p a (q s) -> p a q s", q=4) for dr in range(2))
                kk = KK[b % 2][0:SC]
                by_a = kk.rearrange("p (q a) s c -> p a q (s c)", a=2)
                k.link(dve, dve.tensor_copy(by_a[:, :, :, SC * (L - 1):], f))
                k.link(dve, dve.tensor_copy(by_a[:, :, :, 0:SC * (L - 1)], g[:, :, :, 0:SC * (L - 1)]))
                lag0 = by_a[:, :, :, SC * (L - 1):SC * L]
                tt(lag0, lag0, g[:, :, :, SC * (L - 1):], ALU.add)
                dve.tensor_tensor(kk[:, :, L - 1, :], kk[:, :, L - 1, :], dD[0:SC, 8 * b:8 * b + 8, :],
                                  ALU.add).then_inc(kk_ok, 1)
            for b in range(1, 8, 2):
                dve.wait_ge(y_mm, b + 1)
                dve.tensor_copy(y_bank(b),
                                k.ps[0:NCH, b, :].rearrange("p (g i c) -> p i g c", g=4, i=L)).then_inc(y_v, 1)



def mix_mid(k):
    nc, d = k.nc, k.d
    ys, gyT = view(k, H0, NT, 512), view(k, H0 + 2048, 4, S)
    sgT = view(k, U0, 4, S)
    cosS, sinS, dft = view(k, Z0, NT, S), view(k, Z0 + 2048, NT, S), view(k, Z0 + 4096, 2 * P)
    FA = view(k, Z0 + 4352, NT, 2, FG, P)
    FT = view(k, Z0 + 8448, FG, S)
    tmp = view(k, Z0 + 10496, 2, S)
    k.merged = view(k, Z0 + 12544 - 1024, NT, D)
    sig = view(k, U0 + 2048, 4, S)
    y = view(k, Y0, NT, 2 * D)
    first = first_chunk(k, "mix_mid")
    (tabs, ys_in, fa_mm, fa_a, fa_v, ys_T, gy_ok, ft_mm, ft_ok, glu_mm, sig_ok, sg_ok, p_mm, p_ok) = (
        k.sem("mid_" + n) for n in ("tables", "ys_loaded", "channel_dft", "channel_act", "channel_dve", "ys_turned",
                                    "gelu", "token_dft", "token_copied", "glu_done", "sigmoid", "gated", "proj_done",
                                    "merged"))

    with nc.Block() as block:
        @block.sync
        def _(sp):
            sp.dma_start(dft, d["dft"]).then_inc(tabs, 16)
            sp.dma_start(ys, k.ys_dram.rearrange("(m p) n -> p m n", p=P)).then_inc(ys_in, 16)
            sp.dma_start(view(k, Z0, 2048), d["cosS"]).then_inc(tabs, 16)
            sp.dma_start(view(k, Z0 + 2048, 2048), d["sinS"]).then_inc(tabs, 16)
            load_weights(k, sp, "mix_mid")

        @block.tensor
        def _(pe):
            pe.wait_ge(tabs, 48)
            for m in range(NT):
                for g in range(FG):
                    mm = pe.matmul(k.ps[:, 2 * m + g // 2, 256 * (g % 2):256 * (g % 2) + 256],
                                   k.ufT[:, g, m * P:(m + 1) * P], dft, start=True, stop=True)
                    if g % 2:
                        mm.then_inc(fa_mm, 1)
            pe.wait_ge(ys_in, 16)
            for c in range(4):
                if c < 2:
                    pe.wait_ge(fa_a, c + 1)
                    pe.wait_ge(fa_v, c + 1)
                for m in range(NT):
                    t = pe.transpose(k.ps[:, c, m * P:(m + 1) * P], ys[:, m, c * P:(c + 1) * P], k.ident)
                t.then_inc(ys_T, 1)
            pe.wait_ge(fa_a, NT)
            pe.wait_ge(fa_v, NT)
            for g in range(FG):
                for m in range(NT):
                    for ri in range(2):
                        mm = pe.matmul(k.ps[:, 4 + g, :], FA[:, m, ri, g, :], (cosS, sinS)[ri][:, m, :],
                                       start=m == 0 and ri == 0, stop=m == NT - 1 and ri == 1)
                mm.then_inc(ft_mm, 1)
            pe.wait_ge(gy_ok, 4)
            wait_chunk(k, pe, first)
            w = view(k, k.slot(first), 4, 512)
            for c in range(4):
                for kk in range(4):
                    mm = pe.matmul(k.ps[:, c, :], w[:, kk, c * P:(c + 1) * P], gyT[:, kk, :], start=kk == 0,
                                   stop=kk == 3)
                mm.then_inc(glu_mm if c < 3 else k.chunk_used, 1)
            pe.wait_ge(ft_ok, FG)
            for i, xT in enumerate((sgT, FT)):
                wait_chunk(k, pe, first + 1 + i)
                w = view(k, k.slot(first + 1 + i), 4, D)
                for m in range(NT):
                    for n in range(2):
                        b = 2 * m + n
                        if i:
                            pe.wait_ge(p_ok, b + 1)
                        elif b == 0:
                            pe.wait_ge(sg_ok, 4)
                        for kk in range(4):
                            mm = pe.matmul(k.ps[:, b, :], xT[:, kk, m * P:(m + 1) * P], w[:, kk, 512 * n:512 * n + 512],
                                           start=kk == 0, stop=kk == 3)
                        mm.then_inc(p_mm if b < 7 else k.chunk_used, 1)

        @block.scalar
        def _(act):
            for m in range(NT):
                act.wait_ge(fa_mm, 2 * m + 1)
                act.copy(FA[:, m, :, 0:2, :], k.ps[:, 2 * m, :].rearrange("p (g r c) -> p r g c", g=2, r=2)).then_inc(fa_a, 1)
            for c in range(4):
                act.wait_ge(ys_T, c + 1)
                act.activation(gyT[:, c, :], k.ps[:, c, :], ACT.Gelu_apprx_tanh).then_inc(gy_ok, 1)
            for c in range(4):
                if c < 3:
                    act.wait_ge(glu_mm, c + 1)
                else:
                    act.wait_ge(k.chunk_used, first + 1)
                act.activation(sig[:, c, :], k.ps[:, c, :], ACT.Sigmoid).then_inc(sig_ok, 1)

        @block.vector
        def _(dve):
            for m in range(NT):
                dve.wait_ge(fa_mm, 2 * m + 2)
                dve.tensor_copy(FA[:, m, :, 2:4, :], k.ps[:, 2 * m + 1, :]
                                .rearrange("p (g r c) -> p r g c", g=2, r=2)).then_inc(fa_v, 1)
            for g in range(FG):
                dve.wait_ge(ft_mm, g + 1)
                dve.tensor_copy(FT[:, g, :], k.ps[:, 4 + g, :]).then_inc(ft_ok, 1)
            for c in range(4):
                dve.wait_ge(sig_ok, c + 1)
                dve.tensor_tensor(sgT[:, c, :], sig[:, c, :], gyT[:, c, :], ALU.mult).then_inc(sg_ok, 1)
            for i in range(2):
                for b in range(8):
                    m, n = b // 2, b % 2
                    if b < 7:
                        dve.wait_ge(p_mm, 7 * i + b + 1)
                    else:
                        dve.wait_ge(k.chunk_used, first + 2 + i)
                    dst = k.merged[:, m, 512 * n:512 * n + 512]
                    gate = y[:, m, D * (1 - i) + 512 * n:D * (1 - i) + 512 * n + 512]
                    if i == 0:
                        dve.tensor_tensor(dst, k.ps[:, b, :], gate, ALU.mult).then_inc(p_ok, 1)
                    else:
                        if b < 2:
                            dve.wait_ge(p_ok, 8)
                        k.link(dve, dve.tensor_tensor(tmp[:, b % 2, :], k.ps[:, b, :], gate, ALU.mult))
                        k.link(dve, dve.tensor_tensor(dst, dst, tmp[:, b % 2, :], ALU.add))



def expert_slot(k, e, i):
    return RING + i * SLOT if e % 2 == 0 else U0 + i * SLOT


def expert_source(k, e, i):
    w = (k.d["expert_w_gate_2"], k.d["expert_w_up_2"], k.d["expert_w_down_2"])[i]
    return w[0, e].rearrange("(k p) n -> p k n", p=P)


def expert_view(k, e, i):
    return view(k, expert_slot(k, e, i), *((KD, DE) if i < 2 else (KE, D)))


def mix_out(k):
    nc, d = k.nc, k.d
    h = view(k, H0, NT, D)
    k.hn = view(k, Y0, NT, D)
    hnT = view(k, Y0 + 4096, KD, S)
    mT = view(k, Z0 + 4096, KD, S)
    gain = view(k, Z0 + 8192, D)
    squares = view(k, Z0 + 9216, D)
    wr = view(k, Z0 + 10240, KD, EG + NE)
    br = view(k, Z0 + 10816, EG + NE)
    lg = view(k, Z0 + 10896, NT, EG + NE)
    R0 = Z0 + 11520 - 336
    oh_g = view(k, R0, NT, EG)
    cand = view(k, R0 + 32, NT, EG)
    eg = view(k, R0 + 64, NT, EG)
    es = view(k, R0 + 96, NT, EPG)
    oh_e = view(k, R0 + 128, 2, NT, EPG)
    pick = view(k, R0 + 192, NT, EG, EPG)
    OH = [view(k, R0 + 448 + 256 * i, NT, NE) for i in range(2)]
    M = view(k, R0 + 960, NT, NE)
    rank = view(k, R0 + 1216, NT, NE)
    prod = view(k, R0 + 1472, NT, NE)
    cnt = view(k, R0 + 1728, NE)
    before = view(k, R0 + 1792, P)
    ones = view(k, R0 + 1920, P)
    sm = view(k, R0 + 2048, 16, NT)
    blk = view(k, R0 + 2112, NT, 2)
    zero64 = view(k, R0 + 2120, NE)
    tmp64 = view(k, R0 + 2184, NE)
    K0 = Z0 + 16640
    k.rk = view(k, K0, NT, NE)
    k.gate_w = view(k, K0 + 256, 2, NT)
    k.dest = view(k, K0 + 264, 2, NT)
    k.flag = view(k, K0 + 272, 1)
    k.starts = view(k, K0 + 280, NE)
    k.nb = view(k, K0 + 344, NE)
    k.iota = view(k, K0 + 408, NE)
    n1 = Norm(k, "norm_ffn", h, NT, scratch=squares, stat=0, dst=k.hn)
    first = first_chunk(k, "mix_out")
    k.e_loaded = [[k.lasting_sem(f"expert_{a}_{w}") for w in ("gate", "up", "down")] for a in ("even", "odd")]
    (small, h_in, m_T, m_a, m_v, bank, added, gained, x_st, hn_T, hn_out, lg_mm, ge_ok, ge_out, ex_in, ex_out, m_ok, r_mm,
     done) = (k.sem("out_" + n) for n in
              ("small", "h_loaded", "turned", "copied_act", "copied_dve", "bank_done", "added", "gained", "x_stored",
               "hn_turned", "hn_copied", "logits", "group_shifted", "group_exp", "pair_in", "pair_exp", "chosen",
               "ranked", "routed"))

    with nc.Block() as block:
        @block.sync
        def _(sp):
            sp.dma_start(h, k.h_dram[1].rearrange("(m p) n -> p m n", p=P)).then_inc(h_in, 16)
            sp.dma_start(gain, d["ffn_norm_g_2"].to_broadcast([P, D])).then_inc(small, 16)
            sp.dma_start(wr[:, :, 0:EG], d["router_group_w_2"][0].rearrange("(k p) n -> p k n", p=P)).then_inc(small, 16)
            sp.dma_start(wr[:, :, EG:], d["router_expert_w_2"][0].rearrange("(k p) n -> p k n", p=P)).then_inc(small, 16)
            sp.dma_start(br[:, 0:EG], d["router_group_b_2"].to_broadcast([P, EG])).then_inc(small, 16)
            sp.dma_start(br[:, EG:], d["router_expert_b_2"].to_broadcast([P, NE])).then_inc(small, 16)
            sp.dma_start(k.iota, d["iota"]).then_inc(small, 16)
            load_weights(k, sp, "mix_out")
            sp.wait_ge(m_T, KD)
            sp.dma_start(before, d["before"]).then_inc(small, 16)
            for i in range(3):
                sp.dma_start(expert_view(k, 1, i), expert_source(k, 1, i)).then_inc(k.e_loaded[1][i], 16)
            sp.wait_ge(k.chunk_used, len(k.chunks))
            for i in range(3):
                sp.dma_start(expert_view(k, 0, i), expert_source(k, 0, i)).then_inc(k.e_loaded[0][i], 16)

        @block.gpsimd
        def _(pool):
            pool.wait_ge(m_T, KD)
            pool.memset(ones, 1.0).then_inc(done, 1)

        @block.tensor
        def _(pe):
            for kk in range(KD):
                for m in range(NT):
                    t = pe.transpose(k.ps[:, kk, m * P:(m + 1) * P], k.merged[:, m, kk * P:(kk + 1) * P], k.ident)
                t.then_inc(m_T, 1)
            pe.wait_ge(m_a, KD // 2)
            pe.wait_ge(m_v, KD // 2)
            for n in range(2):
                wait_chunk(k, pe, first + n)
                w = view(k, k.slot(first + n), KD, 512)
                for m in range(NT):
                    for kk in range(KD):
                        mm = pe.matmul(k.ps[:, 4 * n + m, :], mT[:, kk, m * P:(m + 1) * P], w[:, kk, :], start=kk == 0,
                                       stop=kk == KD - 1)
                    mm.then_inc(bank if m < NT - 1 else k.chunk_used, 1)
            pe.wait_ge(gained, NT)
            for kk in range(KD):
                for m in range(NT):
                    t = pe.transpose(k.ps[:, kk, m * P:(m + 1) * P], k.hn[:, m, kk * P:(kk + 1) * P], k.ident)
                t.then_inc(hn_T, 1)
            pe.wait_ge(hn_out, KD)
            pe.wait_ge(small, 16 * 7)
            for m in range(NT):
                for kk in range(KD):
                    mm = pe.matmul(k.ps[:, m, 0:EG + NE], hnT[:, kk, m * P:(m + 1) * P], wr[:, kk, :], start=kk == 0,
                                   stop=kk == KD - 1)
                mm.then_inc(lg_mm, 1)
            pe.wait_ge(m_ok, 1)
            pe.wait_ge(done, 1)
            for m in range(NT):
                for b in range(m):
                    pe.matmul(k.ps[:, 4, NE * m:NE * (m + 1)], ones, M[:, b, :], start=b == 0, stop=False)
                pe.matmul(k.ps[:, 4, NE * m:NE * (m + 1)], before, M[:, m, :], start=m == 0, stop=True)
            for m in range(NT):
                mm = pe.matmul(k.ps[:, 5, 0:NE], ones, M[:, m, :], start=m == 0, stop=m == NT - 1)
            mm.then_inc(r_mm, 1)

        @block.scalar
        def _(act):
            for kk in range(0, KD, 2):
                act.wait_ge(m_T, kk + 1)
                act.copy(mT[:, kk, :], k.ps[:, kk, :]).then_inc(m_a, 1)
            act.wait_ge(added, 2 * NT)
            n1.scalar_sums(act)
            n1.scalar_root(act)
            for kk in range(KD):
                act.wait_ge(hn_T, kk + 1)
                act.copy(hnT[:, kk, :], k.ps[:, kk, :]).then_inc(hn_out, 1)
            act.wait_ge(ge_ok, 1)
            act.activation(eg, eg, ACT.Exp).then_inc(ge_out, 1)
            act.wait_ge(ex_in, 1)
            act.activation(sm[:, 3, :], sm[:, 3, :], ACT.Exp).then_inc(ex_out, 1)

        @block.vector
        def _(dve):
            def tt(o, a, b, op):
                k.link(dve, dve.tensor_tensor(o, a, b, op))

            def ts(o, i, s1, s2, op0, op1=None):
                k.link(dve, dve.tensor_scalar(o, i, s1, s2, op0, op1) if op1 else dve.tensor_scalar(o, i, s1, None, op0))

            for kk in range(1, KD, 2):
                dve.wait_ge(m_T, kk + 1)
                dve.tensor_copy(mT[:, kk, :], k.ps[:, kk, :]).then_inc(m_v, 1)
            dve.wait_ge(h_in, 16)
            for n in range(2):
                for m in range(NT):
                    if m < NT - 1:
                        dve.wait_ge(bank, (NT - 1) * n + m + 1)
                    else:
                        dve.wait_ge(k.chunk_used, first + n + 1)
                    hs = h[:, m, n * 512:(n + 1) * 512]
                    dve.tensor_tensor(hs, hs, k.ps[:, 4 * n + m, :], ALU.add).then_inc(added, 1)
            n1.vector_mean(dve)
            n1.vector_scale(dve)
            dve.wait_ge(n1.normed, NT)
            dve.wait_ge(small, 16 * 7)
            for m in range(NT):
                dve.tensor_tensor(k.hn[:, m, :], k.hn[:, m, :], gain, ALU.mult).then_inc(gained, 1)
            dve.wait_ge(lg_mm, NT)
            for m in range(NT):
                ins = dve.tensor_tensor(lg[:, m, :], k.ps[:, m, 0:EG + NE], br, ALU.add)
            k.link(dve, ins)
            iota8 = spread(k.iota[:, 0:8], 1, NT)

            def first_max(x, top, hot, w):
                k.link(dve, dve.tensor_reduce(top, x, AX_X, ALU.max))
                tt(w, x, spread(top, 2, 8), ALU.is_equal)
                k.link(dve, dve.scalar_tensor_tensor(out=w, in0=w, scalar=-64.0, in1=iota8, op0=ALU.mult, op1=ALU.add))
                k.link(dve, dve.tensor_reduce(sm[:, 15, :], w, AX_X, ALU.min))
                tt(hot, w, spread(sm[:, 15, :], 2, 8), ALU.is_equal)

            gl = lg[:, :, 0:EG]
            first_max(gl, sm[:, 0, :], oh_g, cand)
            dve.tensor_tensor(eg, gl, spread(sm[:, 0, :], 2, EG), ALU.subtract).then_inc(ge_ok, 1)
            tt(pick, lg[:, :, EG:].rearrange("p t (g e) -> p t g e", g=EG), spread(oh_g, 3, EPG), ALU.mult)
            k.link(dve, dve.tensor_reduce(es, pick.rearrange("p t g e -> p t e g"), AX_X, ALU.add))
            first_max(es, sm[:, 1, :], oh_e[:, 0, :, :], cand)
            k.link(dve, dve.scalar_tensor_tensor(out=es, in0=oh_e[:, 0, :, :], scalar=-BIG, in1=es, op0=ALU.mult,
                                                 op1=ALU.add))
            first_max(es, sm[:, 2, :], oh_e[:, 1, :, :], cand)
            dve.tensor_tensor(sm[:, 3, :], sm[:, 2, :], sm[:, 1, :], ALU.subtract).then_inc(ex_in, 1)
            for c in range(2):
                tt(OH[c].rearrange("p t (g e) -> p t g e", g=EG), spread(oh_g, 3, EPG), spread(oh_e[:, c, :, :], 2, EG),
                   ALU.mult)
            dve.tensor_tensor(M, OH[0], OH[1], ALU.add).then_inc(m_ok, 1)
            dve.wait_ge(ge_out, 1)
            k.link(dve, dve.tensor_reduce(sm[:, 4, :], eg, AX_X, ALU.add))
            dve.wait_ge(ex_out, 1)
            ts(sm[:, 5, :], sm[:, 3, :], 1.0, None, ALU.add)
            tt(sm[:, 5, :], sm[:, 5, :], sm[:, 4, :], ALU.mult)
            k.link(dve, dve.reciprocal(k.gate_w[:, 0, :], sm[:, 5, :]))
            tt(k.gate_w[:, 1, :], k.gate_w[:, 0, :], sm[:, 3, :], ALU.mult)
            dve.wait_ge(r_mm, 1)
            k.link(dve, dve.tensor_copy(rank, k.ps[:, 4, 0:NT * NE].rearrange("p (t e) -> p t e", t=NT)))
            k.link(dve, dve.tensor_copy(cnt, k.ps[:, 5, 0:NE]))
            k.link(dve, dve.scalar_tensor_tensor(out=k.rk, in0=rank, scalar=1.0, in1=M, op0=ALU.add, op1=ALU.mult))
            ts(k.rk, k.rk, -1.0, None, ALU.add)
            k.link(dve, dve.memset(zero64, 0.0))
            ts(k.nb, cnt, float(SLOTS), None, ALU.is_gt)
            for i in range(2, 8):
                k.link(dve, dve.scalar_tensor_tensor(out=k.nb, in0=cnt, scalar=float(SLOTS * i), in1=k.nb,
                                                     op0=ALU.is_gt, op1=ALU.add))
            k.link(dve, dve.tensor_tensor_scan(tmp64, k.nb, zero64, 0.0, ALU.add, ALU.add))
            tt(k.starts, tmp64, k.nb, ALU.subtract)
            k.link(dve, dve.tensor_copy(k.flag.bitcast(I32), tmp64[:, NE - 1:NE]))
            for c in range(2):
                r, e, st, b, z = (sm[:, 6 + i, :] for i in range(5))
                for o, tab in ((r, rank), (e, spread(k.iota, 1, NT)), (st, spread(k.starts, 1, NT))):
                    tt(prod, OH[c], tab, ALU.mult)
                    k.link(dve, dve.tensor_reduce(o, prod, AX_X, ALU.add))
                ts(b, r, float(SLOTS), None, ALU.is_ge)
                for i in range(2, 8):
                    k.link(dve, dve.scalar_tensor_tensor(out=b, in0=r, scalar=float(SLOTS * i), in1=b, op0=ALU.is_ge,
                                                         op1=ALU.add))
                ts(z, b, 0.0, None, ALU.is_equal)
                tt(st, st, b, ALU.add)
                ts(st, st, float(NE - 1), None, ALU.add)
                tt(e, e, st, ALU.subtract)
                tt(e, e, z, ALU.mult)
                tt(e, e, st, ALU.add)
                tt(e, e, b, ALU.subtract)
                k.link(dve, dve.scalar_tensor_tensor(out=e, in0=e, scalar=float(SLOTS), in1=r, op0=ALU.mult,
                                                     op1=ALU.add))
                k.link(dve, dve.tensor_copy(k.dest[:, c, :].bitcast(U32), e))



def since(eng, sem, v):
    if not isinstance(v, int) or v > 0:
        eng.wait_ge(sem, v)


def moe(k):
    nc, ps = k.nc, k.ps
    t = Z0 + 4096
    pick = view(k, t, 2, NT, SLOTS)
    xT = view(k, t + 512, 2, KD, SLOTS)
    sg = view(k, t + 1536, 2, KE * SLOTS)
    aT = view(k, t + 2048, 2, KE * SLOTS)
    yT = view(k, t + 2560, 2, KD * SLOTS)
    yn = view(k, t + 3584, 2, D)
    picked, x_done, x_ready, gu_done, silu_done, a_ready, y_done, y_ready, turned, rows_ready = (
        k.sem("moe_" + n) for n in ("picked", "x_done", "x_ready", "hidden_done", "silu_done", "a_ready", "y_done",
                                    "y_ready", "turned", "rows_ready"))
    stored = [k.sem(f"moe_stored{i}") for i in range(2)]
    half = NE // 2

    def pairs(eng, step, first=1, last=half):
        with eng.Fori(first, last) as r:
            for a in range(2):
                step(2 * r + a, a, r)

    with nc.Block() as block:
        @block.sync
        def _(sp):
            def load(e, a, r):
                for i in range(3):
                    w = (k.d["expert_w_gate_2"], k.d["expert_w_up_2"], k.d["expert_w_down_2"])[i][0]
                    sp.wait_ge(y_done if i == 2 else gu_done, e - 1)
                    src = w[bass.ds(e, 1)].rearrange("e (k p) n -> p (e k) n", p=P)
                    sp.dma_start(expert_view(k, a, i), src).then_inc(k.e_loaded[a][i], 16)

            pairs(sp, load)

        @block.tensor
        def _(pe):
            def gather(e, a):
                pe.wait_ge(picked, e + 1)
                since(pe, x_ready, e - 1)
                for kk in range(KD):
                    for m in range(NT):
                        mm = pe.matmul(ps[:, a, SLOTS * kk:SLOTS * (kk + 1)], k.hn[:, m, kk * P:(kk + 1) * P],
                                       pick[:, a, m, :], start=m == 0, stop=m == NT - 1)
                mm.then_inc(x_done, 1)

            def hidden(e, a, r):
                pe.wait_ge(x_ready, e + 1)
                since(pe, a_ready, e - 1)
                for i in range(2):
                    pe.wait_ge(k.e_loaded[a][i], 16 * r + 16)
                    w = expert_view(k, a, i)
                    for f in range(KE):
                        o = KE * SLOTS * i + SLOTS * f
                        for kk in range(KD):
                            mm = pe.matmul(ps[:, 2 + a, o:o + SLOTS], w[:, kk, f * P:(f + 1) * P], xT[:, a, kk, :],
                                           start=kk == 0, stop=kk == KD - 1)
                mm.then_inc(gu_done, 1)

            def turn(e, a):
                for kk in range(KD):
                    tr = pe.transpose(ps[0:SLOTS, 5 + kk // 4, P * (kk % 4):P * (kk % 4 + 1)],
                                      yT[:, a, SLOTS * kk:SLOTS * (kk + 1)], k.ident)
                tr.then_inc(turned, 1)

            def result(e, a, r):
                pe.wait_ge(a_ready, e + 1)
                since(pe, y_ready, e)
                pe.wait_ge(k.e_loaded[a][2], 16 * r + 16)
                w = expert_view(k, a, 2)
                for kk in range(KD):
                    for f in range(KE):
                        mm = pe.matmul(ps[:, 4, SLOTS * kk:SLOTS * (kk + 1)], w[:, f, kk * P:(kk + 1) * P],
                                       aT[:, a, SLOTS * f:SLOTS * (f + 1)], start=f == 0, stop=f == KE - 1)
                mm.then_inc(y_done, 1)

            def step(e, a, r, first=False, last=False):
                hidden(e, a, r)
                if not first:
                    pe.wait_ge(y_ready, e)
                    since(pe, rows_ready, e - 1)
                if not last:
                    gather(e + 1, 1 - a)
                if not first:
                    turn(e - 1, 1 - a)
                result(e, a, r)

            gather(0, 0)
            step(0, 0, 0, first=True)
            step(1, 1, 0)
            pairs(pe, step, 1, half - 1)
            step(NE - 2, 0, half - 1)
            step(NE - 1, 1, half - 1, last=True)
            pe.wait_ge(y_ready, NE)
            pe.wait_ge(rows_ready, NE - 1)
            turn(NE - 1, 1)

        @block.scalar
        def _(act):
            def silu(e, a):
                act.wait_ge(gu_done, e + 1)
                since(act, a_ready, e - 1)
                act.activation(sg[:, a, :], ps[:, 2 + a, 0:KE * SLOTS], ACT.Silu).then_inc(silu_done, 1)

            def rows(e, a, r):
                act.wait_ge(turned, e + 1)
                since(act, stored[a], 16 * r)
                act.copy(yn[0:SLOTS, a, :], ps[0:SLOTS, 5:7, :].rearrange("p b n -> p (b n)")).then_inc(rows_ready, 1)
                act.wait_ge(rows_ready, e + 1)
                act.dma_start(k.ypad[bass.ds(SLOTS * e, SLOTS)], yn[0:SLOTS, a, :]).then_inc(stored[a], 16)

            def step(e, a, r):
                silu(e, a)
                rows(e - 1, 1 - a, r - (1 - a))

            silu(0, 0)
            silu(1, 1)
            rows(0, 0, 0)
            step(2, 0, 1)
            step(3, 1, 1)
            pairs(act, step, 2)
            rows(NE - 1, 1, half - 1)
            for a in range(2):
                act.wait_ge(stored[a], 16 * half)

        @block.vector
        def _(dve):
            def choose(e, a):
                since(dve, x_done, e - 1)
                dve.tensor_tensor(pick[:, a, :, :], spread(k.iota, 1, NT),
                                  k.rk[:, :, bass.ds(e, 1)].to_broadcast([P, NT, SLOTS]),
                                  ALU.is_equal).then_inc(picked, 1)

            def tokens(e, a):
                dve.wait_ge(x_done, e + 1)
                since(dve, gu_done, e - 1)
                dve.tensor_copy(xT[:, a, :, :], ps[:, a, :].rearrange("p (k s) -> p k s", k=KD)).then_inc(x_ready, 1)

            def gated(e, a):
                dve.wait_ge(silu_done, e + 1)
                since(dve, y_done, e - 1)
                dve.tensor_tensor(aT[:, a, :], sg[:, a, :], ps[:, 2 + a, KE * SLOTS:], ALU.mult).then_inc(a_ready, 1)

            def results(e, a):
                dve.wait_ge(y_done, e + 1)
                since(dve, turned, e - 1)
                dve.tensor_copy(yT[:, a, :], ps[:, 4, :]).then_inc(y_ready, 1)

            def step(e, a, r, last=False):
                if not last:
                    choose(e + 1, 1 - a)
                gated(e, a)
                if not last:
                    tokens(e + 1, 1 - a)
                results(e, a)

            choose(0, 0)
            tokens(0, 0)
            step(0, 0, 0)
            step(1, 1, 0)
            pairs(dve, step, 1, half - 1)
            step(NE - 2, 0, half - 1)
            step(NE - 1, 1, half - 1, last=True)


def more_blocks(k):
    nc, ps = k.nc, k.ps
    t = Z0 + 4096
    table = view(k, t, 16, NE)
    prod = view(k, t + 1024, 16, NE)
    ids, base, upto = (view(k, t + 2048 + 16 * i, 16) for i in range(3))
    ends = view(k, t + 2112, NE)
    number = k.iota[:, 0:16]
    pick = view(k, t + 2176, NT, SLOTS)
    want = view(k, t + 2432, NT)
    want0 = view(k, t + 2440, NT)
    xT = view(k, t + 2560, KD, SLOTS)
    sg, aT = view(k, t + 3072, KE * SLOTS), view(k, t + 3328, KE * SLOTS)
    yT = view(k, t + 3584, KD * SLOTS)
    yn = view(k, t + 4096, D)
    (listed, loaded, picked, x_done, x_ready, gu_done, silu_done, a_ready, y_done, y_ready, turned, rows_ready,
     stored) = (k.sem("more_" + n) for n in
                ("listed", "loaded", "picked", "x_done", "x_ready", "hidden_done", "silu_done", "a_ready", "y_done",
                 "y_ready", "turned", "rows_ready", "stored"))

    list_step = Counter(k.sem("more_list_step"))

    def if_any(eng, body):
        n = eng.value_load(k.flag[0:1, 0:1].bitcast(I32), min_val=0, max_val=XB)
        with eng.If(n > 0):
            body()

    def blocks(eng, step):
        step(0)
        with eng.Fori(1, XB) as b:
            step(b)

    with nc.Block() as block:
        @block.sync
        def _(sp):
            def step(b):
                since(sp, y_done, b)
                e = sp.value_load(ids[0:1, bass.ds(b, 1)].bitcast(I32), min_val=0, max_val=NE - 1)
                for i, w in enumerate((k.d["expert_w_gate_2"], k.d["expert_w_up_2"], k.d["expert_w_down_2"])):
                    src = w[0][bass.ds(e, 1)].rearrange("e (k p) n -> p (e k) n", p=P)
                    sp.dma_start(expert_view(k, 0, i), src).then_inc(loaded, 16)

            def body():
                sp.wait_ge(listed, 1)
                blocks(sp, step)

            if_any(sp, body)

        @block.vector
        def _(dve):
            def tt(o, a, b, op):
                k.link(dve, dve.tensor_tensor(o, a, b, op), list_step)

            def step(b):
                e = dve.value_load(ids[0:1, bass.ds(b, 1)].bitcast(I32), min_val=0, max_val=NE - 1)
                since(dve, x_done, b)
                dve.tensor_copy(want0, k.rk[:, :, bass.ds(e, 1)].rearrange("p t o -> p (t o)")).then_inc(picked, 1)
                dve.wait_ge(picked, 3 * b + 1)
                dve.tensor_scalar(want, want0, base[:, bass.ds(b, 1)], None, ALU.subtract).then_inc(picked, 1)
                dve.wait_ge(picked, 3 * b + 2)
                dve.tensor_tensor(pick, spread(k.iota, 1, NT), spread(want, 2, SLOTS), ALU.is_equal).then_inc(picked, 1)
                dve.wait_ge(x_done, b + 1)
                dve.tensor_copy(xT, ps[:, 0, :].rearrange("p (k s) -> p k s", k=KD)).then_inc(x_ready, 1)
                dve.wait_ge(silu_done, b + 1)
                dve.tensor_tensor(aT, sg, ps[:, 1, KE * SLOTS:], ALU.mult).then_inc(a_ready, 1)
                dve.wait_ge(y_done, b + 1)
                dve.tensor_copy(yT, ps[:, 2, :]).then_inc(y_ready, 1)

            def body():
                tt(ends, k.starts, k.nb, ALU.add)
                tt(table, spread(number, 2, NE), spread(k.starts, 1, 16), ALU.is_ge)
                tt(prod, spread(number, 2, NE), spread(ends, 1, 16), ALU.is_ge)
                tt(table, table, prod, ALU.subtract)
                tt(prod, table, spread(k.iota, 1, 16), ALU.mult)
                k.link(dve, dve.tensor_reduce(upto, prod, AX_X, ALU.add), list_step)
                tt(prod, table, spread(k.starts, 1, 16), ALU.mult)
                k.link(dve, dve.tensor_reduce(base, prod, AX_X, ALU.add), list_step)
                tt(base, number, base, ALU.subtract)
                k.link(dve, dve.tensor_scalar(base, base, 1.0, float(SLOTS), ALU.add, ALU.mult), list_step)
                dve.tensor_copy(ids.bitcast(I32), upto).then_inc(listed, 1)
                dve.wait_ge(listed, 1)
                blocks(dve, step)

            if_any(dve, body)

        @block.tensor
        def _(pe):
            def step(b):
                pe.wait_ge(picked, 3 * b + 3)
                for kk in range(KD):
                    for m in range(NT):
                        mm = pe.matmul(ps[:, 0, SLOTS * kk:SLOTS * (kk + 1)], k.hn[:, m, kk * P:(kk + 1) * P],
                                       pick[:, m, :], start=m == 0, stop=m == NT - 1)
                mm.then_inc(x_done, 1)
                pe.wait_ge(x_ready, b + 1)
                pe.wait_ge(loaded, 48 * b + 48)
                for i in range(2):
                    w = expert_view(k, 0, i)
                    for f in range(KE):
                        o = KE * SLOTS * i + SLOTS * f
                        for kk in range(KD):
                            mm = pe.matmul(ps[:, 1, o:o + SLOTS], w[:, kk, f * P:(f + 1) * P], xT[:, kk, :],
                                           start=kk == 0, stop=kk == KD - 1)
                mm.then_inc(gu_done, 1)
                pe.wait_ge(a_ready, b + 1)
                w = expert_view(k, 0, 2)
                for kk in range(KD):
                    for f in range(KE):
                        mm = pe.matmul(ps[:, 2, SLOTS * kk:SLOTS * (kk + 1)], w[:, f, kk * P:(kk + 1) * P],
                                       aT[:, SLOTS * f:SLOTS * (f + 1)], start=f == 0, stop=f == KE - 1)
                mm.then_inc(y_done, 1)
                pe.wait_ge(y_ready, b + 1)
                since(pe, rows_ready, b)
                for kk in range(KD):
                    tr = pe.matmul(ps[0:SLOTS, 5 + kk // 4, P * (kk % 4):P * (kk % 4 + 1)],
                                   yT[:, SLOTS * kk:SLOTS * (kk + 1)], k.ident, start=True, stop=True)
                tr.then_inc(turned, 1)

            if_any(pe, lambda: blocks(pe, step))

        @block.scalar
        def _(act):
            def step(b):
                act.wait_ge(gu_done, b + 1)
                act.activation(sg, ps[:, 1, 0:KE * SLOTS], ACT.Silu).then_inc(silu_done, 1)
                act.wait_ge(turned, b + 1)
                since(act, stored, 16 * b)
                act.copy(yn[0:SLOTS], ps[0:SLOTS, 5:7, :].rearrange("p b n -> p (b n)")).then_inc(rows_ready, 1)
                act.wait_ge(rows_ready, b + 1)
                act.dma_start(k.ypad[bass.ds(SLOTS * (NE + b), SLOTS)], yn[0:SLOTS]).then_inc(stored, 16)

            def body():
                blocks(act, step)
                act.wait_ge(stored, 16 * XB)

            if_any(act, body)



def finish(k):
    nc, d = k.nc, k.d
    x3 = view(k, H0, NT, D)
    rows = [view(k, RING, NT, D), view(k, RING + 4096, NT, D)]
    gain = view(k, RING + 8192, D)
    squares = view(k, RING + 9216, D)
    n1 = Norm(k, "norm_last", x3, NT, scratch=squares, stat=0)
    gathered = [k.sem(f"gathered{i}") for i in range(2 * NT)]
    g_in, x_in, summed, gained, out_st = (k.sem("last_" + n) for n in ("gain", "x_loaded", "summed", "gained", "stored"))
    out = k.out[0].rearrange("(m p) n -> p m n", p=P)

    with nc.Block() as block:
        @block.gpsimd
        def _(pool):
            for m in range(NT):
                for c in range(2):
                    pool.indirect_dma_start(rows[c][:, m, :], None, k.ypad,
                                            bass.IndirectOffsetOnAxis(ap=k.dest[:, c, m:m + 1].bitcast(U32), axis=0)
                                            ).then_inc(gathered[2 * m + c], 16)

        @block.sync
        def _(sp):
            sp.dma_start(gain, d["final_norm_g_2"].rearrange("(a n) -> a n", a=1).to_broadcast([P, D])).then_inc(g_in, 16)
            sp.wait_ge(gained, NT)
            sp.dma_start(out, x3).then_inc(out_st, 16)
            sp.wait_ge(out_st, 16)

        @block.scalar
        def _(act):
            act.wait_ge(summed, 2 * NT)
            n1.scalar_sums(act)
            n1.scalar_root(act)

        @block.vector
        def _(dve):
            for m in range(NT):
                for c in range(2):
                    dve.wait_ge(gathered[2 * m + c], 16)
                    if c:
                        dve.wait_ge(summed, 2 * m + 1)
                    dve.scalar_tensor_tensor(out=x3[:, m, :], in0=rows[c][:, m, :], scalar=k.gate_w[:, c, m:m + 1],
                                             in1=x3[:, m, :], op0=ALU.mult, op1=ALU.add).then_inc(summed, 1)
            n1.vector_mean(dve)
            n1.vector_scale(dve)
            dve.wait_ge(n1.normed, NT)
            dve.wait_ge(g_in, 16)
            for m in range(NT):
                dve.tensor_tensor(x3[:, m, :], x3[:, m, :], gain, ALU.mult).then_inc(gained, 1)





def program(nc, dram, out, stop=None):
    with ExitStack() as ctx:
        k = Kernel(nc, ctx, dram, out)
        k.chunks, k.next_chunk = weight_chunks(k), 0
        k.h_dram = [nc.dram_tensor(f"h{i}", (S, D), F32, kind="Internal").ap() for i in range(4)]
        k.bias_dram = nc.dram_tensor("bias", (NH, 2048), F32, kind="Internal").ap()
        k.us_dram = nc.dram_tensor("us", (S, 512), F32, kind="Internal").ap()
        k.ys_dram = nc.dram_tensor("ys", (S, 512), F32, kind="Internal").ap()
        k.ypad = nc.dram_tensor("ypad", (N_ROWS, D), F32, kind="Internal").ap()
        for f in STAGES:
            f(k)
            if f is not finish:
                k.end_phase()
            if stop == f.__name__:
                break
        return k


def even_out(k):
    out_projection(k, "even_out", "even_out", k.d["x"][0], k.h_dram[0])


def odd_out(k):
    out_projection(k, "odd_out", "odd_out", k.h_dram[0], None)


STAGES = [even_in, even_mix, even_out, odd_in, compress, nsa, odd_out, mix_in, ssm, mix_mid, mix_out, moe, more_blocks, finish]

_INS = ["x", "mem", "norm_g", "final_g", "mem_norm_g", "rel_bias", "ev_w_in", "ev_pool_w", "ev_pool_scale",
        "ev_w_mem_kv", "ev_w_out", "od_w_in", "od_cmp_pe", "od_cmp_w1", "od_cmp_b1", "od_cmp_w2", "od_w_mem_kv",
        "od_w_out", "mix_norm_g_2", "w_in_2", "w_fourier_out_2", "ssm_A_re_2", "ssm_A_im_2", "ssm_log_dt_2",
        "ssm_B_re_2", "ssm_B_im_2", "ssm_C_re_2", "ssm_C_im_2", "ssm_D_2", "ssm_w_glu_2", "w_ssm_out_2", "w_out_2",
        "ffn_norm_g_2", "router_group_w_2", "router_group_b_2", "router_expert_w_2", "router_expert_b_2",
        "expert_w_gate_2", "expert_w_up_2", "expert_w_down_2", "final_norm_g_2"]


def kernel(**inputs):
    import numpy as _np
    import concourse.bacc as _bacc
    from concourse import mybir as _mybir
    from concourse.bass_utils import run_bass_kernel_spmd as _run

    nc = _bacc.Bacc("TRN2", target_bir_lowering=False, num_devices=1)
    arrays, dram = {}, {}
    held = {name: _np.ascontiguousarray(inputs[name]) for name in _INS}
    held.update(shape_constants())
    for name, a in held.items():
        arrays[f"in_{name}"] = a
        dram[name] = nc.dram_tensor(f"in_{name}", a.shape, _mybir.dt.from_np(a.dtype), kind="ExternalInput").ap()
    out = nc.dram_tensor("out_0", (1, S, D), _mybir.dt.from_np(_np.dtype("float32")), kind="ExternalOutput").ap()
    program(nc, dram, out)
    r = _run(nc, [arrays], core_ids=[0])
    return r.results[0]["out_0"]
```

```python
from contextlib import ExitStack

import numpy as np

import concourse.bass as bass
from concourse import mybir

ALU = mybir.AluOpType
ACT = mybir.ActivationFunctionType
AX_X = mybir.AxisListType.X
F32 = mybir.dt.float32
F32R = mybir.dt.float32r
I32 = mybir.dt.int32
U32 = mybir.dt.uint32

P = 128
S = 512
NT = S // P
D = 1024
KD = D // P
EPS = 1e-6
BIG = 1e30

POOL_W, N_WIN = 768, 4
WINDOWS = (2, 4, 8, 16)
PG = POOL_W // N_WIN
PH = PG // 2
RH, RDK, RDV = 4, 128, 192
MH, MDH, N_MEM = 4, 128, 256
MT = N_MEM // P
D_IN = 2048
KI = D_IN // P
NH, NKV, DH = 12, 2, 128
HPG = NH // NKV
NCMP = 31
CMP_HID = 256
NBUCKET = 32
FW, FG = 512, 4
SG, SC, SN = 32, 16, 64
GP = SG // 2
L = 8
NCH = S // L
EG, EPG, NE = 8, 8, 64
DE = 512
KE = DE // P
SLOTS = 64
XB = 15
N_ROWS = (NE + XB) * SLOTS

SLOT = 4096
RING, NRING = 0, 3
PIECE = 256
H0 = RING + NRING * SLOT
Y0 = H0 + 4096
U0 = Y0 + 8192
Z0 = U0 + 8192
C0 = Z0 + 17408
TOTAL = C0 + 3000


def shape_constants():
    c = {}
    c["ident"] = np.eye(P, dtype=np.float32)
    half = RDK // 2
    inv = np.float32(10000.0) ** (-np.arange(half, dtype=np.float32) / half)
    ang = (np.arange(S, dtype=np.float32)[:, None] * inv[None, :].astype(np.float32)).astype(np.float32)
    cos, sin = np.cos(ang.astype(np.float64)), np.sin(ang.astype(np.float64))
    sc = RDK ** -0.5
    rot = np.stack([cos * sc, sin * sc, cos, sin])
    c["rot"] = rot.reshape(4, NT, P, half).transpose(2, 0, 1, 3).reshape(P, -1).astype(np.float32)
    lg = np.log(1.0 - np.exp2(-5.0 - np.arange(RH)))
    diff = np.arange(S)[None, :] - np.arange(P)[:, None]
    dec = np.where(diff >= 0, np.exp(lg[:, None, None] * np.maximum(diff, 0)), 0.0)
    c["decay"] = dec.transpose(1, 0, 2).reshape(P, -1).astype(np.float32)
    s, t = np.arange(P)[:, None], np.arange(P)[None, :]
    band = []
    for w in WINDOWS:
        cur = ((t >= s) & (t - s < w)).astype(np.float64)
        first = cur / np.minimum(t + 1, w) - (s == t)
        prev = ((t + P - s) < w).astype(np.float64) / w
        band += [first, cur / w - (s == t), prev]
    c["band"] = np.stack(band).transpose(1, 0, 2).reshape(P, -1).astype(np.float32)

    def bucket(rel):
        n = np.maximum(rel, 0)
        nf = np.maximum(n, 1).astype(np.float32)
        large = 16 + (np.log(nf / np.float32(16)) / np.float32(np.log(8.0)) * np.float32(16)).astype(np.int32)
        return np.where(n < 16, n, np.minimum(large, 31))

    rel_n = np.arange(1024) - 512
    b, m = np.arange(16)[:, None], np.arange(64)[None, :]
    rel_c = (497 + b - 16 * m).reshape(-1)
    rel = np.concatenate([rel_n, rel_c])
    hot = np.zeros((NBUCKET + 1, 2048), np.float32)
    ok = rel >= 0
    hot[bucket(rel)[ok], np.nonzero(ok)[0]] = 1
    hot[NBUCKET, ~ok] = 1
    c["hot"] = hot
    c["from31"] = (np.arange(P) >= 31).astype(np.float32)[:, None]
    a = 2 * np.pi * np.outer(np.arange(S), np.arange(S)) / S
    c["cosS"] = (np.cos(a) / 256).reshape(NT, P, S).transpose(1, 0, 2).reshape(P, -1).astype(np.float32)
    c["sinS"] = (-np.sin(a) / 256).reshape(NT, P, S).transpose(1, 0, 2).reshape(P, -1).astype(np.float32)
    a = 2 * np.pi * np.outer(np.arange(P), np.arange(P)) / P
    c["dft"] = np.concatenate([np.cos(a), np.sin(a)], 1).astype(np.float32)
    c["before"] = (s < t).astype(np.float32)
    c["iota"] = np.tile(np.arange(64, dtype=np.float32), (P, 1))
    return c


def view(k, off, *shape):
    n = int(np.prod(shape))
    ap = k.mem[:, off:off + n]
    if len(shape) == 2:
        return ap.rearrange("p (a b) -> p a b", a=shape[0])
    if len(shape) == 3:
        return ap.rearrange("p (a b c) -> p a b c", a=shape[0], b=shape[1])
    if len(shape) == 4:
        return ap.rearrange("p (a b c d) -> p a b c d", a=shape[0], b=shape[1], c=shape[2])
    return ap


def spread(ap, dim, n):
    dims = [list(x) for x in ap.ap]
    dims.insert(dim, [0, n])
    return bass.AP(ap.tensor, ap.offset, dims)


def backwards(ap):
    dims = [list(x) for x in ap.ap]
    step, n = dims[-1]
    dims[-1] = [-step, n]
    return bass.AP(ap.tensor, ap.offset + step * (n - 1), dims)


class Counter:

    def __init__(self, sem):
        self.sem, self.n = sem, 0

    def inc(self, ins, by=1):
        ins.then_inc(self.sem, by)
        self.n += by
        return self.n


class Kernel:
    def __init__(self, nc, ctx, dram, out):
        self.nc, self.ctx, self.d, self.out = nc, ctx, dram, out
        self.mem = ctx.enter_context(nc.sbuf_tensor("mem", [P, TOTAL], F32))
        base = nc.sbuf_base - 4 * TOTAL
        self.u_parts = nc.alloc_sbuf_tensor_at("u_parts", [P, 2 * KD * S], F32R, offset=base + 4 * U0).ap().rearrange(
            "p (i k s) -> p i k s", i=2, k=KD)
        self.w_parts = nc.alloc_sbuf_tensor_at("w_parts", [P, 4 * KD * PIECE], F32R, offset=base + 4 * (RING + SLOT)
                                               ).ap()
        self.u_parts2 = nc.alloc_sbuf_tensor_at("u_parts2", [P, 2 * KD * S], F32R, offset=base + 4 * Z0).ap().rearrange(
            "p (i k s) -> p i k s", i=2, k=KD)
        self.w_raw = nc.alloc_sbuf_tensor_at("w_raw", [P, 2 * KD * PIECE], F32, offset=base + 4 * RING).ap()
        gains = nc.alloc_sbuf_tensor_at("gains", [P, 4 * KD], F32, offset=base + 4 * (C0 + P)).ap()
        self.ps = ctx.enter_context(nc.psum_tensor("ps", [P, 8, 512], F32))
        self.phase_sems = []
        self.w_loaded = [self.lasting_sem(f"w_loaded{i}") for i in range(NRING)]
        self.chunk_used = self.lasting_sem("chunk_used")
        self.dve_step = Counter(self.lasting_sem("dve_step"))
        self.ident = view(self, C0, P)
        self.g_even = gains[:, 0 * KD:1 * KD]
        self.g_odd = gains[:, 1 * KD:2 * KD]
        self.g_mem = gains[:, 2 * KD:3 * KD]
        self.g_mix = gains[:, 3 * KD:4 * KD]
        self.stat = view(self, C0 + 160, 64)
        self.misc = C0 + 256

    def lasting_sem(self, name):
        return self.ctx.enter_context(self.nc.semaphore(name))

    def sem(self, name):
        s = self.nc.alloc_semaphore(name)
        self.phase_sems.append(s)
        return s

    def end_phase(self):
        self.nc.all_engine_barrier()
        self.nc.clear_and_free_semaphores(self.phase_sems)
        self.nc.all_engine_barrier()
        self.phase_sems = []

    def link(self, eng, ins, which=None):
        c = which or self.dve_step
        c.inc(ins)
        eng.wait_ge(c.sem, c.n)

    def slot(self, n):
        return RING + (n % NRING) * SLOT



def weight_chunks(k):
    d = k.d
    w = []

    def cols(phase, src, lo, n):
        w.append((phase, src.rearrange("(k p) n -> p k n", p=P)[:, :, lo:lo + n]))

    for layer in (d["ev_w_mem_kv"][0], d["od_w_mem_kv"][0]):
        for c in range(2):
            cols("mem_in", layer, 512 * c, 512)

    for kv in range(2):
        for half in range(2):
            w.append(("compress", d["od_cmp_w1"][0, kv].rearrange("(l d) n -> d l n", d=DH)
                      [:, 16 * half:16 * half + 16, :]))
    w.append(("mix_mid", d["ssm_w_glu_2"][0].rearrange("(k p) n -> p k n", p=P)))
    w.append(("mix_mid", d["w_ssm_out_2"][0].rearrange("(k p) n -> p k n", p=P)))
    w.append(("mix_mid", d["w_fourier_out_2"][0].rearrange("(k p) n -> p k n", p=P)))
    for c in range(2):
        cols("mix_out", d["w_out_2"][0], 512 * c, 512)
    return w


PHASES = ["mem_in", "even_in", "even_mix", "even_out", "odd_in", "compress", "nsa", "odd_out", "mix_in", "ssm",
          "mix_mid", "mix_out"]
SPLIT_PHASES = ("even_in", "even_out", "odd_in", "odd_out", "mix_in")


def pieces(*ranges):
    return [(what, lo + c, min(PIECE, n - c), turned) for what, lo, n, turned in ranges for c in range(0, n, PIECE)]


EVEN_IN = pieces(("za", 0, 768, False), ("rq", 768, 512, False), ("rk", 1280, 512, False), ("rv", 1792, 768, False),
                 ("xq", 2560, 512, True), ("gate", 3072, 2048, False))
ODD_IN = pieces(("q", 0, 1536, True), ("kcvc", 1536, 512, True), ("ks", 2048, 256, True), ("vs", 2304, 256, False),
                ("kw", 2560, 256, True), ("vw", 2816, 256, False), ("gl", 3072, 36, False), ("xq", 3108, 512, True),
                ("gate", 3620, 2048, False))
MIX_IN = pieces(("us", 512, 512, False), ("uf", 0, 512, True), ("gate", 1024, 2048, False))


def load_weights(k, eng, phase):
    at = PHASES.index(phase)
    while k.next_chunk < len(k.chunks):
        n = k.next_chunk
        use = PHASES.index(k.chunks[n][0])
        if (n >= NRING and PHASES.index(k.chunks[n - NRING][0]) > at
                or any(at <= PHASES.index(x) < use for x in SPLIT_PHASES)):
            return
        src = k.chunks[n][1]
        if n >= NRING:
            eng.wait_ge(k.chunk_used, n - NRING + 1)
        a, b = src.shape[1], src.shape[2]
        eng.dma_start(view(k, k.slot(n), a, b), src).then_inc(k.w_loaded[n % NRING], 16)
        k.next_chunk += 1


def first_chunk(k, phase):
    return [i for i, c in enumerate(k.chunks) if c[0] == phase][0]


def wait_chunk(k, eng, n):
    eng.wait_ge(k.w_loaded[n % NRING], 16 * (n // NRING + 1))


class Group:

    def __init__(self, i, n, what, col, width, turned, t, last, done, evac, place):
        self.i, self.n, self.what, self.col, self.width, self.turned, self.t = i, n, what, col, width, turned, t
        self.last, self.done, self.evac, self.place = last, done, evac, place
        self.bank = i % 8


def plan(table, first, row_tiles, on_act):
    groups, done, place = [], 0, {"act": 0, "dve": 0}
    base_col = {}
    for c, (what, lo, n, turned) in enumerate(table):
        base_col.setdefault(what, lo)
        tiles = n // P if turned else row_tiles
        for t in range(tiles):
            last = t == tiles - 1
            done += 0 if last else 1
            eng = "act" if what in on_act else "dve"
            place[eng] += 1
            groups.append(Group(len(groups), first + c, what, lo - base_col[what], n, turned, t, last, done, eng,
                                place[eng]))
    return groups


class Projection:

    def __init__(self, k, name, table, first, row_tiles, on_act, uT, n_tok):
        self.k, self.uT, self.n_tok = k, uT, n_tok
        self.groups = plan(table, first, row_tiles, on_act)
        self.group_done = k.sem(name + "_group_done")
        self.emptied = {"act": k.sem(name + "_emptied_by_act"), "dve": k.sem(name + "_emptied_by_dve")}

    def tensor(self, pe):
        k = self.k
        for g in self.groups:
            if g.t == 0:
                wait_chunk(k, pe, g.n)
            if g.i >= 8:
                old = self.groups[g.i - 8]
                pe.wait_ge(self.emptied[old.evac], old.place)
            w = view(k, k.slot(g.n), KD, g.width)
            for kk in range(KD):
                if g.turned:
                    mm = pe.matmul(k.ps[:, g.bank, 0:self.n_tok], w[:, kk, g.t * P:(g.t + 1) * P],
                                   self.uT[:, kk, :], start=kk == 0, stop=kk == KD - 1)
                else:
                    mm = pe.matmul(k.ps[:, g.bank, 0:g.width], self.uT[:, kk, g.t * P:(g.t + 1) * P],
                                   w[:, kk, :], start=kk == 0, stop=kk == KD - 1)
            mm.then_inc(k.chunk_used if g.last else self.group_done, 1)

    def wait_group(self, eng, g):
        if g.last:
            eng.wait_ge(self.k.chunk_used, g.n + 1)
        else:
            eng.wait_ge(self.group_done, g.done)


class SplitProjection:

    def __init__(self, k, name, table, src, on_act=()):
        self.k, self.table = k, table
        rows = src.rearrange("(h k p) n -> h p k n", k=KD, p=P)
        self.src = [rows[n % rows.shape[0], :, :, lo:lo + w] for n, (_, lo, w, _) in enumerate(table)]
        self.groups = plan(table, 0, NT, on_act)
        self.upto = [sum(g.n <= n for g in self.groups) for n in range(len(table))]
        self.loaded = [k.sem(f"{name}_piece_loaded{i}") for i in range(2)]
        self.high, self.low = k.sem(name + "_high_ready"), k.sem(name + "_low_ready")
        self.group_done = k.sem(name + "_group_done")
        self.emptied = {"act": k.sem(name + "_emptied_by_act"), "dve": k.sem(name + "_emptied_by_dve")}

    def raw(self, n):
        w = self.table[n][2]
        o = KD * PIECE * (n % 2)
        return self.k.w_raw[:, o:o + KD * w].rearrange("p (k n) -> p k n", k=KD)

    def part(self, n, i):
        w, o = self.table[n][2], KD * PIECE * (2 * (n % 2) + i)
        return self.k.w_parts[:, o:o + KD * w].rearrange("p (k n) -> p k n", k=KD)

    def sync(self, sp):
        for n in range(len(self.table)):
            if n >= 2:
                sp.wait_ge(self.low, n - 1)
            sp.dma_start(self.raw(n), self.src[n]).then_inc(self.loaded[n % 2], 16)

    def scalar_split(self, act, n):
        if n < len(self.table):
            act.wait_ge(self.loaded[n % 2], 16 * (n // 2 + 1))
            if n >= 2:
                act.wait_ge(self.group_done, self.upto[n - 2])
            act.copy(self.part(n, 0), self.raw(n)).then_inc(self.high, 1)

    def vector_split(self, dve, n):
        if n < len(self.table):
            dve.wait_ge(self.high, n + 1)
            dve.tensor_tensor(self.part(n, 1), self.raw(n), self.part(n, 0).bitcast(F32),
                              ALU.subtract).then_inc(self.low, 1)

    def tensor(self, pe):
        k = self.k
        for g in self.groups:
            if g.t == 0:
                pe.wait_ge(self.low, g.n + 1)
            if g.i >= 8:
                old = self.groups[g.i - 8]
                pe.wait_ge(self.emptied[old.evac], old.place)
            out = k.ps[:, g.bank, 0:S if g.turned else g.width]
            w, u = [self.part(g.n, i) for i in range(2)], k.u_parts
            for kk in range(KD):
                for x, y in ((0, 0), (0, 1), (1, 0)):
                    first, last = kk == 0 and x + y == 0, kk == KD - 1 and x == 1
                    if g.turned:
                        mm = pe.matmul(out, w[x][:, kk, g.t * P:(g.t + 1) * P], u[:, y, kk, :], start=first, stop=last)
                    else:
                        mm = pe.matmul(out, u[:, x, kk, g.t * P:(g.t + 1) * P], w[y][:, kk, :], start=first, stop=last)
            mm.then_inc(self.group_done, 1)

    def wait_group(self, eng, g):
        eng.wait_ge(self.group_done, g.i + 1)



class Norm:

    def __init__(self, k, name, src, T, uT=None, gT=None, scratch=None, stat=0, prior=None, dst=None):
        self.k, self.src, self.T, self.uT, self.gT, self.scratch = k, src, T, uT, gT, scratch
        self.dst = src if dst is None else dst
        self.ss = k.stat[:, stat:stat + T]
        self.ms = k.stat[:, stat + T:stat + 2 * T]
        self.sd = k.stat[:, stat + 2 * T:stat + 3 * T]
        self.rs = k.stat[:, stat + 3 * T:stat + 4 * T]
        self.squared, self.mean, self.root = k.sem(name + "_squared"), k.sem(name + "_mean"), k.sem(name + "_root")
        self.normed, self.turned, self.ready = k.sem(name + "_normed"), k.sem(name + "_turned"), k.sem(name + "_uT")
        self.low = k.sem(name + "_low_ready")
        self.prior = prior

    def scalar_sums(self, act, loaded=None):
        for m in range(self.T):
            if loaded is not None:
                act.wait_ge(loaded[m], 16)
            if m:
                act.wait_ge(self.squared, m)
            ins = act.activation(self.scratch, self.src[:, m, :], ACT.Square, accum_out=self.ss[:, m:m + 1])
            ins.then_inc(self.squared, 1)

    def vector_mean(self, dve):
        dve.wait_ge(self.squared, self.T)
        dve.tensor_scalar(self.ms, self.ss, 1.0 / D, EPS, ALU.mult, ALU.add).then_inc(self.mean, 1)

    def scalar_root(self, act):
        act.wait_ge(self.mean, 1)
        act.activation(self.sd, self.ms, ACT.Sqrt).then_inc(self.root, 1)

    def vector_scale(self, dve):
        dve.wait_ge(self.root, 1)
        self.k.link(dve, dve.reciprocal(self.rs, self.sd))
        for m in range(self.T):
            dve.tensor_scalar(self.dst[:, m, :], self.src[:, m, :], self.rs[:, m:m + 1], None,
                              ALU.mult).then_inc(self.normed, 1)

    def tensor_turn(self, pe, normed=None):
        if normed is None:
            pe.wait_ge(self.normed, self.T)
        for kk in range(KD):
            if self.prior:
                pe.wait_ge(self.prior, kk + 1)
            for m in range(self.T):
                t = pe.transpose(self.k.ps[:, kk, m * P:(m + 1) * P], self.dst[:, m, kk * P:(kk + 1) * P],
                                 self.k.ident)
            t.then_inc(self.turned, 1)

    def scalar_high(self, act):
        for kk in range(KD):
            act.wait_ge(self.turned, kk + 1)
            act.activation(self.k.u_parts[:, 0, kk, :], self.k.ps[:, kk, :], ACT.Copy,
                           scale=self.gT[:, kk:kk + 1]).then_inc(self.ready, 1)

    def vector_low(self, dve):
        for kk in range(KD):
            dve.wait_ge(self.ready, kk + 1)
            dve.scalar_tensor_tensor(out=self.k.u_parts[:, 1, kk, :], in0=self.k.ps[:, kk, :],
                                     scalar=self.gT[:, kk:kk + 1], in1=self.k.u_parts[:, 0, kk, :].bitcast(F32),
                                     op0=ALU.mult, op1=ALU.subtract).then_inc(self.low, 1)

    def scalar_out(self, act):
        for kk in range(KD):
            act.wait_ge(self.turned, kk + 1)
            act.activation(self.uT[:, kk, :], self.k.ps[:, kk, 0:self.T * P], ACT.Copy,
                           scale=self.gT[:, kk:kk + 1]).then_inc(self.ready, 1)



MEM_KV_E = [("mk_e", 0, 512, True), ("mv_e", 512, 512, False)]
MEM_KV_O = [("mk_o", 0, 512, True), ("mv_o", 512, 512, False)]


def mem_in(k):
    nc, d = k.nc, k.d
    mem_nat = view(k, Y0, MT, D)
    memT = view(k, Z0 + 14336, KD, N_MEM)
    zeros = view(k, Z0 + 16384, D)
    x_nat = view(k, H0, NT, D)
    squares = view(k, Z0, D)
    k.mk = [view(k, Z0 + 9216, MH, N_MEM), view(k, Z0 + 11264, MH, N_MEM)]
    k.mv = [view(k, Z0 + 10240, MT, 512), view(k, Z0 + 12288, MT, 512)]
    const_loaded = k.sem("const_loaded")
    zeroed, ypad_zeroed = k.sem("zeroed"), k.sem("ypad_zeroed")
    mem_loaded = [k.sem(f"mem_loaded{m}") for m in range(MT)]
    x_loaded = [k.sem(f"x_loaded{m}") for m in range(NT)]
    norm_m = Norm(k, "norm_mem", mem_nat, MT, memT, k.g_mem, squares, 0)
    norm_x = Norm(k, "norm_even", x_nat, NT, scratch=squares, stat=8)
    kv = Projection(k, "mem_kv", MEM_KV_E + MEM_KV_O, 0, MT, ("mv_e", "mv_o"), memT, N_MEM)

    with nc.Block() as block:
        @block.sync
        def _(sp):
            mem_r = d["mem"][0].rearrange("(m p) n -> p m n", p=P)
            x_r = d["x"][0].rearrange("(m p) n -> p m n", p=P)
            for m in range(MT):
                sp.dma_start(mem_nat[:, m, :], mem_r[:, m, :]).then_inc(mem_loaded[m], 16)
            sp.dma_start(k.ident, d["ident"]).then_inc(const_loaded, 16)
            with nc.allow_non_contiguous_dma(reason="a norm's gains, one per partition"):
                sp.dma_start(k.g_mem, d["mem_norm_g"].rearrange("(k p) -> p k", p=P)).then_inc(const_loaded, 16)
                for m in range(NT):
                    sp.dma_start(x_nat[:, m, :], x_r[:, m, :]).then_inc(x_loaded[m], 16)
                sp.dma_start(k.g_even, d["norm_g"][0].rearrange("(k p) -> p k", p=P)).then_inc(const_loaded, 16)
                sp.dma_start(k.g_odd, d["norm_g"][1].rearrange("(k p) -> p k", p=P)).then_inc(const_loaded, 16)
                sp.dma_start(k.g_mix, d["mix_norm_g_2"][0].rearrange("(k p) -> p k", p=P)).then_inc(const_loaded, 16)
            load_weights(k, sp, "mem_in")
            sp.wait_ge(zeroed, 1)
            sp.dma_start(k.ypad[NE * SLOTS:].rearrange("(p r) n -> p r n", r=8),
                         spread(zeros[0:XB * SLOTS // 8, :], 1, 8)).then_inc(ypad_zeroed, 16)
            sp.wait_ge(ypad_zeroed, 16)

        @block.gpsimd
        def _(pool):
            pool.memset(zeros, 0.0).then_inc(zeroed, 1)

        @block.tensor
        def _(pe):
            pe.wait_ge(const_loaded, 16 * 5)
            norm_m.tensor_turn(pe)
            pe.wait_ge(norm_m.ready, KD)
            kv.tensor(pe)

        @block.scalar
        def _(act):
            norm_m.scalar_sums(act, mem_loaded)
            norm_m.scalar_root(act)
            act.wait_ge(const_loaded, 16 * 5)
            norm_m.scalar_out(act)
            act.wait_ge(norm_m.squared, MT)
            norm_x.scalar_sums(act, x_loaded)
            norm_x.scalar_root(act)
            for g in kv.groups:
                if g.evac == "act":
                    kv.wait_group(act, g)
                    dst = k.mv[g.what == "mv_o"]
                    act.activation(dst[:, g.t, :], k.ps[:, g.bank, :], ACT.Copy).then_inc(kv.emptied["act"], 1)

        @block.vector
        def _(dve):
            norm_m.vector_mean(dve)
            norm_m.vector_scale(dve)
            norm_x.vector_mean(dve)
            norm_x.vector_scale(dve)
            for g in kv.groups:
                if g.evac == "dve":
                    kv.wait_group(dve, g)
                    dst = k.mk[g.what == "mk_o"]
                    dve.tensor_copy(dst[:, g.t, :], k.ps[:, g.bank, 0:N_MEM]).then_inc(kv.emptied["dve"], 1)



def even_in(k):
    nc, d = k.nc, k.d
    x_nat = view(k, H0, NT, D)
    za = view(k, H0, NT, POOL_W)
    rq, rk = view(k, Z0, NT, 512), view(k, Z0 + 2048, NT, 512)
    rv = view(k, Z0 + 4096, NT, RH * RDV)
    k.xqT = view(k, Z0 + 7168, MH, S)
    rot = view(k, Z0 + 14336, 4, NT, 64)
    tmp = view(k, Z0 + 15360, PIECE // RDK, 64)
    y = view(k, Y0, NT, D_IN)
    rot_loaded = k.sem("rot_loaded")
    turn = Norm(k, "turn_even", x_nat, NT, gT=k.g_even)
    pr = SplitProjection(k, "even", EVEN_IN, d["ev_w_in"][0], ("gate",))

    with nc.Block() as block:
        @block.sync
        def _(sp):
            sp.dma_start(view(k, Z0 + 14336, 1024), d["rot"]).then_inc(rot_loaded, 16)
            pr.sync(sp)

        @block.tensor
        def _(pe):
            turn.tensor_turn(pe, 0)
            pe.wait_ge(turn.low, KD)
            pr.tensor(pe)

        @block.scalar
        def _(act):
            turn.scalar_high(act)
            pr.scalar_split(act, 0)
            for g in pr.groups:
                if g.t == 0:
                    pr.scalar_split(act, g.n + 1)
                if g.evac == "act":
                    pr.wait_group(act, g)
                    act.activation(y[:, g.t, g.col:g.col + g.width], k.ps[:, g.bank, 0:g.width],
                                   ACT.Silu).then_inc(pr.emptied["act"], 1)

        @block.vector
        def _(dve):
            turn.vector_low(dve)
            pr.vector_split(dve, 0)
            dve.wait_ge(rot_loaded, 16)
            for g in pr.groups:
                if g.t == 0:
                    pr.vector_split(dve, g.n + 1)
                if g.evac != "dve":
                    continue
                pr.wait_group(dve, g)
                bank = k.ps[:, g.bank, 0:S if g.turned else g.width]
                if g.what in ("rq", "rk"):
                    dve.wait_ge(pr.emptied["dve"], g.place - 1)
                    tab = 0 if g.what == "rq" else 2
                    heads = g.width // RDK
                    cos, sin = (spread(rot[:, tab + i, g.t, :], 1, heads) for i in range(2))
                    x = bank.rearrange("p (h c) -> p h c", h=heads)
                    o = (rq if g.what == "rq" else rk)[:, g.t, g.col:g.col + g.width].rearrange(
                        "p (h c) -> p h c", h=heads)
                    dve.tensor_tensor(o[:, :, 0:64], x[:, :, 0:64], cos, ALU.mult)
                    k.link(dve, dve.tensor_tensor(tmp, x[:, :, 64:128], sin, ALU.mult))
                    k.link(dve, dve.tensor_tensor(o[:, :, 0:64], o[:, :, 0:64], tmp, ALU.subtract))
                    dve.tensor_tensor(o[:, :, 64:128], x[:, :, 0:64], sin, ALU.mult)
                    k.link(dve, dve.tensor_tensor(tmp, x[:, :, 64:128], cos, ALU.mult))
                    ins = dve.tensor_tensor(o[:, :, 64:128], o[:, :, 64:128], tmp, ALU.add)
                elif g.what == "xq":
                    ins = dve.tensor_scalar(k.xqT[:, g.col // P + g.t, :], bank, -(MDH ** -0.5), None, ALU.mult)
                else:
                    dst = za if g.what == "za" else rv
                    ins = dve.tensor_copy(dst[:, g.t, g.col:g.col + g.width], bank)
                ins.then_inc(pr.emptied["dve"], 1)



class MemAttention:

    def __init__(self, k, name, layer, xqT, scratch, stat):
        self.k, self.mk, self.mv, self.xqT = k, k.mk[layer], k.mv[layer], xqT
        self.p = view(k, scratch, 3, N_MEM)
        self.pT = view(k, scratch + 3 * N_MEM, 2, MT, P)
        self.st = view(k, stat, 4, 4)
        self.y = view(k, Y0, NT, D_IN)
        self.scored, self.low, self.exped, self.turned, self.copied, self.mixed, self.stored = (
            k.sem(f"{name}_{n}") for n in ("scored", "low", "exped", "turned", "copied", "mixed", "stored"))
        self.steps = [(h, t) for h in range(MH) for t in range(NT)]

    def tensor(self, pe):
        k, n = self.k, len(self.steps)
        for u in range(n + 3):
            if u < n:
                h, t = self.steps[u]
                if u >= 2:
                    pe.wait_ge(self.exped, u - 1)
                pe.matmul(k.ps[:, u % 2, 0:N_MEM], self.xqT[:, h, t * P:(t + 1) * P], self.mk[:, h, :],
                          start=True, stop=True).then_inc(self.scored, 1)
            if 2 <= u < n + 2:
                v = u - 2
                pe.wait_ge(self.exped, v + 1)
                if v >= 2:
                    pe.wait_ge(self.copied, v - 1)
                for m in range(MT):
                    tr = pe.transpose(k.ps[:, 2 + v % 2, m * P:(m + 1) * P], self.p[:, v % 3, m * P:(m + 1) * P],
                                      k.ident)
                tr.then_inc(self.turned, 1)
            if u >= 3:
                v = u - 3
                h = self.steps[v][0]
                pe.wait_ge(self.copied, v + 1)
                if v >= 2:
                    pe.wait_ge(self.stored, v - 1)
                for m in range(MT):
                    mm = pe.matmul(k.ps[:, 4 + v % 2, 0:MDH], self.pT[:, v % 2, m, :],
                                   self.mv[:, m, h * MDH:(h + 1) * MDH], start=m == 0, stop=m == MT - 1)
                mm.then_inc(self.mixed, 1)

    def scalar(self, act):
        for u in range(len(self.steps)):
            act.wait_ge(self.low, u + 1)
            if u >= 3:
                act.wait_ge(self.turned, u - 2)
            if u >= 4:
                act.wait_ge(self.stored, u - 3)
            act.activation(self.p[:, u % 3, :], self.k.ps[:, u % 2, 0:N_MEM], ACT.Exp, scale=-1.0,
                           bias=self.st[:, u % 4, 0:1], accum_out=self.st[:, u % 4, 1:2]).then_inc(self.exped, 1)

    def vector(self, dve):
        k, n = self.k, len(self.steps)
        for u in range(n + 3):
            if u < n:
                dve.wait_ge(self.scored, u + 1)
                if u >= 2:
                    dve.wait_ge(self.exped, u - 1)
                dve.tensor_reduce(self.st[:, u % 4, 0:1], k.ps[:, u % 2, 0:N_MEM], AX_X, ALU.min).then_inc(self.low, 1)
            if 2 <= u < n + 2:
                v = u - 2
                dve.wait_ge(self.turned, v + 1)
                if v >= 2:
                    dve.wait_ge(self.mixed, v - 1)
                dve.tensor_copy(self.pT[:, v % 2, :, :], k.ps[:, 2 + v % 2, 0:N_MEM]
                                .rearrange("p (m q) -> p m q", m=MT)).then_inc(self.copied, 1)
            if u >= 3:
                v = u - 3
                h, t = self.steps[v]
                dve.wait_ge(self.mixed, v + 1)
                k.link(dve, dve.reciprocal(self.st[:, v % 4, 2:3], self.st[:, v % 4, 1:2]))
                ys = self.y[:, t, 1536 + h * MDH:1536 + (h + 1) * MDH]
                dve.scalar_tensor_tensor(out=ys, in0=k.ps[:, 4 + v % 2, 0:MDH], scalar=self.st[:, v % 4, 2:3],
                                         in1=ys, op0=ALU.mult, op1=ALU.mult).then_inc(self.stored, 1)



def even_mix(k):
    nc, d = k.nc, k.d
    za = view(k, H0, NT, POOL_W)
    rq, rk = view(k, Z0, NT, 512), view(k, Z0 + 2048, NT, 512)
    rv = view(k, Z0 + 4096, NT, RH * RDV)
    rqT, rkT = view(k, U0, RH, S), view(k, U0 + 2048, RH, S)
    decay = view(k, U0 + 4096, RH, S)
    att = view(k, Z0, 2, NT, S)
    pooled = [view(k, U0 + 7168, 2, S), view(k, H0 + 3072, 2, S)]
    band = view(k, Z0 + 13312, N_WIN * 3, P)
    pool_w = view(k, Z0 + 14848, N_WIN, 2, PG)
    pscale = view(k, Z0 + 16384, POOL_W)
    ln = view(k, k.misc + 1024, 2, RDV)
    bn = view(k, k.misc + 1408, 2, NT, 6)
    mv = view(k, k.misc + 1456, 2, NT, 2)
    sd = view(k, k.misc + 1472, 2, NT, 3)
    ptmp = view(k, U0 + 6144, 2, PG)
    y = view(k, Y0, NT, D_IN)
    ma = MemAttention(k, "mem_e", 0, k.xqT, k.misc, k.misc + 1536)
    tab, turned, copied_a, copied_v, scored, decayed, mixed, ln_in, ln_root, ln_out = (
        k.sem("ret_" + n) for n in ("tables", "turned", "copied_act", "copied_dve", "scored", "decayed", "mixed",
                                    "moments", "root", "normed"))
    pool_in, pooled_by, pool_mm, pool_out = (k.sem("pool_" + n) for n in ("banded", "copied", "mixed", "stored"))

    with nc.Block() as block:
        @block.sync
        def _(sp):
            sp.dma_start(view(k, U0 + 4096, 2048), d["decay"]).then_inc(tab, 16)
            sp.dma_start(view(k, Z0 + 13312, 1536), d["band"]).then_inc(tab, 16)
            sp.dma_start(pool_w[0:PH], d["ev_pool_w"][0].rearrange("g (h c) n -> c g h n", h=2)).then_inc(tab, 16)
            sp.dma_start(pscale, d["ev_pool_scale"].to_broadcast([P, POOL_W])).then_inc(tab, 16)
            load_weights(k, sp, "even_mix")

        @block.tensor
        def _(pe):
            for i in range(2 * RH):
                src = rq if i % 2 == 0 else rk
                for m in range(NT):
                    t = pe.transpose(k.ps[:, i, m * P:(m + 1) * P], src[:, m, (i // 2) * P:(i // 2 + 1) * P], k.ident)
                t.then_inc(turned, 1)
            pe.wait_ge(copied_a, RH)
            pe.wait_ge(copied_v, RH)
            for h in range(RH + 1):
                if h < RH:
                    for kt in range(NT):
                        if h:
                            pe.wait_ge(decayed, NT * (h - 1) + kt + 1)
                        pe.matmul(k.ps[:, kt, kt * P:S], rkT[:, h, kt * P:(kt + 1) * P], rqT[:, h, kt * P:S],
                                  start=True, stop=True).then_inc(scored, 1)
                if h:
                    g = h - 1
                    pe.wait_ge(decayed, NT * (g + 1))
                    if g >= 2:
                        pe.wait_ge(ln_out, g - 1)
                    for t in range(NT):
                        bank = 4 + 2 * (g % 2) + t // 2
                        o = (t % 2) * RDV
                        for kt in range(t + 1):
                            mm = pe.matmul(k.ps[:, bank, o:o + RDV], att[:, g % 2, kt, t * P:(t + 1) * P],
                                           rv[:, kt, g * RDV:(g + 1) * RDV], start=kt == 0, stop=kt == t)
                    mm.then_inc(mixed, 1)
            pe.wait_ge(ln_out, RH)
            pe.wait_ge(tab, 16 * 4)
            for g in range(N_WIN):
                for c in range(2):
                    i = 2 * g + c
                    if i >= 2:
                        pe.wait_ge(pooled_by, i - 1)
                    for t in range(NT):
                        o = k.ps[0:PH, i % 2, t * P:(t + 1) * P]
                        ch = slice(i * PH, (i + 1) * PH)
                        if t:
                            pe.matmul(o, za[:, t - 1, ch], band[:, 3 * g + 2, :], start=True, stop=False)
                        mm = pe.matmul(o, za[:, t, ch], band[:, 3 * g + (t > 0), :], start=t == 0, stop=True)
                    mm.then_inc(pool_in, 1)
                for t in range(NT):
                    u = NT * g + t
                    pe.wait_ge(pooled_by, 2 * g + 2)
                    if u >= 4:
                        pe.wait_ge(pool_out, u - 3)
                    for c in range(2):
                        mm = pe.matmul(k.ps[:, 2 + u % 4, 0:PG], pooled[g % 2][0:PH, c, t * P:(t + 1) * P],
                                       pool_w[0:PH, g, c, :], start=c == 0, stop=c == 1)
                    mm.then_inc(pool_mm, 1)
            pe.wait_ge(pool_out, N_WIN * NT)
            ma.tensor(pe)

        @block.scalar
        def _(act):
            for h in range(RH):
                act.wait_ge(turned, 2 * h + 1)
                act.copy(rqT[:, h, :], k.ps[:, 2 * h, :]).then_inc(copied_a, 1)
            for h in range(RH):
                act.wait_ge(ln_in, h + 1)
                act.activation(sd[:, h % 2, :, 1], sd[:, h % 2, :, 0], ACT.Sqrt).then_inc(ln_root, 1)
            for i in range(2 * N_WIN):
                act.wait_ge(pool_in, i + 1)
                if i >= 4:
                    act.wait_ge(pool_mm, NT * (i // 2 - 1))
                act.copy(pooled[(i // 2) % 2][0:PH, i % 2, :], k.ps[0:PH, i % 2, :]).then_inc(pooled_by, 1)
            ma.scalar(act)

        @block.vector
        def _(dve):
            for h in range(RH):
                dve.wait_ge(turned, 2 * h + 2)
                dve.tensor_copy(rkT[:, h, :], k.ps[:, 2 * h + 1, :]).then_inc(copied_v, 1)
            dve.wait_ge(tab, 16 * 4)
            dve.wait_ge(turned, 2 * RH)
            for h in range(RH + 1):
                if h < RH:
                    for kt in range(NT):
                        dve.wait_ge(scored, NT * h + kt + 1)
                        if h >= 2 and kt == 0:
                            dve.wait_ge(mixed, h - 1)
                        dve.tensor_tensor(att[:, h % 2, kt, kt * P:S], k.ps[:, kt, kt * P:S],
                                          decay[:, h, 0:S - kt * P], ALU.mult).then_inc(decayed, 1)
                if h:
                    g = h - 1
                    dve.wait_ge(mixed, h)
                    o = [k.ps[:, 4 + 2 * (g % 2) + t // 2, (t % 2) * RDV:(t % 2 + 1) * RDV] for t in range(NT)]
                    for t in range(NT):
                        ins = dve.bn_stats(bn[:, g % 2, t, :], o[t])
                    k.link(dve, ins)
                    for t in range(NT):
                        ins = dve.bn_aggr(mv[:, g % 2, t, :], bn[:, g % 2, t, :])
                    k.link(dve, ins)
                    dve.tensor_scalar(sd[:, g % 2, :, 0], mv[:, g % 2, :, 1], EPS, None, ALU.add).then_inc(ln_in, 1)
                    dve.wait_ge(ln_root, g + 1)
                    k.link(dve, dve.reciprocal(sd[:, g % 2, :, 2], sd[:, g % 2, :, 1]))
                    for t in range(NT):
                        ys = y[:, t, POOL_W + g * RDV:POOL_W + (g + 1) * RDV]
                        k.link(dve, dve.tensor_scalar(ln[:, t % 2, :], o[t], mv[:, g % 2, t, 0:1],
                                                      sd[:, g % 2, t, 2:3], ALU.subtract, ALU.mult))
                        ins = dve.tensor_tensor(ys, ys, ln[:, t % 2, :], ALU.mult)
                        if t < NT - 1:
                            k.link(dve, ins)
                    ins.then_inc(ln_out, 1)
                    dve.wait_ge(ln_out, g + 1)
            for g in range(N_WIN):
                for t in range(NT):
                    u = NT * g + t
                    dve.wait_ge(pool_mm, u + 1)
                    if u >= 2:
                        dve.wait_ge(pool_out, u - 1)
                    ys = y[:, t, g * PG:(g + 1) * PG]
                    k.link(dve, dve.tensor_tensor(ptmp[:, u % 2, :], k.ps[:, 2 + u % 4, 0:PG],
                                                  pscale[:, g * PG:(g + 1) * PG], ALU.mult))
                    dve.tensor_tensor(ys, ys, ptmp[:, u % 2, :], ALU.mult).then_inc(pool_out, 1)
            ma.vector(dve)



def out_projection(k, name, w_out, h_dram, spill):
    nc = k.nc
    y = view(k, Y0, NT, D_IN)
    parts = (k.u_parts, k.u_parts2)
    h = view(k, H0, NT, D)
    turned, high, low, loaded, added, spilled = (
        k.sem(f"{name}_{n}") for n in ("turned", "y_high", "y_low", "h_loaded", "added", "spilled"))
    table = [("h", PIECE * (n // 2), PIECE, False) for n in range(2 * D // PIECE)]
    pr = SplitProjection(k, name, table, w_out)

    def turned_bank(kk):
        return kk if kk < 8 else 4 + kk % 4

    def sum_bank(g):
        return 4 * (g.n // 2 % 2) + g.t

    with nc.Block() as block:
        @block.sync
        def _(sp):
            pr.sync(sp)
            if spill is not None:
                sp.wait_ge(added, NT * D // PIECE)
                sp.dma_start(spill.rearrange("(m p) n -> p m n", p=P), h).then_inc(spilled, 16)
                sp.wait_ge(spilled, 16)

        @block.gpsimd
        def _(pool):
            pool.dma_start(h, h_dram.rearrange("(m p) n -> p m n", p=P)).then_inc(loaded, 16)

        @block.tensor
        def _(pe):
            for kk in range(KI):
                if kk >= 8:
                    pe.wait_ge(low, kk - 3)
                for m in range(NT):
                    t = pe.transpose(k.ps[:, turned_bank(kk), m * P:(m + 1) * P], y[:, m, kk * P:(kk + 1) * P],
                                     k.ident)
                t.then_inc(turned, 1)
            for g in pr.groups:
                half, c = g.n % 2, g.n // 2
                if g.t == 0:
                    pe.wait_ge(pr.low, g.n + 1)
                    if c == 0:
                        pe.wait_ge(low, KD * (half + 1))
                if half == 0 and c >= 2:
                    pe.wait_ge(added, NT * (c - 2) + g.t + 1)
                w = [pr.part(g.n, i) for i in range(2)]
                for kk in range(KD):
                    for x, z in ((0, 0), (0, 1), (1, 0)):
                        mm = pe.matmul(k.ps[:, sum_bank(g), 0:PIECE], parts[half][:, x, kk, g.t * P:(g.t + 1) * P],
                                       w[z][:, kk, :], start=half == 0 and kk == 0 and x + z == 0,
                                       stop=half == 1 and kk == KD - 1 and x == 1)
                mm.then_inc(pr.group_done, 1)

        @block.scalar
        def _(act):
            for kk in range(KI):
                act.wait_ge(turned, kk + 1)
                act.copy(parts[kk // KD][:, 0, kk % KD, :], k.ps[:, turned_bank(kk), :]).then_inc(high, 1)
                if kk in (KD - 1, KI - 1):
                    pr.scalar_split(act, kk // KD)
            for n in range(2, len(table)):
                pr.scalar_split(act, n)

        @block.vector
        def _(dve):
            for kk in range(KI):
                dve.wait_ge(high, kk + 1)
                dve.tensor_tensor(parts[kk // KD][:, 1, kk % KD, :], k.ps[:, turned_bank(kk), :],
                                  parts[kk // KD][:, 0, kk % KD, :].bitcast(F32), ALU.subtract).then_inc(low, 1)
                if kk in (KD - 1, KI - 1):
                    pr.vector_split(dve, kk // KD)
            dve.wait_ge(loaded, 16)
            for g in pr.groups:
                if g.t == 0 and g.n:
                    pr.vector_split(dve, g.n + 1)
                if g.n % 2:
                    pr.wait_group(dve, g)
                    c = g.n // 2
                    hs = h[:, g.t, PIECE * c:PIECE * (c + 1)]
                    dve.tensor_tensor(hs, hs, k.ps[:, sum_bank(g), 0:PIECE], ALU.add).then_inc(added, 1)



def odd_in(k):
    nc, d = k.nc, k.d
    h = view(k, H0, NT, D)
    squares = view(k, Z0, D)
    y = view(k, Y0, NT, D_IN)
    k.kc2 = view(k, H0, 2, 2, NKV, S)
    k.qT = view(k, Z0, NH, S)
    k.ksT, k.kwT = view(k, Z0 + 6144, NKV, S), view(k, Z0 + 7168, NKV, S)
    k.xqT = view(k, Z0 + 8192, MH, S)
    k.vs, k.vw = view(k, Z0 + 13312, NT, 256), view(k, Z0 + 14336, NT, 256)
    k.gsig = view(k, Z0 + 15360, NT, 36)
    pe_nat = view(k, Z0 + 15504, DH)
    k.posT = view(k, Z0 + 15632, 2, 2, 16)
    from31 = view(k, Z0 + 15696, 1)
    norm = Norm(k, "norm_odd", h, NT, gT=k.g_odd, scratch=squares, stat=0)
    pr = SplitProjection(k, "odd", ODD_IN, d["od_w_in"][0], ("gate", "gl"))
    small, posed, posed_out = k.sem("odd_small"), k.sem("odd_positions"), k.sem("odd_positions_copied")

    with nc.Block() as block:
        @block.sync
        def _(sp):
            sp.dma_start(pe_nat[0:64, :], d["od_cmp_pe"][0].rearrange("a l d -> (a l) d")).then_inc(small, 16)
            sp.dma_start(from31, d["from31"]).then_inc(small, 16)
            pr.sync(sp)

        @block.tensor
        def _(pe):
            norm.tensor_turn(pe)
            pe.wait_ge(norm.low, KD)
            pe.wait_ge(small, 32)
            pe.transpose(k.ps[:, 7, 0:64], pe_nat[0:64, :], k.ident[0:64, 0:64]).then_inc(posed, 1)
            pe.wait_ge(posed_out, 1)
            pr.tensor(pe)

        @block.scalar
        def _(act):
            norm.scalar_sums(act)
            norm.scalar_root(act)
            norm.scalar_high(act)
            pr.scalar_split(act, 0)
            for g in pr.groups:
                if g.t == 0:
                    pr.scalar_split(act, g.n + 1)
                if g.evac != "act":
                    continue
                pr.wait_group(act, g)
                bank = k.ps[:, g.bank, 0:g.width]
                if g.what == "gl":
                    ins = act.activation(k.gsig[:, g.t, :], bank, ACT.Sigmoid)
                else:
                    ins = act.activation(y[:, g.t, g.col:g.col + g.width], bank, ACT.Silu)
                ins.then_inc(pr.emptied["act"], 1)

        @block.vector
        def _(dve):
            norm.vector_mean(dve)
            norm.vector_scale(dve)
            norm.vector_low(dve)
            dve.wait_ge(posed, 1)
            dve.tensor_copy(k.posT, k.ps[:, 7, 0:64].rearrange("p (a b c) -> p a b c", a=2, b=2)).then_inc(posed_out, 1)
            dve.wait_ge(posed_out, 1)
            pr.vector_split(dve, 0)
            for g in pr.groups:
                if g.t == 0:
                    pr.vector_split(dve, g.n + 1)
                if g.evac != "dve":
                    continue
                pr.wait_group(dve, g)
                bank = k.ps[:, g.bank, 0:S if g.turned else g.width]
                if g.what == "q":
                    ins = dve.tensor_scalar(k.qT[:, g.col // P + g.t, :], bank, -(DH ** -0.5), None, ALU.mult)
                elif g.what == "xq":
                    ins = dve.tensor_scalar(k.xqT[:, g.col // P + g.t, :], bank, -(MDH ** -0.5), None, ALU.mult)
                elif g.what == "kcvc":
                    for half in range(2):
                        dst = k.kc2[:, g.col // PIECE, half, g.t, :].rearrange("p (j l) -> p j l", l=16)
                        ins = dve.tensor_tensor(dst, bank.rearrange("p (j l) -> p j l", l=16),
                                                spread(k.posT[:, g.col // PIECE, half, :], 1, S // 16), ALU.add)
                elif g.turned:
                    ins = dve.tensor_copy({"ks": k.ksT, "kw": k.kwT}[g.what][:, g.t, :], bank)
                else:
                    ins = dve.tensor_copy({"vs": k.vs, "vw": k.vw}[g.what][:, g.t, :], bank)
                ins.then_inc(pr.emptied["dve"], 1)



def compress(k):
    nc, d = k.nc, k.d
    w2 = view(k, U0, 2, 2, DH)
    b1 = view(k, U0 + 512, 2, 2)
    hid = view(k, U0 + 516, 2, 2, NKV * NCMP)
    k.kcmpT = view(k, Z0 + 10240, NKV, NCMP)
    k.vcmp = view(k, Z0 + 10302, NKV, DH)
    table = view(k, U0 + 1024, NH)
    hot = view(k, U0 + 1040, 2048)
    tab = view(k, U0 + 3088, 2048)
    first = first_chunk(k, "compress")
    small, masked, hid_done, hid_out, k_done, k_out, t_done, t_out = (
        k.sem("cmp_" + n) for n in ("small", "mask_row", "hidden", "silu", "second", "copied", "biased", "negated"))
    k.bias_stored = k.lasting_sem("bias_stored")

    with nc.Block() as block:
        @block.sync
        def _(sp):
            for kv in range(2):
                sp.dma_start(w2[:, kv, :, :], d["od_cmp_w2"][0, kv].rearrange("(h p) n -> p h n", p=P)).then_inc(small, 16)
                with nc.allow_non_contiguous_dma(reason="512 biases, one per partition"):
                    for ht in range(2):
                        sp.dma_start(b1[:, kv, ht:ht + 1], d["od_cmp_b1"][0, kv, ht * P:(ht + 1) * P]
                                     .rearrange("(p a) -> p a", a=1)).then_inc(small, 16)
            sp.dma_start(table[0:NBUCKET, :], d["rel_bias"]).then_inc(small, 16)
            sp.dma_start(hot[0:NBUCKET + 1, :], d["hot"]).then_inc(small, 16)
            load_weights(k, sp, "compress")
            sp.wait_ge(t_out, 4)
            sp.dma_start(k.bias_dram, tab[0:NH, :]).then_inc(k.bias_stored, 16)
            sp.wait_ge(k.bias_stored, 16)

        @block.tensor
        def _(pe):
            pe.wait_ge(small, 16 * 8)
            pe.wait_ge(masked, 1)
            for c in range(4):
                pe.matmul(k.ps[0:NH, 4 + c, :], table[0:NBUCKET + 1, :], hot[0:NBUCKET + 1, 512 * c:512 * c + 512],
                          start=True, stop=True).then_inc(t_done, 1)
            for kv in range(2):
                for half in range(2):
                    c = first + 2 * kv + half
                    wait_chunk(k, pe, c)
                    w = view(k, k.slot(c), 16, CMP_HID)
                    for ht in range(2):
                        for l in range(16):
                            src = k.kc2[:, kv, half, :, 16 * half + l:16 * half + l + 16 * (NCMP - 1) + 1:16]
                            mm = pe.matmul(k.ps[:, 2 * kv + ht, 0:NKV * NCMP], w[:, l, ht * P:(ht + 1) * P], src,
                                           start=half == 0 and l == 0, stop=half == 1 and l == 15)
                        if half == 1 and ht == 0:
                            mm.then_inc(hid_done, 1)
                    mm.then_inc(k.chunk_used, 1)
            pe.wait_ge(t_out, 4)
            pe.wait_ge(hid_out, 4)
            for ht in range(2):
                mm = pe.matmul(k.ps[:, 4, 0:NKV * NCMP], w2[:, 0, ht, :], hid[:, 0, ht, :], start=ht == 0, stop=ht == 1)
            mm.then_inc(k_done, 1)
            for g in range(NKV):
                for ht in range(2):
                    mm = pe.matmul(k.ps[0:NCMP, 5 + g, 0:DH], hid[:, 1, ht, g * NCMP:(g + 1) * NCMP], w2[:, 1, ht, :],
                                   start=ht == 0, stop=ht == 1)
                mm.then_inc(k_done, 1)

        @block.scalar
        def _(act):
            act.wait_ge(small, 16 * 8)
            for kv in range(2):
                for ht in range(2):
                    if ht == 0:
                        act.wait_ge(hid_done, kv + 1)
                    else:
                        act.wait_ge(k.chunk_used, first + 2 * kv + 2)
                    act.activation(hid[:, kv, ht, :], k.ps[:, 2 * kv + ht, 0:NKV * NCMP], ACT.Silu,
                                   bias=b1[:, kv, ht:ht + 1]).then_inc(hid_out, 1)

        @block.vector
        def _(dve):
            dve.memset(table[NBUCKET:NBUCKET + 1, :], -BIG).then_inc(masked, 1)
            for c in range(4):
                dve.wait_ge(t_done, c + 1)
                dve.tensor_scalar(tab[0:NH, 512 * c:512 * c + 512], k.ps[0:NH, 4 + c, :], -1.0, None,
                                  ALU.mult).then_inc(t_out, 1)
            k.link(dve, dve.tensor_scalar(k.gsig[:, 0, 0:NH], k.gsig[:, 0, 0:NH], view(k, Z0 + 15696, 1)[:, 0:1], None,
                                          ALU.mult))
            dve.wait_ge(k_done, 1)
            dve.tensor_copy(k.kcmpT, k.ps[:, 4, 0:NKV * NCMP].rearrange("p (g j) -> p g j", g=NKV)).then_inc(k_out, 1)
            for g in range(NKV):
                dve.wait_ge(k_done, g + 2)
                dve.tensor_copy(k.vcmp[0:NCMP, g, :], k.ps[0:NCMP, 5 + g, 0:DH]).then_inc(k_out, 1)



def nsa(k):
    nc = k.nc
    bias_n = view(k, U0, 2, 512)
    pc = view(k, U0 + 1024, NH, NT, NCMP)
    sc = [view(k, o, 2, 512) for o in (U0 + 2512, U0 + 3536, H0)]
    pT = [view(k, U0 + 4560 + 1152 * i, 1152) for i in range(2)]
    acc = view(k, U0 + 6864, 2, P)
    st = view(k, H0 + 1024, 4, 4, 2)
    c_low, c_sum, c_inv = (view(k, U0 + 7136 + 48 * i, NH, NT) for i in range(3))
    y = view(k, Y0, NT, D_IN)
    ma = MemAttention(k, "mem_o", 1, k.xqT, k.misc, k.misc + 1536)
    steps = [(h, t) for h in range(NH) for t in range(NT)]
    n = len(steps)
    bc, c_scored, c_biased, c_shifted, c_exped, c_ready = (
        k.sem("cmp_att_" + x) for x in ("bias_loaded", "scored", "biased", "shifted", "exped", "ready"))
    scored, low, exped, turned, cop_a, cop_v, mixed, stored = (
        k.sem("nsa_" + x) for x in ("scored", "low", "exped", "turned", "copied_act", "copied_dve", "mixed", "stored"))
    bias_loaded = [k.sem(f"nsa_bias{i}") for i in range(2)]

    with nc.Block() as block:
        @block.sync
        def _(sp):
            b = k.bias_dram
            for a in range(8):
                for t in range(NT):
                    src = bass.AP(b.tensor, 1024 + 33 - 8 * t - a, [[64, 16], [2048, NH], [1, NCMP]])
                    sp.dma_start(pc[16 * a:16 * a + 16, :, t, :], src).then_inc(bc, 16)
            for h in range(NH):
                if h >= 2:
                    sp.wait_ge(low, 2 * NT * (h - 1))
                src = bass.AP(b.tensor, 2048 * h + 512 - (P - 1), [[1, P], [1, 512]])
                sp.dma_start(bias_n[:, h % 2, :], src).then_inc(bias_loaded[h % 2], 16)
            load_weights(k, sp, "nsa")

        @block.tensor
        def _(pe):
            for h in range(NH):
                if h >= 8:
                    pe.wait_ge(c_biased, h - 7)
                for t in range(NT):
                    mm = pe.matmul(k.ps[:, h % 8, NCMP * t:NCMP * t + NCMP], k.qT[:, h, t * P:(t + 1) * P],
                                   k.kcmpT[:, h // HPG, :], start=True, stop=True)
                mm.then_inc(c_scored, 1)
            pe.wait_ge(c_biased, NH)
            for u in range(n + 3):
                if u < n:
                    h, t = steps[u]
                    g, m = h // HPG, (t + 1) * P
                    if u >= 2:
                        pe.wait_ge(low, 2 * (u - 1))
                    for i, kT in enumerate((k.ksT, k.kwT)):
                        pe.matmul(k.ps[:, 2 * (u % 2) + i, 0:m], k.qT[:, h, t * P:(t + 1) * P], kT[:, g, 0:m],
                                  start=True, stop=True).then_inc(scored, 1)
                if u >= 3:
                    v = u - 3
                    h, t = steps[v]
                    g = h // HPG
                    pe.wait_ge(cop_a, v + 1)
                    pe.wait_ge(cop_v, 2 * (v + 1))
                    o = k.ps[:, 6 + v % 2, :]
                    for i, vv in enumerate((k.vs, k.vw)):
                        for kt in range(t + 1):
                            pe.matmul(o[:, 128 * i:128 * i + 128], pT[v % 2][:, 512 * i + kt * P:512 * i + kt * P + P],
                                      vv[:, kt, g * DH:(g + 1) * DH], start=kt == 0, stop=kt == t)
                    pe.matmul(o[:, 256:384], pT[v % 2][0:NCMP, 1024:1152], k.vcmp[0:NCMP, g, :], start=True,
                              stop=True).then_inc(mixed, 1)
                if 2 <= u < n + 2:
                    v = u - 2
                    h, t = steps[v]
                    if v == 0:
                        pe.wait_ge(c_ready, 1)
                    if v >= 2:
                        pe.wait_ge(stored, v - 1)
                    pe.transpose(k.ps[0:NCMP, 6 + v % 2, 384:512], pc[:, h, t, :], k.ident).then_inc(turned, 1)
                    for i in range(2):
                        pe.wait_ge(exped, 2 * v + 1 + i)
                        if v:
                            pe.wait_ge(cop_v if i else cop_a, 2 * v if i else v)
                        for kt in range(t + 1):
                            tr = pe.transpose(k.ps[:, 4 + i, kt * P:(kt + 1) * P],
                                              sc[v % 3][:, i, kt * P:(kt + 1) * P], k.ident)
                        tr.then_inc(turned, 1)
            pe.wait_ge(stored, n)
            ma.tensor(pe)

        @block.scalar
        def _(act):
            act.wait_ge(c_shifted, 1)
            act.activation(pc, pc, ACT.Exp, scale=-1.0).then_inc(c_exped, 1)
            for u in range(n + 2):
                if u < n:
                    w = (steps[u][1] + 1) * P
                    for b in range(2):
                        act.wait_ge(low, 2 * u + b + 1)
                        if u >= 4 and b == 0:
                            act.wait_ge(stored, u - 3)
                        x = sc[u % 3][:, b, 0:w]
                        act.activation(x, x, ACT.Exp, scale=-1.0, bias=st[:, u % 4, 0, b:b + 1],
                                       accum_out=st[:, u % 4, 1, b:b + 1]).then_inc(exped, 1)
                if u >= 2:
                    v = u - 2
                    w = (steps[v][1] + 1) * P
                    act.wait_ge(turned, 3 * v + 2)
                    if v >= 2:
                        act.wait_ge(mixed, v - 1)
                    act.copy(pT[v % 2][:, 0:w], k.ps[:, 4, 0:w]).then_inc(cop_a, 1)
            ma.scalar(act)

        @block.vector
        def _(dve):
            dve.wait_ge(bc, 16 * 32)
            for h in range(NH):
                dve.wait_ge(c_scored, h + 1)
                dve.tensor_tensor(pc[:, h, :, :], pc[:, h, :, :],
                                  k.ps[:, h % 8, 0:NT * NCMP].rearrange("p (t j) -> p t j", t=NT),
                                  ALU.add).then_inc(c_biased, 1)
            dve.wait_ge(c_biased, NH)
            k.link(dve, dve.tensor_reduce(c_low, pc, AX_X, ALU.min))
            rows = pc.rearrange("p h t j -> p (h t) j")

            def by_row(x):
                return spread(x.rearrange("p h t -> p (h t)"), 2, NCMP)

            dve.tensor_tensor(rows, rows, by_row(c_low), ALU.subtract).then_inc(c_shifted, 1)
            dve.wait_ge(c_exped, 1)
            k.link(dve, dve.tensor_reduce(c_sum, pc, AX_X, ALU.add))
            k.link(dve, dve.reciprocal(c_inv, c_sum))
            k.link(dve, dve.tensor_tensor(c_low, c_inv, k.gsig[:, :, 0:NH].rearrange("p t h -> p h t"), ALU.mult))
            dve.tensor_tensor(rows, rows, by_row(c_low), ALU.mult).then_inc(c_ready, 1)
            for u in range(n + 3):
                if u < n:
                    h, t = steps[u]
                    if t == 0:
                        dve.wait_ge(bias_loaded[h % 2], 16 * (h // 2 + 1))
                    w = (t + 1) * P
                    for b in range(2):
                        dve.wait_ge(scored, 2 * u + b + 1)
                        if u >= 3:
                            dve.wait_ge(turned, 3 * (u - 3) + b + 2)
                        dve.tensor_tensor_reduce(sc[u % 3][:, b, 0:w], k.ps[:, 2 * (u % 2) + b, 0:w],
                                                 backwards(bias_n[:, h % 2, 0:w]), 1.0, 3e38, ALU.add, ALU.min,
                                                 st[:, u % 4, 0, b:b + 1]).then_inc(low, 1)
                if 2 <= u < n + 2:
                    v = u - 2
                    w = (steps[v][1] + 1) * P
                    if v >= 2:
                        dve.wait_ge(mixed, v - 1)
                    dve.wait_ge(turned, 3 * v + 1)
                    dve.tensor_copy(pT[v % 2][0:NCMP, 1024:1152], k.ps[0:NCMP, 6 + v % 2, 384:512]).then_inc(cop_v, 1)
                    dve.wait_ge(turned, 3 * v + 3)
                    dve.tensor_copy(pT[v % 2][:, 512:512 + w], k.ps[:, 5, 0:w]).then_inc(cop_v, 1)
                if u >= 3:
                    v = u - 3
                    h, t = steps[v]
                    s = st[:, v % 4, :, :]
                    k.link(dve, dve.reciprocal(s[:, 2, :], s[:, 1, :]))
                    k.link(dve, dve.tensor_tensor(s[:, 3, :], s[:, 2, :], k.gsig[:, t, NH + h:2 * NH + h + 1:NH],
                                                  ALU.mult))
                    dve.wait_ge(mixed, v + 1)
                    o = k.ps[:, 6 + v % 2, :]
                    ys = y[:, t, h * DH:(h + 1) * DH]
                    a = acc[:, v % 2, :]
                    k.link(dve, dve.tensor_scalar(a, o[:, 0:128], s[:, 3, 0:1], None, ALU.mult))
                    k.link(dve, dve.scalar_tensor_tensor(out=a, in0=o[:, 128:256], scalar=s[:, 3, 1:2], in1=a,
                                                         op0=ALU.mult, op1=ALU.add))
                    k.link(dve, dve.tensor_tensor(a, a, o[:, 256:384], ALU.add))
                    dve.tensor_tensor(ys, ys, a, ALU.mult).then_inc(stored, 1)
            ma.vector(dve)



def mix_in(k):
    nc, d = k.nc, k.d
    h = view(k, H0, NT, D)
    normed = view(k, Y0, NT, D)
    squares = view(k, Z0 + 4096, D)
    us = view(k, Z0, NT, 512)
    final_g = view(k, Z0 + 2048, D)
    k.ufT = view(k, Z0 + 15360, FG, S)
    y = view(k, Y0, NT, 2 * D)
    n1 = Norm(k, "norm_first_final", h, NT, scratch=squares, stat=0)
    n2 = Norm(k, "norm_mix", h, NT, gT=k.g_mix, scratch=squares, stat=16, dst=normed)
    pr = SplitProjection(k, "mix", MIX_IN, d["w_in_2"][0], ("gate",))
    g_loaded, scaled, x_stored, us_out, us_stored = (
        k.sem("mix_" + n) for n in ("gain_loaded", "x_ready", "x_stored", "us_ready", "us_stored"))

    with nc.Block() as block:
        @block.sync
        def _(sp):
            sp.dma_start(final_g, d["final_g"].rearrange("(a n) -> a n", a=1).to_broadcast([P, D])).then_inc(g_loaded, 16)
            pr.sync(sp)

        @block.gpsimd
        def _(pool):
            pool.wait_ge(scaled, NT)
            pool.dma_start(k.h_dram[1].rearrange("(m p) n -> p m n", p=P), h).then_inc(x_stored, 16)
            pool.wait_ge(pr.emptied["dve"], 2 * NT)
            pool.dma_start(k.us_dram.rearrange("(m p) n -> p m n", p=P), us).then_inc(us_stored, 16)
            pool.wait_ge(x_stored, 16)
            pool.wait_ge(us_stored, 16)

        @block.tensor
        def _(pe):
            n2.tensor_turn(pe)
            pe.wait_ge(n2.low, KD)
            pr.tensor(pe)

        @block.scalar
        def _(act):
            n1.scalar_sums(act)
            n1.scalar_root(act)
            act.wait_ge(scaled, NT)
            n2.scalar_sums(act)
            n2.scalar_root(act)
            n2.scalar_high(act)
            pr.scalar_split(act, 0)
            for g in pr.groups:
                if g.t == 0:
                    pr.scalar_split(act, g.n + 1)
                if g.evac == "act":
                    pr.wait_group(act, g)
                    act.activation(y[:, g.t, g.col:g.col + g.width], k.ps[:, g.bank, 0:g.width],
                                   ACT.Sigmoid).then_inc(pr.emptied["act"], 1)

        @block.vector
        def _(dve):
            n1.vector_mean(dve)
            n1.vector_scale(dve)
            dve.wait_ge(n1.normed, NT)
            dve.wait_ge(g_loaded, 16)
            for m in range(NT):
                dve.tensor_tensor(h[:, m, :], h[:, m, :], final_g, ALU.mult).then_inc(scaled, 1)
            dve.wait_ge(scaled, NT)
            n2.vector_mean(dve)
            n2.vector_scale(dve)
            n2.vector_low(dve)
            pr.vector_split(dve, 0)
            for g in pr.groups:
                if g.t == 0:
                    pr.vector_split(dve, g.n + 1)
                if g.evac == "dve":
                    pr.wait_group(dve, g)
                    dst = k.ufT[:, g.col // P + g.t, :] if g.turned else us[:, g.t, g.col:g.col + g.width]
                    dve.tensor_copy(dst, k.ps[:, g.bank, 0:S if g.turned else g.width]).then_inc(pr.emptied["dve"], 1)



TWO_PI_HI = 6.28125
TWO_PI_LO = 0.0019353071795864769
ROUND = 12582912.0


def ssm(k):
    nc, d = k.nc, k.d
    A = U0 + 11264
    V = view(k, U0, 2 * 2, GP, (L + 1) * SC)
    Bb = view(k, U0 + 9216, 2, 2 * GP, SC)
    u2 = view(k, H0, L, SG, SC)
    u2g = view(k, U0, SG, L, SC)
    tmpB = view(k, A, 2 * GP, SC)
    CT = view(k, k.misc, 2, 2 * GP, SC)
    tmpV = view(k, k.misc + 1024, GP // 4, L + 1, SC)
    Br = view(k, A + 3328, 2, 2 * GP, SC)
    Cn = view(k, A + 4352, 4, 4, 2, SN)
    X = view(k, A, 2, GP, P)
    tmpX = view(k, A + 4096, GP, L, SC)
    W1 = view(k, A + 4096, GP, 2, P)
    E = view(k, A, 2, GP, NCH)
    SH = view(k, A + 2048, 2, GP, NCH)
    tmpS = view(k, A + 4096, GP, NCH)
    R = view(k, A + 5120, GP, NCH)
    T = view(k, A, SG, P)
    KK = [view(k, A + 4096 + 1920 * i, 8, 15, SC) for i in range(2)]
    ysb = view(k, A + 4096, L, 512)
    Uc = view(k, U0 + 19456, SG, NCH)
    Hs = view(k, H0, 2 * 2, GP, NCH)
    PA = view(k, U0 + 21504, 2, 2 * GP, L + 1)
    PD = view(k, U0 + 22080, 2, 2 * GP, L + 1)
    pt = view(k, U0 + 22656, 7, 2 * GP)
    zz = view(k, U0 + 22880, 4, 2 * GP)
    tmp32 = view(k, U0 + 23008, 2 * GP)
    tmp128 = view(k, U0 + 23040, 2 * GP * 4)
    dT = view(k, U0 + 23168, SG)
    eye = view(k, C0, P)
    par = view(k, k.misc, 16, P)
    ldt = view(k, k.misc + 2048, 2)
    dD = view(k, k.misc + 2056, SG, SC)
    (raw, c_raw, u_raw, dt_ok, ang_ok, trig_ok, par_ok, par_T, cT, cT_out, u_T, u_out, x_ok, x_T, w_out, s_ok, h_ok,
     k_mm, kk_ok, t_ok, y_mm, y_a, y_v, y_st, u_by_g, powers, v_ok) = (
        k.sem("ssm_" + n) for n in
        ("params_loaded", "c_loaded", "u_loaded", "dt", "angles", "trig", "params", "params_turned", "c_turned",
         "c_copied", "u_turned", "u_copied", "x_ready", "x_turned", "w_copied", "s_done", "states", "k_done",
         "k_copied", "t_loaded", "y_done", "y_copied_act", "y_copied_dve", "y_stored", "u_by_group",
         "powers", "v_ready"))
    v_step = Counter(k.sem("ssm_v_step"))

    def y_bank(b):
        v = ysb[0:NCH].rearrange("p i (q a c) -> p i q a c", a=2, c=SC)
        return v[:, :, 4 * (b % 4):4 * (b % 4) + 4, b // 4, :]

    def cmul(dve, o_re, o_im, a_re, a_im, b_re, b_im, tmp):
        dve.tensor_tensor(o_re, a_re, b_re, ALU.mult)
        k.link(dve, dve.tensor_tensor(tmp, a_im, b_im, ALU.mult))
        k.link(dve, dve.tensor_tensor(o_re, o_re, tmp, ALU.subtract))
        dve.tensor_tensor(o_im, a_re, b_im, ALU.mult)
        k.link(dve, dve.tensor_tensor(tmp, a_im, b_re, ALU.mult))
        k.link(dve, dve.tensor_tensor(o_im, o_im, tmp, ALU.add))

    with nc.Block() as block:
        @block.gpsimd
        def _(pool):
            pool.wait_ge(u_raw, 16)
            for b in range(4):
                pool.tensor_copy(u2g[0:NCH, 8 * b:8 * b + 8, :, :],
                                 u2[0:NCH, :, 8 * b:8 * b + 8, :].rearrange("p j g c -> p g j c")).then_inc(u_by_g, 1)
            pool.wait_ge(powers, 1)
            pool.wait_ge(cT_out, 4)
            pool.wait_ge(u_T, 4)
            for dr in range(2):
                pw = (PA, PD)[dr]
                for q4 in range(4):
                    q = slice(GP * dr + 4 * q4, GP * dr + 4 * q4 + 4)
                    o_re, o_im = (V[:, 2 * dr + ri, 4 * q4:4 * q4 + 4, :].rearrange("p q (s c) -> p q s c", c=SC)
                                  for ri in range(2))
                    a_re, a_im = (spread(pw[:, ri, q, :], 3, SC) for ri in range(2))
                    c_re, c_mi = (spread(CT[:, ri, q, :], 2, L + 1) for ri in range(2))
                    pool.tensor_tensor(o_re, a_re, c_re, ALU.mult)
                    k.link(pool, pool.tensor_tensor(tmpV, a_im, c_mi, ALU.mult), v_step)
                    k.link(pool, pool.tensor_tensor(o_re, o_re, tmpV, ALU.add), v_step)
                    pool.tensor_tensor(o_im, a_re, c_mi, ALU.mult)
                    k.link(pool, pool.tensor_tensor(tmpV, a_im, c_re, ALU.mult), v_step)
                    k.link(pool, pool.tensor_tensor(o_im, o_im, tmpV, ALU.subtract), v_step)
            pool.sem_inc(v_ok, 1)

        @block.sync
        def _(sp):
            q = 2 * GP
            sp.dma_start(par[0:q, 0, :], d["ssm_A_re_2"][0].rearrange("d (q a) n -> (d q) (a n)", a=2)).then_inc(raw, 16)
            sp.dma_start(par[0:q, 1, :], d["ssm_A_im_2"][0].rearrange("d (q a) n -> (d q) (a n)", a=2)).then_inc(raw, 16)
            sp.dma_start(ldt[0:q, :], d["ssm_log_dt_2"][0].rearrange("d (q a) -> (d q) a", a=2)).then_inc(raw, 16)
            sp.dma_start(view(k, H0, S * L)[0:NCH], k.us_dram.rearrange("(c j) n -> c (j n)", j=L)).then_inc(u_raw, 16)
            with nc.allow_non_contiguous_dma(reason="512 skips, channel by group"):
                sp.dma_start(dT[0:SC, :], d["ssm_D_2"][0].rearrange("(g c) -> c g", c=SC)).then_inc(c_raw, 16)
            for i, n in enumerate(("ssm_C_re_2", "ssm_C_im_2")):
                for dr in range(2):
                    for twice in range(2):
                        sp.dma_start(Cn[:, 2 * i + dr, :, twice, :],
                                     d[n][0, dr].rearrange("(t g) c n -> (g c) t n", t=4)).then_inc(c_raw, 16)
            for i, n in enumerate(("ssm_B_re_2", "ssm_B_im_2")):
                sp.dma_start(Br[:, i, :, :], d[n][0].rearrange("d (q a) n c -> (a n) (d q) c", a=2)).then_inc(c_raw, 16)
            load_weights(k, sp, "ssm")
            for b in range(4):
                sp.wait_ge(kk_ok, b + 1)
                for j in range(L):
                    sp.dma_start(T[SC * j:SC * (j + 1), 8 * b:8 * b + 8, :],
                                 KK[b % 2][0:SC, :, L - 1 - j:2 * L - 1 - j, :]
                                 .rearrange("p g s c -> p g (s c)")).then_inc(t_ok, 16)
            sp.wait_ge(y_a, 4)
            sp.wait_ge(y_v, 4)
            sp.dma_start(k.ys_dram.rearrange("(c j) n -> c j n", j=L), ysb[0:NCH]).then_inc(y_st, 16)
            sp.wait_ge(y_st, 16)

        @block.tensor
        def _(pe):
            for g in range(SG):
                if g % 8 == 0:
                    pe.wait_ge(u_by_g, g // 8 + 1)
                t = pe.transpose(k.ps[:, g // 8, NCH * (g % 8):NCH * (g % 8 + 1)],
                                 u2g[0:NCH, g, :, :].rearrange("p j c -> p (j c)"), k.ident[0:NCH, 0:NCH])
                if g % 8 == 7:
                    t.then_inc(u_T, 1)
            pe.wait_ge(c_raw, 16 * 11)
            for i in range(4):
                for t4 in range(4):
                    t = pe.transpose(k.ps[:, 4 + i, P * t4:P * (t4 + 1)],
                                     Cn[:, i, t4, :, :].rearrange("p a n -> p (a n)"), k.ident)
                t.then_inc(cT, 1)
            pe.wait_ge(par_ok, 1)
            pe.wait_ge(u_out, 4)
            for i in range(7):
                t = pe.transpose(k.ps[:, 0, 32 * i:32 * (i + 1)], par[0:2 * GP, i + 2, :], k.ident[0:32, 0:32])
            t.then_inc(par_T, 1)
            for dr in range(2):
                pe.wait_ge(x_ok, dr + 1)
                if dr == 0:
                    pe.wait_ge(cT_out, 4)
                for i in range(8):
                    if i >= 4 or dr:
                        pe.wait_ge(w_out, 8 * dr + i - 3)
                    for a in range(2):
                        for ri in range(2):
                            t = pe.transpose(k.ps[:, 4 + i % 4, P * (2 * a + ri):P * (2 * a + ri + 1)],
                                             X[:, ri, 2 * i + a, :], k.ident)
                    t.then_inc(x_T, 1)
                pe.wait_ge(w_out, 8 * (dr + 1))
                if dr:
                    pe.wait_ge(h_ok, 1)
                for ri in range(2):
                    for q in range(GP):
                        for a in range(2):
                            mm = pe.matmul(k.ps[SN * a:SN * (a + 1), 2 * ri + q // 8, NCH * (q % 8):NCH * (q % 8 + 1)],
                                           W1[:, q, ri, SN * a:SN * (a + 1)], Uc[:, 2 * q + a, :], start=True, stop=True)
                mm.then_inc(s_ok, 1)
            pe.wait_ge(h_ok, 2)
            pe.wait_ge(v_ok, 1)
            for b in range(4):
                if b >= 2:
                    pe.wait_ge(kk_ok, b - 1)
                for dr in range(2):
                    for g8 in range(8):
                        g = 8 * b + g8
                        q, a = g // 2, g % 2
                        half = slice(SN * a, SN * (a + 1))
                        for ri in range(2):
                            mm = pe.matmul(k.ps[0:SC, 4 * (b % 2) + 2 * dr + a, P * (g8 // 2):P * (g8 // 2 + 1)],
                                           Bb[half, ri, GP * dr + q, :],
                                           V[half, 2 * dr + ri, q, SC * dr:SC * dr + P], start=ri == 0, stop=ri == 1)
                mm.then_inc(k_mm, 1)
            pe.wait_ge(t_ok, 16 * L * 4)
            pe.wait_ge(kk_ok, 4)
            for i in range(SG):
                a, q = i // GP, i % GP
                g = 2 * q + a
                half = slice(SN * a, SN * (a + 1))
                o = k.ps[0:NCH, i // 4, P * (i % 4):P * (i % 4 + 1)]
                pe.matmul(o, Uc[:, g, :], T[:, g, :], start=True, stop=False)
                for dr in range(2):
                    v0 = SC * (1 - dr)
                    for ri in range(2):
                        mm = pe.matmul(o, Hs[half, 2 * dr + ri, q, :], V[half, 2 * dr + ri, q, v0:v0 + P], start=False,
                                       stop=dr == 1 and ri == 1)
                if i % 4 == 3:
                    mm.then_inc(y_mm, 1)

        @block.scalar
        def _(act):
            act.wait_ge(raw, 48)
            act.activation(ldt[0:32, :], ldt[0:32, :], ACT.Exp).then_inc(dt_ok, 1)
            act.wait_ge(ang_ok, 1)
            act.activation(par[0:32, 8, :], par[0:32, 9, :], ACT.Exp).then_inc(trig_ok, 1)
            act.activation(par[0:32, 7, :], par[0:32, 10, :], ACT.Sin).then_inc(trig_ok, 1)
            act.activation(par[0:32, 12, :], par[0:32, 11, :], ACT.Sin).then_inc(trig_ok, 1)
            for b in range(4):
                act.wait_ge(u_T, b + 1)
                act.copy(Uc[:, 8 * b:8 * b + 8, :], k.ps[:, b, :].rearrange("p (g c) -> p g c", g=8)).then_inc(u_out, 1)
            for dr in range(2):
                for i in range(8):
                    act.wait_ge(x_T, 8 * dr + i + 1)
                    act.copy(W1[:, 2 * i:2 * i + 2, :, :], k.ps[:, 4 + i % 4, :]
                             .rearrange("p (a r n) -> p a r n", a=2, r=2)).then_inc(w_out, 1)
            for b in range(0, 8, 2):
                act.wait_ge(y_mm, b + 1)
                act.copy(y_bank(b),
                         k.ps[0:NCH, b, :].rearrange("p (g i c) -> p i g c", g=4, i=L)).then_inc(y_a, 1)

        @block.vector
        def _(dve):
            def ts(o, i, s1, s2, op0, op1=None):
                k.link(dve, dve.tensor_scalar(o, i, s1, s2, op0, op1) if op1 else dve.tensor_scalar(o, i, s1, None, op0))

            def tt(o, a, b, op):
                k.link(dve, dve.tensor_tensor(o, a, b, op))

            r = {n: par[0:32, i, :] for i, n in enumerate(
                ("A_re", "A_im", "a_re", "a_im", "c_re", "c_im", "cos", "sin", "mod", "x", "th", "half", "s2", "n",
                 "t", "inv"))}
            dve.wait_ge(raw, 48)
            dve.wait_ge(dt_ok, 1)
            dt = spread(ldt[0:32, :], 2, SN)
            for o, i in (("x", "A_re"), ("th", "A_im")):
                tt(r[o].rearrange("p (a n) -> p a n", a=2), r[i].rearrange("p (a n) -> p a n", a=2), dt, ALU.mult)
            ts(r["n"], r["th"], 1.0 / (TWO_PI_HI + TWO_PI_LO), ROUND, ALU.mult, ALU.add)
            ts(r["n"], r["n"], ROUND, None, ALU.subtract)
            for c in (TWO_PI_HI, TWO_PI_LO):
                k.link(dve, dve.scalar_tensor_tensor(out=r["th"], in0=r["n"], scalar=-c, in1=r["th"], op0=ALU.mult,
                                                     op1=ALU.add))
            ts(r["th"], r["th"], 3.1415925, -3.1415925, ALU.min, ALU.max)
            dve.tensor_scalar(r["half"], r["th"], 0.5, None, ALU.mult).then_inc(ang_ok, 1)
            dve.wait_ge(trig_ok, 3)
            tt(r["t"], r["s2"], r["s2"], ALU.mult)
            ts(r["cos"], r["t"], -2.0, 1.0, ALU.mult, ALU.add)
            tt(r["a_re"], r["mod"], r["cos"], ALU.mult)
            tt(r["a_im"], r["mod"], r["sin"], ALU.mult)
            tt(r["t"], r["A_re"], r["A_re"], ALU.mult)
            tt(r["inv"], r["A_im"], r["A_im"], ALU.mult)
            tt(r["inv"], r["inv"], r["t"], ALU.add)
            k.link(dve, dve.reciprocal(r["inv"], r["inv"]))
            ts(r["n"], r["a_re"], -1.0, None, ALU.add)
            tt(r["c_re"], r["n"], r["A_re"], ALU.mult)
            tt(r["t"], r["a_im"], r["A_im"], ALU.mult)
            tt(r["c_re"], r["c_re"], r["t"], ALU.add)
            tt(r["c_re"], r["c_re"], r["inv"], ALU.mult)
            tt(r["c_im"], r["a_im"], r["A_re"], ALU.mult)
            tt(r["t"], r["n"], r["A_im"], ALU.mult)
            tt(r["c_im"], r["c_im"], r["t"], ALU.subtract)
            dve.tensor_tensor(r["c_im"], r["c_im"], r["inv"], ALU.mult).then_inc(par_ok, 1)
            dve.wait_ge(par_T, 1)
            k.link(dve, dve.tensor_copy(pt, k.ps[:, 0, 0:224].rearrange("p (i q) -> p i q", i=7)))
            for i in range(4):
                dve.wait_ge(cT, i + 1)
                src = k.ps[:, 4 + i, :].rearrange("p (q a c) -> p q a c", a=2, c=SC)
                for a in range(2):
                    half = slice(SN * a, SN * (a + 1))
                    ins = dve.tensor_scalar(CT[half, i // 2, GP * (i % 2):GP * (i % 2 + 1), :], src[half, :, a, :],
                                            (1.0, -1.0)[i // 2], None, ALU.mult)
                ins.then_inc(cT_out, 1)
            dve.memset(PA[:, 0, :, 0:1], 1.0)
            dve.memset(PA[:, 1, :, 0:1], 0.0)
            k.link(dve, dve.tensor_copy(PA[:, :, :, 1], pt[:, 0:2, :]))
            for lo, n in ((1, 1), (2, 2), (4, 4)):
                def by(ri):
                    return spread(PA[:, ri, :, lo], 2, n)
                cmul(dve, PA[:, 0, :, lo + 1:lo + 1 + n], PA[:, 1, :, lo + 1:lo + 1 + n], PA[:, 0, :, 1:1 + n],
                     PA[:, 1, :, 1:1 + n], by(0), by(1), tmp128.rearrange("p (q n) -> p q n", n=4)[:, :, 0:n])
            for ri in range(2):
                ins = dve.tensor_copy(PD[:, ri, :, :], backwards(PA[:, ri, :, :]))
            ins.then_inc(powers, 1)
            dve.wait_ge(powers, 1)
            src = (pt[:, 4, :], pt[:, 5, :])
            for i in range(3):
                dst = (zz[:, 2 * (i % 2), :], zz[:, 2 * (i % 2) + 1, :])
                cmul(dve, *dst, *src, *src, tmp32)
                src = dst
            z_re, z_im = src
            for i in range(3):
                tt(pt[:, 6, :], pt[:, 6, :], pt[:, 6, :], ALU.mult)
            dve.wait_ge(c_raw, 16 * 11)
            dve.wait_ge(cT_out, 4)
            cmul(dve, Bb[:, 0, :, :], Bb[:, 1, :, :], Br[:, 0, :, :], Br[:, 1, :, :], spread(pt[:, 2, :], 2, SC),
                 spread(pt[:, 3, :], 2, SC), tmpB)
            for dr in range(2):
                q = slice(GP * dr, GP * (dr + 1))
                pw = PA[:, :, q, 0:L] if dr else PD[:, :, q, 1:L + 1]
                cmul(dve, *(X[:, ri, :, :].rearrange("p q (s c) -> p q s c", c=SC) for ri in range(2)),
                     *(spread(pw[:, ri, :, :], 3, SC) for ri in range(2)),
                     *(spread(Bb[:, ri, q, :], 2, L) for ri in range(2)), tmpX)
                dve.sem_inc(x_ok, 1)
                dve.wait_ge(x_T, 8 * (dr + 1))
                k.link(dve, dve.tensor_copy(E[:, 0, :, 0], z_re[:, q]))
                k.link(dve, dve.tensor_copy(E[:, 1, :, 0], z_im[:, q]))
                dve.wait_ge(s_ok, dr + 1)
                n = 1
                while n < NCH:
                    cmul(dve, E[:, 0, :, n:2 * n], E[:, 1, :, n:2 * n], E[:, 0, :, 0:n], E[:, 1, :, 0:n],
                         spread(E[:, 0, :, n - 1], 2, n), spread(E[:, 1, :, n - 1], 2, n), tmpS[:, :, 0:n])
                    n *= 2
                k.link(dve, dve.tensor_copy(R, spread(pt[:, 6, q], 2, NCH)))
                k.link(dve, dve.memset(R[:, :, 0:1], 0.0))
                s_re, s_im = (k.ps[:, 2 * ri:2 * ri + 2, :].rearrange("p b (q c) -> p (b q) c", c=NCH) for ri in range(2))
                if dr:
                    s_re, s_im = backwards(s_re), backwards(s_im)
                tt(SH[:, 0, :, :], s_re, E[:, 0, :, :], ALU.mult)
                tt(tmpS, s_im, E[:, 1, :, :], ALU.mult)
                tt(SH[:, 0, :, :], SH[:, 0, :, :], tmpS, ALU.add)
                tt(SH[:, 1, :, :], s_im, E[:, 0, :, :], ALU.mult)
                tt(tmpS, s_re, E[:, 1, :, :], ALU.mult)
                tt(SH[:, 1, :, :], SH[:, 1, :, :], tmpS, ALU.subtract)
                for ri in range(2):
                    flat = SH[:, ri, :, :].rearrange("p q c -> p (q c)")
                    k.link(dve, dve.tensor_tensor_scan(flat, R.rearrange("p q c -> p (q c)"), flat, 0.0, ALU.mult,
                                                       ALU.add))
                hs = [Hs[:, 2 * dr + ri, :, :] for ri in range(2)]
                m = NCH - 1
                dst = [backwards(x[:, :, 0:m]) if dr else x[:, :, 1:NCH] for x in hs]
                cmul(dve, *dst, SH[:, 0, :, 0:m], SH[:, 1, :, 0:m], E[:, 0, :, 0:m], E[:, 1, :, 0:m], tmpS[:, :, 0:m])
                z = slice(NCH - 1, NCH) if dr else slice(0, 1)
                dve.memset(hs[0][:, :, z], 0.0)
                dve.memset(hs[1][:, :, z], 0.0).then_inc(h_ok, 1)
            tt(dD[0:SC], spread(dT[0:SC, :], 2, SC), spread(eye[0:SC, 0:SC], 1, SG), ALU.mult)
            for b in range(4):
                dve.wait_ge(k_mm, b + 1)
                if b >= 2:
                    dve.wait_ge(t_ok, 16 * L * b)
                f, g = (k.ps[0:SC, 4 * (b % 2) + 2 * dr:4 * (b % 2) + 2 * dr + 2, :]
                        .rearrange("p a (q s) -> p a q s", q=4) for dr in range(2))
                kk = KK[b % 2][0:SC]
                by_a = kk.rearrange("p (q a) s c -> p a q (s c)", a=2)
                k.link(dve, dve.tensor_copy(by_a[:, :, :, SC * (L - 1):], f))
                k.link(dve, dve.tensor_copy(by_a[:, :, :, 0:SC * (L - 1)], g[:, :, :, 0:SC * (L - 1)]))
                lag0 = by_a[:, :, :, SC * (L - 1):SC * L]
                tt(lag0, lag0, g[:, :, :, SC * (L - 1):], ALU.add)
                dve.tensor_tensor(kk[:, :, L - 1, :], kk[:, :, L - 1, :], dD[0:SC, 8 * b:8 * b + 8, :],
                                  ALU.add).then_inc(kk_ok, 1)
            for b in range(1, 8, 2):
                dve.wait_ge(y_mm, b + 1)
                dve.tensor_copy(y_bank(b),
                                k.ps[0:NCH, b, :].rearrange("p (g i c) -> p i g c", g=4, i=L)).then_inc(y_v, 1)



def mix_mid(k):
    nc, d = k.nc, k.d
    ys, gyT = view(k, H0, NT, 512), view(k, H0 + 2048, 4, S)
    sgT = view(k, U0, 4, S)
    cosS, sinS, dft = view(k, Z0, NT, S), view(k, Z0 + 2048, NT, S), view(k, Z0 + 4096, 2 * P)
    FA = view(k, Z0 + 4352, NT, 2, FG, P)
    FT = view(k, Z0 + 8448, FG, S)
    tmp = view(k, Z0 + 10496, 2, S)
    k.merged = view(k, Z0 + 12544 - 1024, NT, D)
    sig = view(k, U0 + 2048, 4, S)
    y = view(k, Y0, NT, 2 * D)
    first = first_chunk(k, "mix_mid")
    (tabs, ys_in, fa_mm, fa_a, fa_v, ys_T, gy_ok, ft_mm, ft_ok, glu_mm, sig_ok, sg_ok, p_mm, p_ok) = (
        k.sem("mid_" + n) for n in ("tables", "ys_loaded", "channel_dft", "channel_act", "channel_dve", "ys_turned",
                                    "gelu", "token_dft", "token_copied", "glu_done", "sigmoid", "gated", "proj_done",
                                    "merged"))

    with nc.Block() as block:
        @block.sync
        def _(sp):
            sp.dma_start(dft, d["dft"]).then_inc(tabs, 16)
            sp.dma_start(ys, k.ys_dram.rearrange("(m p) n -> p m n", p=P)).then_inc(ys_in, 16)
            sp.dma_start(view(k, Z0, 2048), d["cosS"]).then_inc(tabs, 16)
            sp.dma_start(view(k, Z0 + 2048, 2048), d["sinS"]).then_inc(tabs, 16)
            load_weights(k, sp, "mix_mid")

        @block.tensor
        def _(pe):
            pe.wait_ge(tabs, 48)
            for m in range(NT):
                for g in range(FG):
                    mm = pe.matmul(k.ps[:, 2 * m + g // 2, 256 * (g % 2):256 * (g % 2) + 256],
                                   k.ufT[:, g, m * P:(m + 1) * P], dft, start=True, stop=True)
                    if g % 2:
                        mm.then_inc(fa_mm, 1)
            pe.wait_ge(ys_in, 16)
            for c in range(4):
                if c < 2:
                    pe.wait_ge(fa_a, c + 1)
                    pe.wait_ge(fa_v, c + 1)
                for m in range(NT):
                    t = pe.transpose(k.ps[:, c, m * P:(m + 1) * P], ys[:, m, c * P:(c + 1) * P], k.ident)
                t.then_inc(ys_T, 1)
            pe.wait_ge(fa_a, NT)
            pe.wait_ge(fa_v, NT)
            for g in range(FG):
                for m in range(NT):
                    for ri in range(2):
                        mm = pe.matmul(k.ps[:, 4 + g, :], FA[:, m, ri, g, :], (cosS, sinS)[ri][:, m, :],
                                       start=m == 0 and ri == 0, stop=m == NT - 1 and ri == 1)
                mm.then_inc(ft_mm, 1)
            pe.wait_ge(gy_ok, 4)
            wait_chunk(k, pe, first)
            w = view(k, k.slot(first), 4, 512)
            for c in range(4):
                for kk in range(4):
                    mm = pe.matmul(k.ps[:, c, :], w[:, kk, c * P:(c + 1) * P], gyT[:, kk, :], start=kk == 0,
                                   stop=kk == 3)
                mm.then_inc(glu_mm if c < 3 else k.chunk_used, 1)
            pe.wait_ge(ft_ok, FG)
            for i, xT in enumerate((sgT, FT)):
                wait_chunk(k, pe, first + 1 + i)
                w = view(k, k.slot(first + 1 + i), 4, D)
                for m in range(NT):
                    for n in range(2):
                        b = 2 * m + n
                        if i:
                            pe.wait_ge(p_ok, b + 1)
                        elif b == 0:
                            pe.wait_ge(sg_ok, 4)
                        for kk in range(4):
                            mm = pe.matmul(k.ps[:, b, :], xT[:, kk, m * P:(m + 1) * P], w[:, kk, 512 * n:512 * n + 512],
                                           start=kk == 0, stop=kk == 3)
                        mm.then_inc(p_mm if b < 7 else k.chunk_used, 1)

        @block.scalar
        def _(act):
            for m in range(NT):
                act.wait_ge(fa_mm, 2 * m + 1)
                act.copy(FA[:, m, :, 0:2, :], k.ps[:, 2 * m, :].rearrange("p (g r c) -> p r g c", g=2, r=2)).then_inc(fa_a, 1)
            for c in range(4):
                act.wait_ge(ys_T, c + 1)
                act.activation(gyT[:, c, :], k.ps[:, c, :], ACT.Gelu_apprx_tanh).then_inc(gy_ok, 1)
            for c in range(4):
                if c < 3:
                    act.wait_ge(glu_mm, c + 1)
                else:
                    act.wait_ge(k.chunk_used, first + 1)
                act.activation(sig[:, c, :], k.ps[:, c, :], ACT.Sigmoid).then_inc(sig_ok, 1)

        @block.vector
        def _(dve):
            for m in range(NT):
                dve.wait_ge(fa_mm, 2 * m + 2)
                dve.tensor_copy(FA[:, m, :, 2:4, :], k.ps[:, 2 * m + 1, :]
                                .rearrange("p (g r c) -> p r g c", g=2, r=2)).then_inc(fa_v, 1)
            for g in range(FG):
                dve.wait_ge(ft_mm, g + 1)
                dve.tensor_copy(FT[:, g, :], k.ps[:, 4 + g, :]).then_inc(ft_ok, 1)
            for c in range(4):
                dve.wait_ge(sig_ok, c + 1)
                dve.tensor_tensor(sgT[:, c, :], sig[:, c, :], gyT[:, c, :], ALU.mult).then_inc(sg_ok, 1)
            for i in range(2):
                for b in range(8):
                    m, n = b // 2, b % 2
                    if b < 7:
                        dve.wait_ge(p_mm, 7 * i + b + 1)
                    else:
                        dve.wait_ge(k.chunk_used, first + 2 + i)
                    dst = k.merged[:, m, 512 * n:512 * n + 512]
                    gate = y[:, m, D * (1 - i) + 512 * n:D * (1 - i) + 512 * n + 512]
                    if i == 0:
                        dve.tensor_tensor(dst, k.ps[:, b, :], gate, ALU.mult).then_inc(p_ok, 1)
                    else:
                        if b < 2:
                            dve.wait_ge(p_ok, 8)
                        k.link(dve, dve.tensor_tensor(tmp[:, b % 2, :], k.ps[:, b, :], gate, ALU.mult))
                        k.link(dve, dve.tensor_tensor(dst, dst, tmp[:, b % 2, :], ALU.add))



def expert_slot(k, e, i):
    return RING + i * SLOT if e % 2 == 0 else U0 + i * SLOT


def expert_source(k, e, i):
    w = (k.d["expert_w_gate_2"], k.d["expert_w_up_2"], k.d["expert_w_down_2"])[i]
    return w[0, e].rearrange("(k p) n -> p k n", p=P)


def expert_view(k, e, i):
    return view(k, expert_slot(k, e, i), *((KD, DE) if i < 2 else (KE, D)))


def mix_out(k):
    nc, d = k.nc, k.d
    h = view(k, H0, NT, D)
    k.hn = view(k, Y0, NT, D)
    hnT = view(k, Y0 + 4096, KD, S)
    mT = view(k, Z0 + 4096, KD, S)
    gain = view(k, Z0 + 8192, D)
    squares = view(k, Z0 + 9216, D)
    wr = view(k, Z0 + 10240, KD, EG + NE)
    br = view(k, Z0 + 10816, EG + NE)
    lg = view(k, Z0 + 10896, NT, EG + NE)
    R0 = Z0 + 11520 - 336
    oh_g = view(k, R0, NT, EG)
    cand = view(k, R0 + 32, NT, EG)
    eg = view(k, R0 + 64, NT, EG)
    es = view(k, R0 + 96, NT, EPG)
    oh_e = view(k, R0 + 128, 2, NT, EPG)
    pick = view(k, R0 + 192, NT, EG, EPG)
    OH = [view(k, R0 + 448 + 256 * i, NT, NE) for i in range(2)]
    M = view(k, R0 + 960, NT, NE)
    rank = view(k, R0 + 1216, NT, NE)
    prod = view(k, R0 + 1472, NT, NE)
    cnt = view(k, R0 + 1728, NE)
    before = view(k, R0 + 1792, P)
    ones = view(k, R0 + 1920, P)
    sm = view(k, R0 + 2048, 16, NT)
    blk = view(k, R0 + 2112, NT, 2)
    zero64 = view(k, R0 + 2120, NE)
    tmp64 = view(k, R0 + 2184, NE)
    K0 = Z0 + 16640
    k.rk = view(k, K0, NT, NE)
    k.gate_w = view(k, K0 + 256, 2, NT)
    k.dest = view(k, K0 + 264, 2, NT)
    k.flag = view(k, K0 + 272, 1)
    k.starts = view(k, K0 + 280, NE)
    k.nb = view(k, K0 + 344, NE)
    k.iota = view(k, K0 + 408, NE)
    n1 = Norm(k, "norm_ffn", h, NT, scratch=squares, stat=0, dst=k.hn)
    first = first_chunk(k, "mix_out")
    k.e_loaded = [[k.lasting_sem(f"expert_{a}_{w}") for w in ("gate", "up", "down")] for a in ("even", "odd")]
    (small, h_in, m_T, m_a, m_v, bank, added, gained, x_st, hn_T, hn_out, lg_mm, ge_ok, ge_out, ex_in, ex_out, m_ok, r_mm,
     done) = (k.sem("out_" + n) for n in
              ("small", "h_loaded", "turned", "copied_act", "copied_dve", "bank_done", "added", "gained", "x_stored",
               "hn_turned", "hn_copied", "logits", "group_shifted", "group_exp", "pair_in", "pair_exp", "chosen",
               "ranked", "routed"))

    with nc.Block() as block:
        @block.sync
        def _(sp):
            sp.dma_start(h, k.h_dram[1].rearrange("(m p) n -> p m n", p=P)).then_inc(h_in, 16)
            sp.dma_start(gain, d["ffn_norm_g_2"].to_broadcast([P, D])).then_inc(small, 16)
            sp.dma_start(wr[:, :, 0:EG], d["router_group_w_2"][0].rearrange("(k p) n -> p k n", p=P)).then_inc(small, 16)
            sp.dma_start(wr[:, :, EG:], d["router_expert_w_2"][0].rearrange("(k p) n -> p k n", p=P)).then_inc(small, 16)
            sp.dma_start(br[:, 0:EG], d["router_group_b_2"].to_broadcast([P, EG])).then_inc(small, 16)
            sp.dma_start(br[:, EG:], d["router_expert_b_2"].to_broadcast([P, NE])).then_inc(small, 16)
            sp.dma_start(k.iota, d["iota"]).then_inc(small, 16)
            load_weights(k, sp, "mix_out")
            sp.wait_ge(m_T, KD)
            sp.dma_start(before, d["before"]).then_inc(small, 16)
            for i in range(3):
                sp.dma_start(expert_view(k, 1, i), expert_source(k, 1, i)).then_inc(k.e_loaded[1][i], 16)
            sp.wait_ge(k.chunk_used, len(k.chunks))
            for i in range(3):
                sp.dma_start(expert_view(k, 0, i), expert_source(k, 0, i)).then_inc(k.e_loaded[0][i], 16)

        @block.gpsimd
        def _(pool):
            pool.wait_ge(m_T, KD)
            pool.memset(ones, 1.0).then_inc(done, 1)

        @block.tensor
        def _(pe):
            for kk in range(KD):
                for m in range(NT):
                    t = pe.transpose(k.ps[:, kk, m * P:(m + 1) * P], k.merged[:, m, kk * P:(kk + 1) * P], k.ident)
                t.then_inc(m_T, 1)
            pe.wait_ge(m_a, KD // 2)
            pe.wait_ge(m_v, KD // 2)
            for n in range(2):
                wait_chunk(k, pe, first + n)
                w = view(k, k.slot(first + n), KD, 512)
                for m in range(NT):
                    for kk in range(KD):
                        mm = pe.matmul(k.ps[:, 4 * n + m, :], mT[:, kk, m * P:(m + 1) * P], w[:, kk, :], start=kk == 0,
                                       stop=kk == KD - 1)
                    mm.then_inc(bank if m < NT - 1 else k.chunk_used, 1)
            pe.wait_ge(gained, NT)
            for kk in range(KD):
                for m in range(NT):
                    t = pe.transpose(k.ps[:, kk, m * P:(m + 1) * P], k.hn[:, m, kk * P:(kk + 1) * P], k.ident)
                t.then_inc(hn_T, 1)
            pe.wait_ge(hn_out, KD)
            pe.wait_ge(small, 16 * 7)
            for m in range(NT):
                for kk in range(KD):
                    mm = pe.matmul(k.ps[:, m, 0:EG + NE], hnT[:, kk, m * P:(m + 1) * P], wr[:, kk, :], start=kk == 0,
                                   stop=kk == KD - 1)
                mm.then_inc(lg_mm, 1)
            pe.wait_ge(m_ok, 1)
            pe.wait_ge(done, 1)
            for m in range(NT):
                for b in range(m):
                    pe.matmul(k.ps[:, 4, NE * m:NE * (m + 1)], ones, M[:, b, :], start=b == 0, stop=False)
                pe.matmul(k.ps[:, 4, NE * m:NE * (m + 1)], before, M[:, m, :], start=m == 0, stop=True)
            for m in range(NT):
                mm = pe.matmul(k.ps[:, 5, 0:NE], ones, M[:, m, :], start=m == 0, stop=m == NT - 1)
            mm.then_inc(r_mm, 1)

        @block.scalar
        def _(act):
            for kk in range(0, KD, 2):
                act.wait_ge(m_T, kk + 1)
                act.copy(mT[:, kk, :], k.ps[:, kk, :]).then_inc(m_a, 1)
            act.wait_ge(added, 2 * NT)
            n1.scalar_sums(act)
            n1.scalar_root(act)
            for kk in range(KD):
                act.wait_ge(hn_T, kk + 1)
                act.copy(hnT[:, kk, :], k.ps[:, kk, :]).then_inc(hn_out, 1)
            act.wait_ge(ge_ok, 1)
            act.activation(eg, eg, ACT.Exp).then_inc(ge_out, 1)
            act.wait_ge(ex_in, 1)
            act.activation(sm[:, 3, :], sm[:, 3, :], ACT.Exp).then_inc(ex_out, 1)

        @block.vector
        def _(dve):
            def tt(o, a, b, op):
                k.link(dve, dve.tensor_tensor(o, a, b, op))

            def ts(o, i, s1, s2, op0, op1=None):
                k.link(dve, dve.tensor_scalar(o, i, s1, s2, op0, op1) if op1 else dve.tensor_scalar(o, i, s1, None, op0))

            for kk in range(1, KD, 2):
                dve.wait_ge(m_T, kk + 1)
                dve.tensor_copy(mT[:, kk, :], k.ps[:, kk, :]).then_inc(m_v, 1)
            dve.wait_ge(h_in, 16)
            for n in range(2):
                for m in range(NT):
                    if m < NT - 1:
                        dve.wait_ge(bank, (NT - 1) * n + m + 1)
                    else:
                        dve.wait_ge(k.chunk_used, first + n + 1)
                    hs = h[:, m, n * 512:(n + 1) * 512]
                    dve.tensor_tensor(hs, hs, k.ps[:, 4 * n + m, :], ALU.add).then_inc(added, 1)
            n1.vector_mean(dve)
            n1.vector_scale(dve)
            dve.wait_ge(n1.normed, NT)
            dve.wait_ge(small, 16 * 7)
            for m in range(NT):
                dve.tensor_tensor(k.hn[:, m, :], k.hn[:, m, :], gain, ALU.mult).then_inc(gained, 1)
            dve.wait_ge(lg_mm, NT)
            for m in range(NT):
                ins = dve.tensor_tensor(lg[:, m, :], k.ps[:, m, 0:EG + NE], br, ALU.add)
            k.link(dve, ins)
            iota8 = spread(k.iota[:, 0:8], 1, NT)

            def first_max(x, top, hot, w):
                k.link(dve, dve.tensor_reduce(top, x, AX_X, ALU.max))
                tt(w, x, spread(top, 2, 8), ALU.is_equal)
                k.link(dve, dve.scalar_tensor_tensor(out=w, in0=w, scalar=-64.0, in1=iota8, op0=ALU.mult, op1=ALU.add))
                k.link(dve, dve.tensor_reduce(sm[:, 15, :], w, AX_X, ALU.min))
                tt(hot, w, spread(sm[:, 15, :], 2, 8), ALU.is_equal)

            gl = lg[:, :, 0:EG]
            first_max(gl, sm[:, 0, :], oh_g, cand)
            dve.tensor_tensor(eg, gl, spread(sm[:, 0, :], 2, EG), ALU.subtract).then_inc(ge_ok, 1)
            tt(pick, lg[:, :, EG:].rearrange("p t (g e) -> p t g e", g=EG), spread(oh_g, 3, EPG), ALU.mult)
            k.link(dve, dve.tensor_reduce(es, pick.rearrange("p t g e -> p t e g"), AX_X, ALU.add))
            first_max(es, sm[:, 1, :], oh_e[:, 0, :, :], cand)
            k.link(dve, dve.scalar_tensor_tensor(out=es, in0=oh_e[:, 0, :, :], scalar=-BIG, in1=es, op0=ALU.mult,
                                                 op1=ALU.add))
            first_max(es, sm[:, 2, :], oh_e[:, 1, :, :], cand)
            dve.tensor_tensor(sm[:, 3, :], sm[:, 2, :], sm[:, 1, :], ALU.subtract).then_inc(ex_in, 1)
            for c in range(2):
                tt(OH[c].rearrange("p t (g e) -> p t g e", g=EG), spread(oh_g, 3, EPG), spread(oh_e[:, c, :, :], 2, EG),
                   ALU.mult)
            dve.tensor_tensor(M, OH[0], OH[1], ALU.add).then_inc(m_ok, 1)
            dve.wait_ge(ge_out, 1)
            k.link(dve, dve.tensor_reduce(sm[:, 4, :], eg, AX_X, ALU.add))
            dve.wait_ge(ex_out, 1)
            ts(sm[:, 5, :], sm[:, 3, :], 1.0, None, ALU.add)
            tt(sm[:, 5, :], sm[:, 5, :], sm[:, 4, :], ALU.mult)
            k.link(dve, dve.reciprocal(k.gate_w[:, 0, :], sm[:, 5, :]))
            tt(k.gate_w[:, 1, :], k.gate_w[:, 0, :], sm[:, 3, :], ALU.mult)
            dve.wait_ge(r_mm, 1)
            k.link(dve, dve.tensor_copy(rank, k.ps[:, 4, 0:NT * NE].rearrange("p (t e) -> p t e", t=NT)))
            k.link(dve, dve.tensor_copy(cnt, k.ps[:, 5, 0:NE]))
            k.link(dve, dve.scalar_tensor_tensor(out=k.rk, in0=rank, scalar=1.0, in1=M, op0=ALU.add, op1=ALU.mult))
            ts(k.rk, k.rk, -1.0, None, ALU.add)
            k.link(dve, dve.memset(zero64, 0.0))
            ts(k.nb, cnt, float(SLOTS), None, ALU.is_gt)
            for i in range(2, 8):
                k.link(dve, dve.scalar_tensor_tensor(out=k.nb, in0=cnt, scalar=float(SLOTS * i), in1=k.nb,
                                                     op0=ALU.is_gt, op1=ALU.add))
            k.link(dve, dve.tensor_tensor_scan(tmp64, k.nb, zero64, 0.0, ALU.add, ALU.add))
            tt(k.starts, tmp64, k.nb, ALU.subtract)
            k.link(dve, dve.tensor_copy(k.flag.bitcast(I32), tmp64[:, NE - 1:NE]))
            for c in range(2):
                r, e, st, b, z = (sm[:, 6 + i, :] for i in range(5))
                for o, tab in ((r, rank), (e, spread(k.iota, 1, NT)), (st, spread(k.starts, 1, NT))):
                    tt(prod, OH[c], tab, ALU.mult)
                    k.link(dve, dve.tensor_reduce(o, prod, AX_X, ALU.add))
                ts(b, r, float(SLOTS), None, ALU.is_ge)
                for i in range(2, 8):
                    k.link(dve, dve.scalar_tensor_tensor(out=b, in0=r, scalar=float(SLOTS * i), in1=b, op0=ALU.is_ge,
                                                         op1=ALU.add))
                ts(z, b, 0.0, None, ALU.is_equal)
                tt(st, st, b, ALU.add)
                ts(st, st, float(NE - 1), None, ALU.add)
                tt(e, e, st, ALU.subtract)
                tt(e, e, z, ALU.mult)
                tt(e, e, st, ALU.add)
                tt(e, e, b, ALU.subtract)
                k.link(dve, dve.scalar_tensor_tensor(out=e, in0=e, scalar=float(SLOTS), in1=r, op0=ALU.mult,
                                                     op1=ALU.add))
                k.link(dve, dve.tensor_copy(k.dest[:, c, :].bitcast(U32), e))



def since(eng, sem, v):
    if not isinstance(v, int) or v > 0:
        eng.wait_ge(sem, v)


def moe(k):
    nc, ps = k.nc, k.ps
    t = Z0 + 4096
    pick = view(k, t, 2, NT, SLOTS)
    xg = view(k, t + 512, 2, 512)
    xT = view(k, t + 1536, 2, KE, 2 * SLOTS)
    gu = view(k, t + 2560, 2, 512)
    sg = view(k, t + 3584, 2, KE, SLOTS)
    aT = view(k, t + 4096, 2, KE, SLOTS)
    yn = view(k, t + 4608, 2, 512)
    (picked, x_done, xg_ready, x_turned, x_ready, gu_done, gu_ready, gu_turned, silu_done, a_ready, y_done,
     rows_ready) = (k.sem("moe_" + n) for n in
                    ("picked", "x_gathered", "x_copied", "x_turned", "xT_ready", "hidden_done", "hidden_copied",
                     "hidden_turned", "silu_done", "a_ready", "y_done", "rows_ready"))
    stored = [k.sem(f"moe_stored{i}") for i in range(2)]
    pairs_n = NE // 2

    def pairs(eng, step, first, last):
        with eng.Fori(first, last) as r:
            for a in range(2):
                step(2 * r + a, a, r)

    def all_pairs(eng, step):
        for r in range(2):
            for a in range(2):
                step(2 * r + a, a, r)
        pairs(eng, step, 2, pairs_n - 1)
        for a in range(2):
            step(NE - 2 + a, a, pairs_n - 1)

    def exists(e):
        return not isinstance(e, int) or 0 <= e < NE

    with nc.Block() as block:
        @block.sync
        def _(sp):
            def load(e, a, r):
                for i in range(3):
                    w = (k.d["expert_w_gate_2"], k.d["expert_w_up_2"], k.d["expert_w_down_2"])[i][0]
                    sp.wait_ge(y_done if i == 2 else gu_done, e - 1)
                    src = w[bass.ds(e, 1)].rearrange("e (k p) n -> p (e k) n", p=P)
                    sp.dma_start(expert_view(k, a, i), src).then_inc(k.e_loaded[a][i], 16)

            pairs(sp, load, 1, pairs_n)

        @block.tensor
        def _(pe):
            def gather(e, a):
                pe.wait_ge(picked, e + 1)
                since(pe, xg_ready, e - 1)
                for m in range(NT):
                    for c in range(2):
                        mm = pe.matmul(ps[SLOTS * c:SLOTS * (c + 1), a, :], pick[:, a, m, :],
                                       k.hn[:, m, 512 * c:512 * (c + 1)], start=m == 0, stop=m == NT - 1)
                mm.then_inc(x_done, 1)

            def turn_x(e, a):
                pe.wait_ge(xg_ready, e + 1)
                since(pe, x_ready, e)
                for j in range(KE):
                    tr = pe.transpose(ps[:, 2, P * j:P * (j + 1)], xg[:, a, P * j:P * (j + 1)], k.ident)
                tr.then_inc(x_turned, 1)

            def hidden(e, a, r):
                pe.wait_ge(x_ready, e + 1)
                since(pe, gu_ready, e - 1)
                for i in range(2):
                    pe.wait_ge(k.e_loaded[a][i], 16 * r + 16)
                for kk in range(KD):
                    for i in range(2):
                        mm = pe.matmul(ps[SLOTS * i:SLOTS * (i + 1), 3 + a, :],
                                       xT[:, a, kk % KE, SLOTS * (kk // KE):SLOTS * (kk // KE + 1)],
                                       expert_view(k, a, i)[:, kk, :], start=kk == 0, stop=kk == KD - 1)
                mm.then_inc(gu_done, 1)

            def turn_hidden(e, a):
                pe.wait_ge(gu_ready, e + 1)
                since(pe, a_ready, e)
                for f in range(KE):
                    tr = pe.transpose(ps[:, 5, P * f:P * (f + 1)], gu[:, a, P * f:P * (f + 1)], k.ident)
                tr.then_inc(gu_turned, 1)

            def result(e, a, loads):
                pe.wait_ge(a_ready, e + 1)
                since(pe, rows_ready, e - 1)
                pe.wait_ge(k.e_loaded[a][2], 16 * loads)
                w = expert_view(k, a, 2)
                for f in range(KE):
                    for c in range(2):
                        mm = pe.matmul(ps[SLOTS * c:SLOTS * (c + 1), 6 + a, :], aT[:, a, f, :],
                                       w[:, f, 512 * c:512 * (c + 1)], start=f == 0, stop=f == KE - 1)
                mm.then_inc(y_done, 1)

            def step(e, a, r):
                hidden(e, a, r)
                if exists(e - 1):
                    result(e - 1, 1 - a, r + a)
                turn_hidden(e, a)
                if exists(e + 1):
                    turn_x(e + 1, 1 - a)
                if exists(e + 2):
                    gather(e + 2, a)

            gather(0, 0)
            gather(1, 1)
            turn_x(0, 0)
            all_pairs(pe, step)
            result(NE - 1, 1, pairs_n)

        @block.scalar
        def _(act):
            def hidden(e, a):
                act.wait_ge(gu_done, e + 1)
                since(act, gu_turned, e - 1)
                act.copy(gu[:, a, :], ps[:, 3 + a, :]).then_inc(gu_ready, 1)

            def rows(e, a, r):
                act.wait_ge(y_done, e + 1)
                since(act, stored[a], 16 * r)
                act.copy(yn[:, a, :], ps[:, 6 + a, :]).then_inc(rows_ready, 1)
                act.wait_ge(rows_ready, e + 1)
                act.dma_start(k.ypad[bass.ds(SLOTS * e, SLOTS)].rearrange("s (c n) -> c s n", c=2),
                              yn[:, a, :]).then_inc(stored[a], 16)

            def silu(e, a):
                act.wait_ge(gu_turned, e + 1)
                since(act, a_ready, e - 1)
                act.activation(sg[:, a, :, :], ps[:, 5, :].rearrange("p (f s) -> p f s", f=KE)[:, :, 0:SLOTS],
                               ACT.Silu).then_inc(silu_done, 1)

            def step(e, a, r):
                hidden(e, a)
                if exists(e - 1):
                    rows(e - 1, 1 - a, r - 1 + a)
                silu(e, a)

            all_pairs(act, step)
            rows(NE - 1, 1, pairs_n - 1)
            for a in range(2):
                act.wait_ge(stored[a], 16 * pairs_n)

        @block.vector
        def _(dve):
            def choose(e, a):
                since(dve, x_done, e - 1)
                dve.tensor_tensor(pick[:, a, :, :], spread(k.iota, 1, NT),
                                  k.rk[:, :, bass.ds(e, 1)].to_broadcast([P, NT, SLOTS]),
                                  ALU.is_equal).then_inc(picked, 1)

            def gathered(e, a):
                dve.wait_ge(x_done, e + 1)
                since(dve, x_turned, e - 1)
                dve.tensor_copy(xg[:, a, :], ps[:, a, :]).then_inc(xg_ready, 1)

            def turned(e, a):
                dve.wait_ge(x_turned, e + 1)
                since(dve, gu_done, e - 1)
                dve.tensor_copy(xT[:, a, :, :], ps[:, 2, :].rearrange("p (j s) -> p j s", j=KE)).then_inc(x_ready, 1)

            def gated(e, a):
                dve.wait_ge(silu_done, e + 1)
                since(dve, y_done, e - 1)
                dve.tensor_tensor(aT[:, a, :, :], sg[:, a, :, :],
                                  ps[:, 5, :].rearrange("p (f s) -> p f s", f=KE)[:, :, SLOTS:],
                                  ALU.mult).then_inc(a_ready, 1)

            def step(e, a, r):
                if exists(e + 2):
                    choose(e + 2, a)
                gated(e, a)
                if exists(e + 1):
                    turned(e + 1, 1 - a)
                if exists(e + 2):
                    gathered(e + 2, a)

            choose(0, 0)
            choose(1, 1)
            gathered(0, 0)
            gathered(1, 1)
            turned(0, 0)
            all_pairs(dve, step)


def more_blocks(k):
    nc, ps = k.nc, k.ps
    t = Z0 + 4096
    table = view(k, t, 16, NE)
    prod = view(k, t + 1024, 16, NE)
    ids, base, upto = (view(k, t + 2048 + 16 * i, 16) for i in range(3))
    ends = view(k, t + 2112, NE)
    number = k.iota[:, 0:16]
    pick = view(k, t + 2176, NT, SLOTS)
    want = view(k, t + 2432, NT)
    want0 = view(k, t + 2440, NT)
    xT = view(k, t + 2560, KD, SLOTS)
    sg, aT = view(k, t + 3072, KE * SLOTS), view(k, t + 3328, KE * SLOTS)
    yT = view(k, t + 3584, KD * SLOTS)
    yn = view(k, t + 4096, D)
    (listed, loaded, picked, x_done, x_ready, gu_done, silu_done, a_ready, y_done, y_ready, turned, rows_ready,
     stored) = (k.sem("more_" + n) for n in
                ("listed", "loaded", "picked", "x_done", "x_ready", "hidden_done", "silu_done", "a_ready", "y_done",
                 "y_ready", "turned", "rows_ready", "stored"))

    list_step = Counter(k.sem("more_list_step"))

    def if_any(eng, body):
        n = eng.value_load(k.flag[0:1, 0:1].bitcast(I32), min_val=0, max_val=XB)
        with eng.If(n > 0):
            body()

    def blocks(eng, step):
        step(0)
        with eng.Fori(1, XB) as b:
            step(b)

    with nc.Block() as block:
        @block.sync
        def _(sp):
            def step(b):
                since(sp, y_done, b)
                e = sp.value_load(ids[0:1, bass.ds(b, 1)].bitcast(I32), min_val=0, max_val=NE - 1)
                for i, w in enumerate((k.d["expert_w_gate_2"], k.d["expert_w_up_2"], k.d["expert_w_down_2"])):
                    src = w[0][bass.ds(e, 1)].rearrange("e (k p) n -> p (e k) n", p=P)
                    sp.dma_start(expert_view(k, 0, i), src).then_inc(loaded, 16)

            def body():
                sp.wait_ge(listed, 1)
                blocks(sp, step)

            if_any(sp, body)

        @block.vector
        def _(dve):
            def tt(o, a, b, op):
                k.link(dve, dve.tensor_tensor(o, a, b, op), list_step)

            def step(b):
                e = dve.value_load(ids[0:1, bass.ds(b, 1)].bitcast(I32), min_val=0, max_val=NE - 1)
                since(dve, x_done, b)
                dve.tensor_copy(want0, k.rk[:, :, bass.ds(e, 1)].rearrange("p t o -> p (t o)")).then_inc(picked, 1)
                dve.wait_ge(picked, 3 * b + 1)
                dve.tensor_scalar(want, want0, base[:, bass.ds(b, 1)], None, ALU.subtract).then_inc(picked, 1)
                dve.wait_ge(picked, 3 * b + 2)
                dve.tensor_tensor(pick, spread(k.iota, 1, NT), spread(want, 2, SLOTS), ALU.is_equal).then_inc(picked, 1)
                dve.wait_ge(x_done, b + 1)
                dve.tensor_copy(xT, ps[:, 0, :].rearrange("p (k s) -> p k s", k=KD)).then_inc(x_ready, 1)
                dve.wait_ge(silu_done, b + 1)
                dve.tensor_tensor(aT, sg, ps[:, 1, KE * SLOTS:], ALU.mult).then_inc(a_ready, 1)
                dve.wait_ge(y_done, b + 1)
                dve.tensor_copy(yT, ps[:, 2, :]).then_inc(y_ready, 1)

            def body():
                tt(ends, k.starts, k.nb, ALU.add)
                tt(table, spread(number, 2, NE), spread(k.starts, 1, 16), ALU.is_ge)
                tt(prod, spread(number, 2, NE), spread(ends, 1, 16), ALU.is_ge)
                tt(table, table, prod, ALU.subtract)
                tt(prod, table, spread(k.iota, 1, 16), ALU.mult)
                k.link(dve, dve.tensor_reduce(upto, prod, AX_X, ALU.add), list_step)
                tt(prod, table, spread(k.starts, 1, 16), ALU.mult)
                k.link(dve, dve.tensor_reduce(base, prod, AX_X, ALU.add), list_step)
                tt(base, number, base, ALU.subtract)
                k.link(dve, dve.tensor_scalar(base, base, 1.0, float(SLOTS), ALU.add, ALU.mult), list_step)
                dve.tensor_copy(ids.bitcast(I32), upto).then_inc(listed, 1)
                dve.wait_ge(listed, 1)
                blocks(dve, step)

            if_any(dve, body)

        @block.tensor
        def _(pe):
            def step(b):
                pe.wait_ge(picked, 3 * b + 3)
                for kk in range(KD):
                    for m in range(NT):
                        mm = pe.matmul(ps[:, 0, SLOTS * kk:SLOTS * (kk + 1)], k.hn[:, m, kk * P:(kk + 1) * P],
                                       pick[:, m, :], start=m == 0, stop=m == NT - 1)
                mm.then_inc(x_done, 1)
                pe.wait_ge(x_ready, b + 1)
                pe.wait_ge(loaded, 48 * b + 48)
                for i in range(2):
                    w = expert_view(k, 0, i)
                    for f in range(KE):
                        o = KE * SLOTS * i + SLOTS * f
                        for kk in range(KD):
                            mm = pe.matmul(ps[:, 1, o:o + SLOTS], w[:, kk, f * P:(f + 1) * P], xT[:, kk, :],
                                           start=kk == 0, stop=kk == KD - 1)
                mm.then_inc(gu_done, 1)
                pe.wait_ge(a_ready, b + 1)
                w = expert_view(k, 0, 2)
                for kk in range(KD):
                    for f in range(KE):
                        mm = pe.matmul(ps[:, 2, SLOTS * kk:SLOTS * (kk + 1)], w[:, f, kk * P:(kk + 1) * P],
                                       aT[:, SLOTS * f:SLOTS * (f + 1)], start=f == 0, stop=f == KE - 1)
                mm.then_inc(y_done, 1)
                pe.wait_ge(y_ready, b + 1)
                since(pe, rows_ready, b)
                for kk in range(KD):
                    tr = pe.matmul(ps[0:SLOTS, 5 + kk // 4, P * (kk % 4):P * (kk % 4 + 1)],
                                   yT[:, SLOTS * kk:SLOTS * (kk + 1)], k.ident, start=True, stop=True)
                tr.then_inc(turned, 1)

            if_any(pe, lambda: blocks(pe, step))

        @block.scalar
        def _(act):
            def step(b):
                act.wait_ge(gu_done, b + 1)
                act.activation(sg, ps[:, 1, 0:KE * SLOTS], ACT.Silu).then_inc(silu_done, 1)
                act.wait_ge(turned, b + 1)
                since(act, stored, 16 * b)
                act.copy(yn[0:SLOTS], ps[0:SLOTS, 5:7, :].rearrange("p b n -> p (b n)")).then_inc(rows_ready, 1)
                act.wait_ge(rows_ready, b + 1)
                act.dma_start(k.ypad[bass.ds(SLOTS * (NE + b), SLOTS)], yn[0:SLOTS]).then_inc(stored, 16)

            def body():
                blocks(act, step)
                act.wait_ge(stored, 16 * XB)

            if_any(act, body)



def finish(k):
    nc, d = k.nc, k.d
    x3 = view(k, H0, NT, D)
    rows = [view(k, RING, NT, D), view(k, RING + 4096, NT, D)]
    gain = view(k, RING + 8192, D)
    squares = view(k, RING + 9216, D)
    n1 = Norm(k, "norm_last", x3, NT, scratch=squares, stat=0)
    gathered = [k.sem(f"gathered{i}") for i in range(2 * NT)]
    g_in, x_in, summed, gained, out_st = (k.sem("last_" + n) for n in ("gain", "x_loaded", "summed", "gained", "stored"))
    out = k.out[0].rearrange("(m p) n -> p m n", p=P)

    with nc.Block() as block:
        @block.gpsimd
        def _(pool):
            for m in range(NT):
                for c in range(2):
                    pool.indirect_dma_start(rows[c][:, m, :], None, k.ypad,
                                            bass.IndirectOffsetOnAxis(ap=k.dest[:, c, m:m + 1].bitcast(U32), axis=0)
                                            ).then_inc(gathered[2 * m + c], 16)

        @block.sync
        def _(sp):
            sp.dma_start(gain, d["final_norm_g_2"].rearrange("(a n) -> a n", a=1).to_broadcast([P, D])).then_inc(g_in, 16)
            sp.wait_ge(gained, NT)
            sp.dma_start(out, x3).then_inc(out_st, 16)
            sp.wait_ge(out_st, 16)

        @block.scalar
        def _(act):
            act.wait_ge(summed, 2 * NT)
            n1.scalar_sums(act)
            n1.scalar_root(act)

        @block.vector
        def _(dve):
            for m in range(NT):
                for c in range(2):
                    dve.wait_ge(gathered[2 * m + c], 16)
                    if c:
                        dve.wait_ge(summed, 2 * m + 1)
                    dve.scalar_tensor_tensor(out=x3[:, m, :], in0=rows[c][:, m, :], scalar=k.gate_w[:, c, m:m + 1],
                                             in1=x3[:, m, :], op0=ALU.mult, op1=ALU.add).then_inc(summed, 1)
            n1.vector_mean(dve)
            n1.vector_scale(dve)
            dve.wait_ge(n1.normed, NT)
            dve.wait_ge(g_in, 16)
            for m in range(NT):
                dve.tensor_tensor(x3[:, m, :], x3[:, m, :], gain, ALU.mult).then_inc(gained, 1)





def program(nc, dram, out, stop=None):
    with ExitStack() as ctx:
        k = Kernel(nc, ctx, dram, out)
        k.chunks, k.next_chunk = weight_chunks(k), 0
        k.h_dram = [nc.dram_tensor(f"h{i}", (S, D), F32, kind="Internal").ap() for i in range(4)]
        k.bias_dram = nc.dram_tensor("bias", (NH, 2048), F32, kind="Internal").ap()
        k.us_dram = nc.dram_tensor("us", (S, 512), F32, kind="Internal").ap()
        k.ys_dram = nc.dram_tensor("ys", (S, 512), F32, kind="Internal").ap()
        k.ypad = nc.dram_tensor("ypad", (N_ROWS, D), F32, kind="Internal").ap()
        for f in STAGES:
            f(k)
            if f is not finish:
                k.end_phase()
            if stop == f.__name__:
                break
        return k


def even_out(k):
    out_projection(k, "even_out", k.d["ev_w_out"][0], k.d["x"][0], k.h_dram[0])


def odd_out(k):
    out_projection(k, "odd_out", k.d["od_w_out"][0], k.h_dram[0], None)


STAGES = [mem_in, even_in, even_mix, even_out, odd_in, compress, nsa, odd_out, mix_in, ssm, mix_mid, mix_out, moe, more_blocks, finish]

_INS = ["x", "mem", "norm_g", "final_g", "mem_norm_g", "rel_bias", "ev_w_in", "ev_pool_w", "ev_pool_scale",
        "ev_w_mem_kv", "ev_w_out", "od_w_in", "od_cmp_pe", "od_cmp_w1", "od_cmp_b1", "od_cmp_w2", "od_w_mem_kv",
        "od_w_out", "mix_norm_g_2", "w_in_2", "w_fourier_out_2", "ssm_A_re_2", "ssm_A_im_2", "ssm_log_dt_2",
        "ssm_B_re_2", "ssm_B_im_2", "ssm_C_re_2", "ssm_C_im_2", "ssm_D_2", "ssm_w_glu_2", "w_ssm_out_2", "w_out_2",
        "ffn_norm_g_2", "router_group_w_2", "router_group_b_2", "router_expert_w_2", "router_expert_b_2",
        "expert_w_gate_2", "expert_w_up_2", "expert_w_down_2", "final_norm_g_2"]


def kernel(**inputs):
    import numpy as _np
    import concourse.bacc as _bacc
    from concourse import mybir as _mybir
    from concourse.bass_utils import run_bass_kernel_spmd as _run

    nc = _bacc.Bacc("TRN2", target_bir_lowering=False, num_devices=1)
    arrays, dram = {}, {}
    held = {name: _np.ascontiguousarray(inputs[name]) for name in _INS}
    held.update(shape_constants())
    for name, a in held.items():
        arrays[f"in_{name}"] = a
        dram[name] = nc.dram_tensor(f"in_{name}", a.shape, _mybir.dt.from_np(a.dtype), kind="ExternalInput").ap()
    out = nc.dram_tensor("out_0", (1, S, D), _mybir.dt.from_np(_np.dtype("float32")), kind="ExternalOutput").ap()
    program(nc, dram, out)
    r = _run(nc, [arrays], core_ids=[0])
    return r.results[0]["out_0"]
```
